# Optimizing a Trainium2 kernel written in Bass

```python
import jax, jax.numpy as jnp
from jax import lax
import numpy as np

D_MODEL = 1024
BATCH = 1
SEQ = 256
DEPTH = 2
DEC_BATCH = 8
DEC_SEQ = 1
PAST_LEN = 2048
PAGE_SIZE = 128

TOK_WIDTH = 3 * D_MODEL // 4
MEM_WIDTH = D_MODEL // 4
MIX_WIDTH = TOK_WIDTH + MEM_WIDTH
MEM_HEADS = 4
MEM_HEAD_DIM = MEM_WIDTH // MEM_HEADS
N_MEM = 256
RWKV_HEAD_DIM = 64
RWKV_HEADS = TOK_WIDTH // RWKV_HEAD_DIM
RWKV_DECAY_RANK = 64
RWKV_A_RANK = 64
RWKV_GATE_RANK = 128
RWKV_GN_EPS = 64e-5
GLA_HEADS = 4
GLA_K_WIDTH = TOK_WIDTH // 2
GLA_DK = GLA_K_WIDTH // GLA_HEADS
GLA_DV = TOK_WIDTH // GLA_HEADS
GLA_GATE_RANK = 16
GLA_TAU = 16.0
GLA_CHUNK = 64
IN_COLS = 3 * TOK_WIDTH + MEM_WIDTH
N_GROUPS = 4
EXPERTS_PER_GROUP = 8
N_EXPERTS = N_GROUPS * EXPERTS_PER_GROUP
TOP_K_IN_GROUP = 2
EXPERT_FF = D_MODEL // 2
MOE_BLOCK = 128
N_RWKV_LAYERS = (DEPTH + 1) // 2
N_GLA_LAYERS = DEPTH // 2
NORM_EPS = 1e-6

kernel_name = 'hybrid_rwkv7_gla_memxattn_hmoe_step'

def rms_norm(x, g):
    xf = x.astype(jnp.float32)
    y = xf * lax.rsqrt(jnp.mean(xf * xf, -1, keepdims=True) + NORM_EPS)
    return (y * g.astype(jnp.float32)).astype(x.dtype)

def rwkv7_mix(h, shift_prev, S0, w_rkv, mu, w0, w1, w2, a0, a1, a2, g1, g2, k_k, k_a, r_k, ln_g, ln_b):
    B, T, _ = h.shape
    H, N = RWKV_HEADS, RWKV_HEAD_DIM
    f32 = jnp.float32
    h_prev = jnp.concatenate([shift_prev[:, None, :].astype(h.dtype), h[:, :-1]], axis=1)
    xx = h_prev - h
    xr, xw, xk, xv, xa, xg = [h + xx * mu[j] for j in range(6)]
    r = xr @ w_rkv[:, :TOK_WIDTH]
    k = xk @ w_rkv[:, TOK_WIDTH:2 * TOK_WIDTH]
    v = xv @ w_rkv[:, 2 * TOK_WIDTH:3 * TOK_WIDTH]
    w_log = -jax.nn.softplus(-(w0 + jnp.tanh(xw @ w1) @ w2).astype(f32)) - 0.5
    decay = jnp.exp(-jnp.exp(w_log))
    a = jax.nn.sigmoid((a0 + (xa @ a1) @ a2).astype(f32))
    g = jax.nn.sigmoid(xg @ g1) @ g2
    heads = lambda t: t.reshape(B, T, H, N)
    kk = heads((k * k_k).astype(f32))
    kk = kk / jnp.maximum(jnp.sqrt(jnp.sum(kk * kk, -1, keepdims=True)), 1e-12)
    k = k.astype(f32) * (1.0 + (a - 1.0) * k_a.astype(f32))
    r4, k4, v4, a4, d4 = heads(r.astype(f32)), heads(k), heads(v.astype(f32)), heads(a), heads(decay)

    def step(S, inp):
        r_t, k_t, v_t, kk_t, b_t, d_t = inp
        sa = jnp.einsum('bhij,bhj->bhi', S, -kk_t)
        S = S * d_t[:, :, None, :] + sa[..., None] * b_t[:, :, None, :] + v_t[..., None] * k_t[:, :, None, :]
        return S, jnp.einsum('bhij,bhj->bhi', S, r_t)

    seq_major = lambda t: jnp.moveaxis(t, 1, 0)
    S_fin, y = lax.scan(step, S0.astype(f32), tuple(seq_major(t) for t in (r4, k4, v4, kk, kk * a4, d4)))
    y = jnp.moveaxis(y, 0, 1)
    mean = jnp.mean(y, -1, keepdims=True)
    var = jnp.mean(jnp.square(y - mean), -1, keepdims=True)
    gn = ((y - mean) * lax.rsqrt(var + RWKV_GN_EPS)).reshape(B, T, TOK_WIDTH) * ln_g.astype(f32) + ln_b.astype(f32)
    bonus = (jnp.sum(r4 * k4 * r_k.astype(f32), -1, keepdims=True) * v4).reshape(B, T, TOK_WIDTH)
    out = ((gn + bonus) * g.astype(f32)).astype(h.dtype)
    return out, h[:, -1], S_fin.astype(S0.dtype)

def gla_mix(h, S0, w_qkvr, a1, a2, ab, norm_g):
    B, T, _ = h.shape
    H, DK, DV = GLA_HEADS, GLA_DK, GLA_DV
    f32 = jnp.float32
    proj = h @ w_qkvr
    q = proj[..., :GLA_K_WIDTH]
    k = proj[..., GLA_K_WIDTH:2 * GLA_K_WIDTH]
    v = proj[..., 2 * GLA_K_WIDTH:2 * GLA_K_WIDTH + TOK_WIDTH]
    r = proj[..., 2 * GLA_K_WIDTH + TOK_WIDTH:]
    log_a = jax.nn.log_sigmoid(((h @ a1) @ a2 + ab).astype(f32)) / GLA_TAU
    C = min(GLA_CHUNK, T)
    n_chunks = -(-T // C)
    Tp = n_chunks * C

    def chunks(t, d):
        t = t.astype(f32).reshape(B, T, H, d)
        t = jnp.pad(t, ((0, 0), (0, Tp - T), (0, 0), (0, 0)))
        return t.reshape(B, n_chunks, C, H, d).transpose(1, 0, 3, 2, 4)

    qc = chunks(q, DK) * (DK ** -0.5)
    kc, vc, lac = chunks(k, DK), chunks(v, DV), chunks(log_a, DK)
    causal = jnp.tril(jnp.ones((C, C), bool))

    def step(S, inp):
        q_c, k_c, v_c, la_c = inp
        b = jnp.cumsum(la_c, axis=2)
        inter = jnp.einsum('bhtd,bhde->bhte', q_c * jnp.exp(b), S)
        gap = jnp.where(causal[:, :, None], b[:, :, :, None, :] - b[:, :, None, :, :], -jnp.inf)
        att = jnp.einsum('bhtd,bhsd,bhtsd->bhts', q_c, k_c, jnp.exp(gap))
        intra = jnp.einsum('bhts,bhse->bhte', att, v_c)
        b_end = b[:, :, -1]
        S = jnp.exp(b_end)[..., None] * S + jnp.einsum('bhsd,bhse->bhde', k_c * jnp.exp(b_end[:, :, None] - b), v_c)
        return S, inter + intra

    S_fin, o = lax.scan(step, S0.astype(f32), (qc, kc, vc, lac))
    o = o.transpose(1, 0, 3, 2, 4).reshape(B, Tp, H, DV)[:, :T]
    o = o * lax.rsqrt(jnp.mean(o * o, -1, keepdims=True) + NORM_EPS) * norm_g.astype(f32)
    out = (o.reshape(B, T, TOK_WIDTH) * jax.nn.silu(r.astype(f32))).astype(h.dtype)
    return out, S_fin.astype(S0.dtype)

def memory_kv(mem, g, w_kv):
    B, M, _ = mem.shape
    kv = rms_norm(mem, g) @ w_kv
    k = kv[..., :MEM_WIDTH].reshape(B, M, MEM_HEADS, MEM_HEAD_DIM)
    v = kv[..., MEM_WIDTH:].reshape(B, M, MEM_HEADS, MEM_HEAD_DIM)
    return k, v

def mem_attention(q, mem_k, mem_v):
    B, T, _ = q.shape
    q = q.reshape(B, T, MEM_HEADS, MEM_HEAD_DIM)
    s = jnp.einsum('bthd,bmhd->bhtm', q, mem_k).astype(jnp.float32) * (MEM_HEAD_DIM ** -0.5)
    p = jax.nn.softmax(s, axis=-1).astype(q.dtype)
    return jnp.einsum('bhtm,bmhd->bthd', p, mem_v).reshape(B, T, MEM_WIDTH)

def hier_moe(h, wg, bg, we, be, w_up, w_down):
    B, T, D = h.shape
    N = B * T
    K = TOP_K_IN_GROUP
    hf = h.reshape(N, D)
    group_logits = (hf @ wg + bg).astype(jnp.float32)
    group = jnp.argmax(group_logits, -1).astype(jnp.int32)
    p_group = jnp.max(jax.nn.softmax(group_logits, -1), -1, keepdims=True)
    exp_logits = (hf @ we + be).astype(jnp.float32).reshape(N, N_GROUPS, EXPERTS_PER_GROUP)
    in_group = exp_logits[jnp.arange(N), group]
    top_val, top_idx = lax.top_k(in_group, K)
    gate = p_group * jax.nn.softmax(top_val, -1)
    expert = group[:, None] * EXPERTS_PER_GROUP + top_idx.astype(jnp.int32)
    A = N * K
    flat_e = expert.reshape(A)
    flat_tok = jnp.arange(A, dtype=jnp.int32) // K
    flat_gate = gate.reshape(A)
    order = jnp.argsort(flat_e)
    e_sorted = flat_e[order]
    counts = jnp.bincount(flat_e, length=N_EXPERTS).astype(jnp.int32)
    padded = (counts + MOE_BLOCK - 1) // MOE_BLOCK * MOE_BLOCK
    padded_end = jnp.cumsum(padded)
    start = jnp.cumsum(counts) - counts
    dest = (padded_end - padded)[e_sorted] + jnp.arange(A, dtype=jnp.int32) - start[e_sorted]
    n_blocks = -(-A // MOE_BLOCK) + N_EXPERTS
    row_tok = jnp.zeros((n_blocks * MOE_BLOCK,), jnp.int32).at[dest].set(flat_tok[order])
    block_expert = jnp.minimum(jnp.searchsorted(padded_end, jnp.arange(n_blocks, dtype=jnp.int32) * MOE_BLOCK, side='right'), N_EXPERTS - 1)

    def run_block(args):
        xb, e = args
        gu = xb @ w_up[e]
        return (jax.nn.silu(gu[:, :EXPERT_FF]) * gu[:, EXPERT_FF:]) @ w_down[e]

    rows = lax.map(run_block, (hf[row_tok].reshape(n_blocks, MOE_BLOCK, D), block_expert))
    contrib = rows.reshape(n_blocks * MOE_BLOCK, D)[dest] * flat_gate[order][:, None].astype(h.dtype)
    y = jnp.zeros((N, D), h.dtype).at[flat_tok[order]].add(contrib)
    return y.reshape(B, T, D)

def run_trunk(x, mem_k, mem_v, rw_S, rw_shift, gla_S, P):
    new_rw_S, new_rw_shift, new_gla_S = [], [], []
    for i in range(DEPTH):
        h = rms_norm(x, P['norm_mix_g'][i])
        w_in = P['w_in'][i]
        j = i // 2
        if i % 2 == 0:
            tok, shift_new, S_new = rwkv7_mix(
                h, rw_shift[j], rw_S[j], w_in[:, :3 * TOK_WIDTH], P['rw_mu'][j], P['rw_w0'][j], P['rw_w1'][j],
                P['rw_w2'][j], P['rw_a0'][j], P['rw_a1'][j], P['rw_a2'][j], P['rw_g1'][j], P['rw_g2'][j],
                P['rw_k_k'][j], P['rw_k_a'][j], P['rw_r_k'][j], P['rw_ln_g'][j], P['rw_ln_b'][j])
            new_rw_S.append(S_new)
            new_rw_shift.append(shift_new)
        else:
            tok, S_new = gla_mix(h, gla_S[j], w_in[:, :3 * TOK_WIDTH], P['gla_a1'][j], P['gla_a2'][j],
                                 P['gla_ab'][j], P['gla_norm_g'][j])
            new_gla_S.append(S_new)
        q_mem = h @ w_in[:, 3 * TOK_WIDTH:]
        mixed = jnp.concatenate([tok, mem_attention(q_mem, mem_k[i], mem_v[i])], axis=-1)
        x = x + mixed @ P['w_out'][i]
        x = x + hier_moe(rms_norm(x, P['norm_ffn_g'][i]), P['router_wg'][i], P['router_bg'][i],
                         P['router_we'][i], P['router_be'][i], P['exp_w_up'][i], P['exp_w_down'][i])
    y = rms_norm(x, P['norm_final_g'])
    return y, jnp.stack(new_rw_S), jnp.stack(new_rw_shift), jnp.stack(new_gla_S)

def setup_inputs(seed: int = 0) -> dict:
    key = jax.random.key(seed)
    ks = iter(jax.random.split(key, 48))
    f32 = jnp.float32

    def nrm(shape, scale=1.0):
        return jax.random.normal(next(ks), shape, f32) * scale

    def gain(shape):
        return 1.0 + nrm(shape, 0.05)

    NA, NB = N_RWKV_LAYERS, N_GLA_LAYERS
    inv = D_MODEL ** -0.5
    return {
        'x_prompt': nrm((BATCH, SEQ, D_MODEL)),
        'x_sample': nrm((DEC_BATCH, DEC_SEQ, D_MODEL)),
        'mem_prompt': nrm((BATCH, N_MEM, D_MODEL)),
        'state_rwkv_S': nrm((NA, DEC_BATCH, RWKV_HEADS, RWKV_HEAD_DIM, RWKV_HEAD_DIM), 0.3),
        'state_rwkv_shift': nrm((NA, DEC_BATCH, D_MODEL)),
        'state_gla_S': nrm((NB, DEC_BATCH, GLA_HEADS, GLA_DK, GLA_DV), 0.3),
        'cache_mem_k': nrm((DEPTH, DEC_BATCH, N_MEM, MEM_HEADS, MEM_HEAD_DIM)),
        'cache_mem_v': nrm((DEPTH, DEC_BATCH, N_MEM, MEM_HEADS, MEM_HEAD_DIM)),
        'norm_mix_g': gain((DEPTH, D_MODEL)),
        'norm_ffn_g': gain((DEPTH, D_MODEL)),
        'norm_mem_g': gain((DEPTH, D_MODEL)),
        'norm_final_g': gain((D_MODEL,)),
        'w_in': nrm((DEPTH, D_MODEL, IN_COLS), inv),
        'w_out': nrm((DEPTH, MIX_WIDTH, D_MODEL), 0.5 * MIX_WIDTH ** -0.5),
        'w_mem_kv': nrm((DEPTH, D_MODEL, 2 * MEM_WIDTH), inv),
        'rw_mu': jax.random.uniform(next(ks), (NA, 6, D_MODEL), f32),
        'rw_w0': jnp.linspace(-6.5, -1.5, TOK_WIDTH, dtype=f32)[None, :] + nrm((NA, TOK_WIDTH), 0.1),
        'rw_w1': nrm((NA, D_MODEL, RWKV_DECAY_RANK), inv),
        'rw_w2': nrm((NA, RWKV_DECAY_RANK, TOK_WIDTH), 0.5 * RWKV_DECAY_RANK ** -0.5),
        'rw_a0': nrm((NA, TOK_WIDTH), 0.1),
        'rw_a1': nrm((NA, D_MODEL, RWKV_A_RANK), inv),
        'rw_a2': nrm((NA, RWKV_A_RANK, TOK_WIDTH), 0.5 * RWKV_A_RANK ** -0.5),
        'rw_g1': nrm((NA, D_MODEL, RWKV_GATE_RANK), inv),
        'rw_g2': nrm((NA, RWKV_GATE_RANK, TOK_WIDTH), RWKV_GATE_RANK ** -0.5),
        'rw_k_k': 0.85 + nrm((NA, TOK_WIDTH), 0.05),
        'rw_k_a': gain((NA, TOK_WIDTH)),
        'rw_r_k': nrm((NA, RWKV_HEADS, RWKV_HEAD_DIM), 0.1),
        'rw_ln_g': gain((NA, TOK_WIDTH)),
        'rw_ln_b': nrm((NA, TOK_WIDTH), 0.02),
        'gla_a1': nrm((NB, D_MODEL, GLA_GATE_RANK), inv),
        'gla_a2': nrm((NB, GLA_GATE_RANK, GLA_K_WIDTH), GLA_GATE_RANK ** -0.5),
        'gla_ab': nrm((NB, GLA_K_WIDTH), 0.1),
        'gla_norm_g': gain((NB, GLA_DV)),
        'router_wg': nrm((DEPTH, D_MODEL, N_GROUPS), inv),
        'router_bg': nrm((DEPTH, N_GROUPS), 0.01),
        'router_we': nrm((DEPTH, D_MODEL, N_EXPERTS), inv),
        'router_be': nrm((DEPTH, N_EXPERTS), 0.01),
        'exp_w_up': nrm((DEPTH, N_EXPERTS, D_MODEL, 2 * EXPERT_FF), inv),
        'exp_w_down': nrm((DEPTH, N_EXPERTS, EXPERT_FF, D_MODEL), EXPERT_FF ** -0.5),
    }

def reference(x_prompt, x_sample, mem_prompt, state_rwkv_S, state_rwkv_shift, state_gla_S, cache_mem_k, cache_mem_v,
              norm_mix_g, norm_ffn_g, norm_mem_g, norm_final_g, w_in, w_out, w_mem_kv,
              rw_mu, rw_w0, rw_w1, rw_w2, rw_a0, rw_a1, rw_a2, rw_g1, rw_g2, rw_k_k, rw_k_a, rw_r_k, rw_ln_g, rw_ln_b,
              gla_a1, gla_a2, gla_ab, gla_norm_g, router_wg, router_bg, router_we, router_be, exp_w_up, exp_w_down):
    P = {
        'norm_mix_g': norm_mix_g, 'norm_ffn_g': norm_ffn_g, 'norm_final_g': norm_final_g,
        'w_in': w_in, 'w_out': w_out,
        'rw_mu': rw_mu, 'rw_w0': rw_w0, 'rw_w1': rw_w1, 'rw_w2': rw_w2, 'rw_a0': rw_a0, 'rw_a1': rw_a1,
        'rw_a2': rw_a2, 'rw_g1': rw_g1, 'rw_g2': rw_g2, 'rw_k_k': rw_k_k, 'rw_k_a': rw_k_a, 'rw_r_k': rw_r_k,
        'rw_ln_g': rw_ln_g, 'rw_ln_b': rw_ln_b,
        'gla_a1': gla_a1, 'gla_a2': gla_a2, 'gla_ab': gla_ab, 'gla_norm_g': gla_norm_g,
        'router_wg': router_wg, 'router_bg': router_bg, 'router_we': router_we, 'router_be': router_be,
        'exp_w_up': exp_w_up, 'exp_w_down': exp_w_down,
    }
    mem_kv = [memory_kv(mem_prompt, norm_mem_g[i], w_mem_kv[i]) for i in range(DEPTH)]
    prompt_mem_k = jnp.stack([kv[0] for kv in mem_kv])
    prompt_mem_v = jnp.stack([kv[1] for kv in mem_kv])
    B = x_prompt.shape[0]
    dt = x_prompt.dtype
    rw_S0 = jnp.zeros((N_RWKV_LAYERS, B, RWKV_HEADS, RWKV_HEAD_DIM, RWKV_HEAD_DIM), dt)
    rw_shift0 = jnp.zeros((N_RWKV_LAYERS, B, D_MODEL), dt)
    gla_S0 = jnp.zeros((N_GLA_LAYERS, B, GLA_HEADS, GLA_DK, GLA_DV), dt)
    y_prompt, prompt_rwkv_S, prompt_rwkv_shift, prompt_gla_S = run_trunk(
        x_prompt, prompt_mem_k, prompt_mem_v, rw_S0, rw_shift0, gla_S0, P)
    y_sample, sample_rwkv_S, sample_rwkv_shift, sample_gla_S = run_trunk(
        x_sample, cache_mem_k, cache_mem_v, state_rwkv_S, state_rwkv_shift, state_gla_S, P)
    return (y_prompt, y_sample, prompt_rwkv_S, prompt_rwkv_shift, prompt_gla_S, prompt_mem_k, prompt_mem_v,
            sample_rwkv_S, sample_rwkv_shift, sample_gla_S)


_drawn_inputs = setup_inputs


def setup_inputs(seed=0):
    import zlib

    import numpy as np

    out = dict(_drawn_inputs(seed))
    spreads = {}
    factors = {}
    for name, (base, spread) in spreads.items():
        noise = np.random.default_rng([zlib.crc32(name.encode()), seed]).standard_normal(out[name].shape)
        drawn = base * np.exp(spread * noise) if base else spread * noise
        out[name] = __import__('jax').numpy.asarray(drawn.astype(out[name].dtype))
    for name, factor in factors.items():
        out[name] = (out[name] * factor).astype(out[name].dtype)
    return out
```

```python
from contextlib import ExitStack

import numpy as np
import concourse.bass as bass
from concourse import mybir

ALU = mybir.AluOpType
ACT = mybir.ActivationFunctionType
F32 = mybir.dt.float32
BF16 = mybir.dt.bfloat16
I32 = mybir.dt.int32
U32 = mybir.dt.uint32
AXX = mybir.AxisListType.X

D = 1024
KT = D // 128
TP = 256
TS = 8
T = TP + TS
TOK = 768
MEMW = 256
N_MEM = 256
C = 64
NCH = TP // C
PAIRS = TOK // 128
TILES = [(0, 128), (128, 128), (256, TS)]
DEPTH = 2
NE = 32
GROUPS = 4
FF = 512
CAP = 64
STEPS_REST = 4
RROWS = CAP * STEPS_REST
EPS = 1e-6
GN_EPS = 64e-5
LN2 = 0.6931471805599453
BIG = 1e30

W_IN = [[(2304, 256), (0, 512), (512, 512), (1024, 512), (1536, 512), (2048, 256)],
        [(2304, 256)] + [(384 * n, 384) for n in range(6)]]
W_OUT = [[(0, 512), (512, 512)], [(256 * n, 256) for n in range(4)]]
TILE_W = [128, 96]
LORA_TILES = [3 + 3 * PAIRS, 1 + 4]
CHUNKS = [1 + len(W_IN[l]) + len(W_OUT[l]) for l in range(2)]


def tiles_through(g):
    total, n = 0, 0
    for l in range(DEPTH):
        parts = [2, 2] + [w // TILE_W[l] for _, w in W_IN[l][1:]] + [3] * len(W_OUT[l])
        for i, m in enumerate(parts):
            if i == 1 + len(W_IN[l]):
                total += LORA_TILES[l]
            total += m
            if n == g:
                return total
            n += 1


ROUNDS = [("N", "dve"), ("NT", "dve"), ("Bn", "act"), ("Kn", "act"), ("Vn", "act"), ("X2", "act"), ("X2T", "act"),
          ("MT", "dve"), ("U1", "dve"), ("UT1", "dve"), ("X4", "act"), ("X4T", "act"), ("PT", "dve"), ("U2", "dve"),
          ("UT2", "dve"), ("X8T", "act"), ("QT", "dve"), ("U3", "dve"), ("UT3", "dve"), ("W1", "act"), ("U4", "dve"),
          ("UT4", "dve"), ("W2", "act"), ("U5", "dve"), ("RHS", "act"), ("SA", "act"), ("Y", "act"), ("Z", "dve")]
ORDER = [n for n, _ in ROUNDS]


def c_ps_at(c, name, half):
    return 2 * (len(ROUNDS) * c + ORDER.index(name)) + half + 1


def c_at(c, name, half):
    mine = [n for n, e in ROUNDS if e == dict(ROUNDS)[name]]
    return 2 * (len(mine) * c + mine.index(name)) + half + 1


C_TOTAL = 2 * NCH * sum(e == "dve" for _, e in ROUNDS)
C_ACT = 2 * NCH * sum(e == "act" for _, e in ROUNDS)
T_SCALED = 6
T_STATE_OUT = 4
OUT_STORES = [3, 5]
SEMS = """consts x_loaded norm_ss norm_rs norm_h hT_ps hT gain_loaded router_w
logit_ps logits gate_e gates rank_ps ranks flagT_ps flag
wup0 wup1 wdn0 wdn1 m_G m_xg_ps m_xgT m_gate_ps m_up_ps m_exp m_swi m_act m_actT_ps m_actT m_dn_ps m_nat h_parts m_ywr0 m_ywr1
rgath0 rgath1 rcomb0 rcomb1 rw0 rG0 rxg0 rxgT0 rgate0 rup0 rexp0 ract0 ratps0 ractT0 rdn0 rnat0 rywa0 rywb0
rw1 rG1 rxg1 rxgT1 rgate1 rup1 rexp1 ract1 ratps1 ractT1 rdn1 rnat1 rywa1 rywb1
gathered combined y_done stored out_stored
vec_in vecT_ps vecT masks lora_in chunk_in0 chunk_in1 chunk_in2 pj_ps pj_out shift_stored
mm_in mm_ss mm_rs mm_h mm_T_ps mm_T kv_stored
kT_ps kT sc_ps sc_max sc_exp sc_prob pT_ps pT at_ps at_out
cache_k cache_v qn_ps qn qb_ps s_score sT_ps s_max s_exp s_prob spT_ps spT sat_ps sat_out
shift_in shiftT_ps shiftT xj lora_e lora_s t_dve t_act sum_ps c_ps c_dve c_act c_pool
dec_scr0 dec_scr1 dec_in dec_mul dec_sum dec_y x_out rswi0 rswi1 act_chain dve_chain pool_chain""".split()


def build(nc, A, O, dbg=None):
    with ExitStack() as ctx:
        s = {n: ctx.enter_context(nc.semaphore(n)) for n in SEMS}

        def sb(name, cols, dt=F32, rows=128):
            return ctx.enter_context(nc.sbuf_tensor(name, [rows, cols], dt))

        slot = [sb("slot0", 12288), sb("slot1", 12288)]
        wup = [t[:, 0:8192].rearrange("p (k n) -> p k n", k=KT) for t in slot]
        wdn = [t[:, 8192:12288].rearrange("p (k n) -> p k n", k=FF // 128) for t in slot]
        x = sb("x", 3 * D)[:, :].rearrange("p (t d) -> p t d", t=3)
        h = sb("h", 3 * D)[:, :].rearrange("p (t d) -> p t d", t=3)
        hT = sb("hT", KT * T)[:, :].rearrange("p (k t) -> p k t", k=KT)
        gain = sb("gain", D)
        ident = sb("ident", 128)
        before = sb("before", 128)
        ones = sb("ones", 128)
        iota_rank = sb("iota_rank", CAP + RROWS)
        iota_e = sb("iota_e", NE)
        iota_g = sb("iota_g", NE)
        valid = sb("valid", 3)
        cst = sb("cst", 8)
        vecT = sb("vecT", 90)
        mlow = sb("mlow", 128)
        mup = sb("mup", 128)
        moff1 = sb("moff1", 128)
        moff2 = sb("moff2", 128)
        upto = sb("upto", 128)
        block64 = sb("block64", 128)
        sel = sb("sel", TS * 128, rows=TS)[:, :].rearrange("k (b n) -> k b n", b=TS)
        mixedT = sb("mixedT", KT * T + 2 * T)[:, :].rearrange("p (k t) -> p k t", t=T)
        nvec = sb("nvec", 12)
        arena = sb("arena", 13600)
        pos = [0]

        def carve(n):
            a = arena[:, pos[0]:pos[0] + n]
            pos[0] += n
            return a

        sq = carve(D)
        st = carve(16)
        mm_st = arena[:, 1024 + 8:1024 + 16]
        wr = carve(KT * 36).rearrange("p (k n) -> p k n", k=KT)
        br = carve(36)
        lg = carve(3 * 36).rearrange("p (t n) -> p t n", t=3)
        g8 = carve(3 * 8).rearrange("p (t n) -> p t n", t=3)
        m8 = carve(3 * 8).rearrange("p (t n) -> p t n", t=3)
        i8 = carve(3 * 8).rearrange("p (t n) -> p t n", t=3)
        i8f = carve(3 * 8).rearrange("p (t n) -> p t n", t=3)
        em = carve(3 * NE).rearrange("p (t n) -> p t n", t=3)
        tmp32 = carve(3 * NE).rearrange("p (t n) -> p t n", t=3)
        a1 = carve(3 * NE).rearrange("p (t n) -> p t n", t=3)
        a2 = carve(3 * NE).rearrange("p (t n) -> p t n", t=3)
        asum = carve(3 * NE).rearrange("p (t n) -> p t n", t=3)
        rank = carve(3 * NE).rearrange("p (t n) -> p t n", t=3)
        R = carve(3 * (NE + 2)).rearrange("p (t n) -> p t n", t=3)
        gt = carve(3 * 8).rearrange("p (t n) -> p t n", t=3)
        rowf = carve(6)
        rowi = carve(6)
        flagf = carve(4)
        bf = lambda n: carve(n // 2).bitcast(BF16)
        hp = [bf(3 * D).rearrange("p (t d) -> p t d", t=3) for _ in range(3)]
        G = [bf(3 * CAP).rearrange("p (t n) -> p t n", t=3) for _ in range(2)]
        xgT = [carve(KT * CAP).rearrange("p (k n) -> p k n", k=KT) for _ in range(2)]
        ex = carve(FF)
        rec = carve(FF)
        sg = carve(FF)
        an = carve(FF)
        actT = carve(4 * CAP).rearrange("p (f n) -> p f n", f=4)
        ynat = [carve(D) for _ in range(2)]
        yg = h
        rows_i = sb("rows_i", 6, I32)
        rows_r = sb("rows_r", 6, I32)
        in_rest = sb("in_rest", 6)
        gr = sb("gr", 6)
        flag_i = sb("flag_i", 2, I32)
        idx_u = sb("idx_u", 3 * 8, U32)[:, :].rearrange("p (t n) -> p t n", t=3)
        ps = [ctx.enter_context(nc.psum_tensor(f"bank{i}", [128, 512], F32)) for i in range(8)]
        wch = [slot[0][:, 4096 * n:4096 * (n + 1)] for n in range(3)]

        class Area:
            def __init__(self, ap, at=0):
                self.ap, self.at = ap, at

            def take(self, n):
                self.at += n
                return self.ap[:, self.at - n:self.at]
        k3 = lambda a, k: a.rearrange("p (k t) -> p k t", k=k)
        AR = 1040
        vraw = arena[:, AR:AR + 128]
        a_ = Area(arena, AR + 128)
        mem = k3(a_.take(2 * D), 2)
        gmem = a_.take(D)
        memT = k3(a_.take(KT * N_MEM), KT)
        kvn = k3(a_.take(2 * 2 * MEMW), 2)
        kT = k3(a_.take(2 * N_MEM), 2)
        qT = k3(a_.take(2 * T), 2)
        qs = a_.take(MEMW)
        smx = a_.take(8)
        snx = a_.take(8)
        ssm = a_.take(8)
        srs = a_.take(8)
        sc_s = a_.take(64)
        sp_s = a_.take(N_MEM)
        spT = a_.take(64)
        attention_end = a_.at
        b_ = Area(slot[1])
        KC = b_.take(4096).rearrange("p (m b n) -> p m b n", m=2, b=TS)
        VC = b_.take(4096).rearrange("p (m b n) -> p m b n", m=2, b=TS)
        P = b_.take(8 * N_MEM).rearrange("p (h t m) -> p h t m", h=4, t=2)
        PT = b_.take(4 * 2 * TP).rearrange("p (h m t) -> p h m t", h=4, m=2)
        a_ = Area(arena, AR + 128)
        Q = [k3(a_.take(PAIRS * T), PAIRS) for _ in range(5)]
        lw1, la1, lg1 = k3(a_.take(512), KT), k3(a_.take(512), KT), k3(a_.take(1024), KT)
        lw2, la2, lg2 = a_.take(TOK), a_.take(TOK), a_.take(TOK)
        lora_at = a_.at - (512 + 512 + 1024 + 3 * TOK)
        w1o, a1o, g1o = mixedT[:, 0, :], mixedT[:, 1, :], mixedT[:, 2, :]
        assert a_.at <= 13600, a_.at
        b_ = Area(slot[1])
        Q += [k3(b_.take(PAIRS * T), PAIRS) for _ in range(3)]
        t_at = b_.at
        TT = [k3(b_.take(KT * T), KT) for _ in range(3)]
        shn = b_.take(D)
        vr, vk, vv, vb, vkk, vL, vg, vld = Q
        b_ = Area(slot[1], t_at)
        c_ = Area(arena, lora_at)
        h_ = Area(h.rearrange("p t d -> p (t d)"))
        t_ = Area(hT.rearrange("p k t -> p (k t)"))
        mats = [k3(b_.take(768), PAIRS) for _ in range(9)] + [k3(c_.take(768), PAIRS) for _ in range(5)] \
            + [k3(h_.take(768), PAIRS) for _ in range(4)] + [k3(t_.take(768), PAIRS) for _ in range(2)] + [k3(gain[:, 0:768], PAIRS)]
        cAT, cBT, cKT, cRT, cN, cN1, cN2, cNT, cX2, cX2T, cX4, cX4T, cUa, cUb, cUTa, cUTb, cQT, cBn, cKn, cVn, cZ = mats
        lam = sb("lam", PAIRS * NCH)[:, :].rearrange("p (q c) -> p q c", c=NCH)
        DS = arena[0:96, lora_at:lora_at + 4096].rearrange("p (i j) -> p i j", i=64)
        Dt = slot[1][0:96, t_at:t_at + 4096].rearrange("p (i j) -> p i j", i=64)
        Dv = slot[1][0:96, t_at + 4096:t_at + 4096 + 6 * 64].rearrange("p (v j) -> p v j", v=6)
        Dsa = slot[1][0:96, t_at + 4500:t_at + 4564]
        Dy = slot[1][0:96, t_at + 4564:t_at + 4628]
        Dn = [mixedT.rearrange("p k t -> p (k t)")[0:TS, TOK * n:TOK * (n + 1)] for n in range(2)]
        dscr = nc.dram_tensor("sample_vectors", [6, TS * TOK], F32, kind="Internal").ap()
        yscr = nc.dram_tensor("sample_y", [TS * TOK], F32, kind="Internal").ap()
        a_ = Area(arena, AR + 128)
        b_ = Area(slot[1])
        gq, gk = k3(a_.take(4 * T), 4), k3(a_.take(4 * T), 4)
        gv, grt = k3(a_.take(8 * T), 8), k3(a_.take(8 * T), 8)
        gl, ge = k3(a_.take(4 * T), 4), k3(a_.take(4 * T), 4)
        gkh, gq2 = k3(a_.take(4 * T), 4), a_.take(0)
        ga1, ga2, ga1o = k3(a_.take(128), KT), a_.take(384), a_.take(T)
        assert a_.at <= 13600, a_.at
        gS = b_.take(TS * TOK).rearrange("p (b h e) -> p b h e", b=TS, h=4)
        go = k3(b_.take(8 * T), 8)
        gZ = k3(b_.take(TOK), 4)
        gZm = k3(b_.take(TOK), 4)
        gvn = b_.take(TOK)
        gkn = b_.take(384)
        gatt = k3(b_.take(4 * C), 4)
        gem = b_.take(4 * NCH)
        gee = b_.take(4 * NCH)
        gvs = b_.take(TOK)
        assert b_.at <= 12288, b_.at
        wo_tiles = [[(k, 128 * k, 128) for k in range(KT)],
                    [(k, 96 * k, 96) for k in range(8)] + [(8 + k, TOK + 128 * k, 128) for k in range(2)]]

        rows_first = [nc.dram_tensor(f"rows_first{l}", [NE * CAP, D], F32, kind="Internal").ap() for l in range(DEPTH)]
        rows_rest = [nc.dram_tensor(f"rows_rest{l}", [NE * RROWS, D], F32, kind="Internal").ap() for l in range(DEPTH)]

        block = ctx.enter_context(nc.Block())

        def chain(eng, sem):
            n = [0]

            def link(ins):
                n[0] += 1
                ins.then_inc(sem, 1)
                eng.wait_ge(sem, n[0])
            return link

        def load_expert(sp, e, sl, l, su, sd):
            sp.dma_start(wup[sl], A["exp_w_up"][l, bass.ds(e, 1)].rearrange("e (k p) n -> p (e k) n", p=128)).then_inc(su, 16)
            sp.dma_start(wdn[sl], A["exp_w_down"][l, bass.ds(e, 1)].rearrange("e (k p) n -> p (e k) n", p=128)).then_inc(sd, 16)

        @block.sync
        def _(sp):
            sp.dma_start(x[:, 0:2, :], A["x_prompt"][0].rearrange("(t p) d -> p t d", p=128)).then_inc(s["x_loaded"], 16)
            sp.dma_start(x[0:TS, 2, :], A["x_sample"].rearrange("b q d -> (b q) d")).then_inc(s["x_loaded"], 16)
            sp.dma_start(vraw[0:48, :], A["rw_mu"][0].rearrange("j (k c) -> (j k) c", c=128)).then_inc(s["vec_in"], 16)
            for n, name in enumerate(("rw_w0", "rw_a0", "rw_k_k", "rw_k_a", "rw_r_k", "rw_ln_g", "rw_ln_b")):
                v = A[name][0].rearrange("(k c) -> k c", c=128) if name != "rw_r_k" else A[name][0].rearrange("(k u) c -> k (u c)", u=2)
                sp.dma_start(vraw[48 + 6 * n:54 + 6 * n, :], v).then_inc(s["vec_in"], 16)
            chunk = 0

            def load_chunk(dst, src):
                nonlocal chunk
                if chunk >= 3:
                    sp.wait_ge(s["pj_ps"], tiles_through(chunk - 3))
                for d, a in zip(dst(wch[chunk % 3]), src):
                    sp.dma_start(d, a).then_inc(s[f"chunk_in{chunk % 3}"], 16)
                chunk += 1

            for l in range(DEPTH):
                if l == 0:
                    sp.dma_start(gain[:, :], A["norm_mix_g"][0:1, :].broadcast_to([128, D])).then_inc(s["gain_loaded"], 16)
                else:
                    sp.wait_ge(s["norm_h"], 6)
                    sp.dma_start(gain[:, :], A["norm_mix_g"][1:2, :].broadcast_to([128, D])).then_inc(s["gain_loaded"], 16)
                    sp.wait_ge(s["combined"], 2)
                    sp.dma_start(vraw[0:4, 0:96], A["gla_ab"][0].rearrange("(k c) -> k c", c=96)).then_inc(s["vec_in"], 16)
                    sp.dma_start(vraw[4:6, 0:96], A["gla_norm_g"][0].rearrange("(k c) -> k c", c=96)).then_inc(s["vec_in"], 16)
                sp.dma_start(mem, A["mem_prompt"][0].rearrange("(m p) d -> p m d", p=128)).then_inc(s["mm_in"], 16)
                sp.dma_start(gmem, A["norm_mem_g"][l:l + 1, :].broadcast_to([128, D])).then_inc(s["mm_in"], 16)
                load_chunk(lambda b: [k3(b, KT)], [A["w_mem_kv"][l].rearrange("(k p) n -> p k n", p=128)])
                if l == 0:
                    sp.dma_start(lw1, A["rw_w1"][0].rearrange("(k p) n -> p k n", p=128)).then_inc(s["lora_in"], 16)
                    sp.dma_start(la1, A["rw_a1"][0].rearrange("(k p) n -> p k n", p=128)).then_inc(s["lora_in"], 16)
                    sp.dma_start(lg1, A["rw_g1"][0].rearrange("(k p) n -> p k n", p=128)).then_inc(s["lora_in"], 16)
                    sp.dma_start(lw2[0:64, :], A["rw_w2"][0]).then_inc(s["lora_in"], 16)
                    sp.dma_start(la2[0:64, :], A["rw_a2"][0]).then_inc(s["lora_in"], 16)
                    sp.dma_start(lg2, A["rw_g2"][0]).then_inc(s["lora_in"], 16)
                else:
                    sp.dma_start(ga1, A["gla_a1"][0].rearrange("(k p) n -> p k n", p=128)).then_inc(s["lora_in"], 16)
                    sp.dma_start(ga2[0:16, :], A["gla_a2"][0]).then_inc(s["lora_in"], 16)
                for m in range(2):
                    sp.dma_start(KC[:, m], A["cache_mem_k"][l].rearrange("b (m p) h d -> m p b (h d)", p=128)[m]).then_inc(s["cache_k"], 16)
                    sp.dma_start(VC[:, m], A["cache_mem_v"][l].rearrange("b (m p) h d -> m p b (h d)", p=128)[m]).then_inc(s["cache_v"], 16)
                for c0, w in W_IN[l]:
                    load_chunk(lambda b: [k3(b[:, 0:KT * w], KT)], [A["w_in"][l].rearrange("(k p) n -> p k n", p=128)[:, :, c0:c0 + w]])
                for c0, w in W_OUT[l]:
                    if l == 0:
                        load_chunk(lambda b: [k3(b[:, 0:KT * w], KT)], [A["w_out"][l].rearrange("(k p) n -> p k n", p=128)[:, :, c0:c0 + w]])
                    else:
                        load_chunk(lambda b: [k3(b[0:96, 0:8 * w], 8), k3(b[:, 8 * w:10 * w], 2)],
                                   [A["w_out"][l][0:TOK, c0:c0 + w].rearrange("(k p) n -> p k n", p=96),
                                    A["w_out"][l][TOK:D, c0:c0 + w].rearrange("(k p) n -> p k n", p=128)])
                sp.wait_ge(s["x_out"], l + 1)
                sp.wait_ge(s["out_stored"], 16 * OUT_STORES[l])
                sp.dma_start(wr[:, :, 0:4], A["router_wg"][l].rearrange("(k p) n -> p k n", p=128)).then_inc(s["router_w"], 16)
                sp.dma_start(wr[:, :, 4:36], A["router_we"][l].rearrange("(k p) n -> p k n", p=128)).then_inc(s["router_w"], 16)
                sp.dma_start(br[:, 0:4], A["router_bg"][l:l + 1, :].broadcast_to([128, 4])).then_inc(s["router_w"], 16)
                sp.dma_start(br[:, 4:36], A["router_be"][l:l + 1, :].broadcast_to([128, 32])).then_inc(s["router_w"], 16)
                sp.dma_start(gain[:, :], A["norm_ffn_g"][l:l + 1, :].broadcast_to([128, D])).then_inc(s["gain_loaded"], 16)
                for j in range(2):
                    load_expert(sp, j, j, l, s[f"wup{j}"], s[f"wdn{j}"])
                with sp.Fori(1, NE // 2) as i:
                    for j in range(2):
                        sp.wait_ge(s["m_up_ps"], NE * l + 2 * i + j - 1)
                        sp.dma_start(wup[j], A["exp_w_up"][l, bass.ds(2 * i + j, 1)].rearrange("e (k p) n -> p (e k) n", p=128)).then_inc(s[f"wup{j}"], 16)
                        sp.wait_ge(s["m_dn_ps"], NE * l + 2 * i + j - 1)
                        sp.dma_start(wdn[j], A["exp_w_down"][l, bass.ds(2 * i + j, 1)].rearrange("e (k p) n -> p (e k) n", p=128)).then_inc(s[f"wdn{j}"], 16)
                sp.wait_ge(s["flag"], l + 1)
                more = sp.value_load(flag_i[0:1, 0:1], min_val=0, max_val=1)
                with sp.If(more > 0):
                    sp.wait_ge(s["m_dn_ps"], NE * (l + 1))
                    with sp.Fori(0, NE) as e:
                        sp.wait_ge(s[f"rdn{l}"], STEPS_REST * e)
                        load_expert(sp, e, 0, l, s[f"rw{l}"], s[f"rw{l}"])
                    sp.wait_ge(s[f"rdn{l}"], STEPS_REST * NE)
                with sp.Else():
                    sp.nop()
            sp.wait_ge(s["norm_h"], 12)
            sp.dma_start(gain[:, :], A["norm_final_g"].rearrange("(a d) -> a d", a=1).broadcast_to([128, D])).then_inc(s["gain_loaded"], 16)
            sp.wait_ge(s["norm_h"], 15)
            sp.dma_start(O["y_prompt"][0].rearrange("(t p) d -> p t d", p=128), h[:, 0:2, :]).then_inc(s["stored"], 16)
            sp.dma_start(O["y_sample"].rearrange("b q d -> (b q) d"), h[0:TS, 2, :]).then_inc(s["stored"], 16)
            sp.wait_ge(s["stored"], 32)
            sp.wait_ge(s["kv_stored"], 64)
            sp.wait_ge(s["shift_stored"], 32)

        @block.gpsimd
        def _(pool):
            link = chain(pool, s["pool_chain"])
            link(pool.memset(ident[:, :], 0.0))
            link(pool.affine_select(out=ident[:, :], in_=ident[:, :], compare_op=ALU.not_equal, fill=1.0, base=0,
                                    pattern=[[-1, 128]], channel_multiplier=1))
            pool.memset(ones[:, :], 1.0)
            link(pool.memset(before[:, :], 1.0))
            link(pool.affine_select(out=before[:, :], in_=before[:, :], compare_op=ALU.is_gt, fill=0.0, base=0,
                                    pattern=[[1, 128]], channel_multiplier=-1))
            pool.iota(iota_rank[:, :], pattern=[[1, CAP + RROWS]], base=0, channel_multiplier=0, allow_small_or_imprecise_dtypes=True)
            pool.iota(iota_e[:, :], pattern=[[1, NE]], base=0, channel_multiplier=0, allow_small_or_imprecise_dtypes=True)
            pool.iota(iota_g[:, :], pattern=[[1, GROUPS], [0, NE // GROUPS]], base=0, channel_multiplier=0, allow_small_or_imprecise_dtypes=True)
            pool.memset(cst[:, 0:1], EPS)
            link(pool.memset(valid[:, :], 1.0))
            link(pool.affine_select(out=valid[:, 2:3], in_=valid[:, 2:3], compare_op=ALU.is_gt, fill=0.0, base=TS,
                                    pattern=[[0, 1]], channel_multiplier=-1))
            link(pool.memset(upto[:, :], 1.0))
            link(pool.affine_select(out=upto[:, :], in_=upto[:, :], compare_op=ALU.is_ge, fill=0.0, base=0,
                                    pattern=[[1, 128]], channel_multiplier=-1))
            pool.iota(mlow[:, :], pattern=[[1, 8], [0, 16]], base=0, channel_multiplier=0, allow_small_or_imprecise_dtypes=True)
            pool.iota(moff1[:, :], pattern=[[1, 4], [0, 32]], base=0, channel_multiplier=0, allow_small_or_imprecise_dtypes=True)
            pool.iota(moff2[:, :], pattern=[[1, 2], [0, 64]], base=0, channel_multiplier=0, allow_small_or_imprecise_dtypes=True)
            for b in range(TS):
                link(pool.tensor_copy(sel[:, b, :], ident[0:TS, b:b + 1].broadcast_to([TS, 128])))
            pool.memset(cst[:, 2:3], GN_EPS)
            pool.memset(cst[:, 3:4], 16 * LN2)
            pool.memset(cst[:, 1:2], 0.0).then_inc(s["consts"], 1)

            pool.wait_ge(s["consts"], 1)

            def mixer0():
                pool.wait_ge(s["norm_h"], 3)
                pool.dma_start(O["prompt_rwkv_shift"][0], h[127:128, 1, :]).then_inc(s["shift_stored"], 16)
                pool.dma_start(O["sample_rwkv_shift"][0], h[0:TS, 2, :]).then_inc(s["shift_stored"], 16)
                store_kv(0)
                pool.wait_ge(s["at_ps"], 1)
                pool.dma_start(shn[0:TS, :], A["state_rwkv_shift"][0]).then_inc(s["shift_in"], 16)
                for n in range(6):
                    pool.wait_ge(s["qn"], n + 2)
                    pool.dma_start(dscr[n].rearrange("(b c) -> b c", b=TS), Dn[n % 2]).then_inc(s[f"dec_scr{n % 2}"], 16)
                pool.wait_ge(s["t_dve"], T_SCALED)
                pool.wait_ge(s["shift_stored"], 32)
                for m in mats:
                    pool.memset(m, 0.0)
                link(pool.memset(cst[:, 4:5], 0.0))
                for c in range(NCH):
                    for i, (dst, src) in enumerate(((cAT, vkk), (cBT, vb), (cKT, vk), (cRT, vr), (cX4, vv))):
                        if c > 0 and i == 0:
                            pool.wait_ge(s["c_ps"], c_ps_at(c - 1, "Z", 1))
                            pool.wait_ge(s["c_dve"], c_at(c - 1, "Z", 1))
                        for u in range(2):
                            rows = slice(64 * u, 64 * u + 64)
                            last = pool.tensor_copy(dst[rows, :, 64 * u:64 * u + 64], src[rows, :, C * c:C * (c + 1)])
                    last.then_inc(s["c_pool"], 1)
                pool.wait_ge(s["t_act"], T_STATE_OUT)
                for u in range(2):
                    pool.dma_start(O["prompt_rwkv_S"][0, 0].rearrange("(q u) i j -> u i q j", u=2)[u], cX2[64 * u:64 * u + 64, :, 64 * u:64 * u + 64]).then_inc(s["out_stored"], 16)
                for n in range(2):
                    pool.wait_ge(s[f"dec_scr{n}"], 48)
                pool.dma_start(DS.rearrange("p i j -> p (i j)"), A["state_rwkv_S"][0].rearrange("b h i j -> (b h) (i j)")).then_inc(s["dec_in"], 16)
                pool.dma_start(Dv, dscr.rearrange("v (p j) -> p v j", j=64)).then_inc(s["dec_in"], 16)
                pool.wait_ge(s["dec_sum"], 1)
                pool.dma_start(O["sample_rwkv_S"][0].rearrange("b h i j -> (b h) (i j)"), DS.rearrange("p i j -> p (i j)")).then_inc(s["out_stored"], 16)
                pool.wait_ge(s["dec_sum"], 2)
                pool.dma_start(yscr.rearrange("(p i) -> p i", i=64), Dy).then_inc(s["dec_y"], 16)
                pool.wait_ge(s["dec_y"], 16)
                pool.dma_start(Dn[0], yscr.rearrange("(b c) -> b c", b=TS)).then_inc(s["dec_y"], 16)

            def mixer1():
                pool.wait_ge(s["combined"], 2)
                pool.wait_ge(s["sat_out"], 2)
                pool.dma_start(gS[0:96, :, :, :].rearrange("p b h e -> p (b h) e"), A["state_gla_S"][0].rearrange("b h d e -> d (b h) e")).then_inc(s["dec_in"], 16)
                store_kv(1)
                pool.wait_ge(s["dec_sum"], 3)
                pool.dma_start(O["sample_gla_S"][0].rearrange("b h d e -> d (b h) e"), gS[0:96, :, :, :].rearrange("p b h e -> p (b h) e")).then_inc(s["out_stored"], 16)
                pool.wait_ge(s["c_dve"], C_TOTAL + 2 * NCH)
                pool.dma_start(O["prompt_gla_S"][0, 0].rearrange("h d e -> d h e"), gZ[0:96]).then_inc(s["out_stored"], 16)

            def store_kv(l):
                pool.wait_ge(s["pj_out"], 2 + (tiles_through(CHUNKS[0] - 1) if l else 0))
                pool.dma_start(O["prompt_mem_k"][l, 0].rearrange("(m p) h d -> p m (h d)", p=128), kvn[:, :, 0:MEMW]).then_inc(s["kv_stored"], 16)
                pool.dma_start(O["prompt_mem_v"][l, 0].rearrange("(m p) h d -> p m (h d)", p=128), kvn[:, :, MEMW:2 * MEMW]).then_inc(s["kv_stored"], 16)

            def write_rows(dst, row, it, par, s_nat, s_wr):
                pool.wait_ge(s_nat, it + 1)
                pool.dma_start(dst[bass.ds(row, CAP), :], ynat[par][0:CAP, :]).then_inc(s_wr, 16)

            def gather_rows(src, index, k, s_done):
                for t, (_, n) in enumerate(TILES):
                    pool.indirect_dma_start(yg[0:n, t, :], None, src, bass.IndirectOffsetOnAxis(ap=index[0:n, 2 * t + k:2 * t + k + 1], axis=0)).then_inc(s_done, 16)

            for l in range(DEPTH):
                (mixer0, mixer1)[l]()
                with pool.Fori(0, NE // 2) as i:
                    for j in range(2):
                        write_rows(rows_first[l], (2 * i + j) * CAP, NE * l + 2 * i + j, j, s["m_nat"], s[f"m_ywr{j}"])
                pool.wait_ge(s["flag"], l + 1)
                more = pool.value_load(flag_i[0:1, 0:1], min_val=0, max_val=1)
                with pool.If(more > 0):
                    with pool.Fori(0, NE) as e:
                        for b in range(STEPS_REST):
                            write_rows(rows_rest[l], e * RROWS + CAP * b, STEPS_REST * e + b, b % 2, s[f"rnat{l}"], s[f"ryw{'ab'[b % 2]}{l}"])
                    pool.wait_ge(s[f"rywa{l}"], 8 * STEPS_REST * NE)
                    pool.wait_ge(s[f"rywb{l}"], 8 * STEPS_REST * NE)
                    for k in range(2):
                        if k == 1 or l == 1:
                            pool.wait_ge(s["combined"], 2 * l)
                            pool.wait_ge(s[f"rcomb{l}"], k)
                        gather_rows(rows_rest[l], rows_r, k, s[f"rgath{l}"])
                    pool.wait_ge(s[f"rcomb{l}"], 2)
                with pool.Else():
                    pool.nop()
                for j in range(2):
                    pool.wait_ge(s[f"m_ywr{j}"], 8 * NE * (l + 1))
                for k in range(2):
                    if k == 1:
                        pool.wait_ge(s["combined"], 2 * l + 1)
                    elif l == 1:
                        pool.wait_ge(s["combined"], 2)
                    gather_rows(rows_first[l], rows_i, k, s["gathered"])

        NEEDS = {"X2": ("NT",), "X2T": ("NT",), "U1": ("X2T", "NT"), "UT1": ("X2T", "NT"), "X4": ("X2T",), "X4T": ("X2T",),
                 "U2": ("X4T", "UT1"), "UT2": ("X4T", "UT1"), "X8T": ("X4T",), "U3": ("X8T", "UT2"), "UT3": ("X8T", "UT2"),
                 "W1": ("U3",), "U4": ("W1", "UT3"), "UT4": ("W1", "UT3"), "W2": ("U4",), "U5": ("W2", "UT4"),
                 "RHS": ("Vn", "MT"), "SA": ("RHS", "U5"), "Y": ("SA", "QT"), "Z": ("SA",)}

        @block.tensor
        def _(pe):
            def transpose_h(n):
                pe.wait_ge(s["norm_h"], 3 * n)
                pe.wait_ge(s["pj_out"], tn[0])
                for k in range(KT):
                    if 8 * (n - 1) + k >= 2:
                        pe.wait_ge(s["hT"], 8 * (n - 1) + k - 1)
                    for t, (c, m) in enumerate(TILES):
                        last = pe.transpose(ps[k % 2][:, c:c + m], h[0:m, t, k * 128:(k + 1) * 128], ident[0:m, 0:m])
                    last.then_inc(s["hT_ps"], 1)

            tn = [0]

            def bank():
                if tn[0] >= 2:
                    pe.wait_ge(s["pj_out"], tn[0] - 1)
                return ps[tn[0] % 2]

            def tile_done(last):
                tn[0] += 1
                last.then_inc(s["pj_ps"], 1)

            wc = [0]

            def chunk_in(n_dmas=1):
                g = wc[0]
                wc[0] += 1
                b = g % 3
                got[b] += 16 * n_dmas
                pe.wait_ge(s[f"chunk_in{b}"], got[b])
                return wch[b]
            got = [0, 0, 0]

            def product(w, m, rhs, kt=KT, rows=128, n=T):
                p = bank()
                for k in range(kt):
                    last = pe.matmul(p[0:m, 0:n], w(k), rhs(k), start=(k == 0), stop=(k == kt - 1))
                tile_done(last)

            def attention(l):
                for k in range(KT):
                    pe.wait_ge(s["mm_h"], 2 * (l + 1))
                    if k >= 2:
                        pe.wait_ge(s["mm_T"], KT * l + k - 1)
                    for m in range(2):
                        last = pe.transpose(ps[2 + k % 2][:, 128 * m:128 * (m + 1)], mem[:, m, k * 128:(k + 1) * 128], ident[:, :])
                    last.then_inc(s["mm_T_ps"], 1)
                pe.wait_ge(s["mm_T"], KT * (l + 1))
                w = k3(chunk_in(), KT)
                for m in range(2):
                    product(lambda k: memT[:, k, 128 * m:128 * (m + 1)], 128, lambda k: w[:, k, :], n=2 * MEMW)
                pe.wait_ge(s["pj_out"], tn[0])
                for hp in range(2):
                    for m in range(2):
                        last = pe.transpose(ps[2][:, 256 * hp + 128 * m:256 * hp + 128 * (m + 1)], kvn[:, m, 128 * hp:128 * (hp + 1)], ident[:, :])
                last.then_inc(s["kT_ps"], 1)
                transpose_h(2 * l + 1)
                pe.wait_ge(s["hT"], KT * (2 * l + 1))
                w = k3(chunk_in()[:, 0:KT * 256], KT)
                for q in range(2):
                    product(lambda k: w[:, k, 128 * q:128 * (q + 1)], 128, lambda k: hT[:, k, :])
                pe.wait_ge(s["pj_out"], tn[0])
                pe.wait_ge(s["kT"], l + 1)
                pe.wait_ge(s["vecT"], l + 1)
                for hd in range(4):
                    rows = slice(64 * (hd % 2), 64 * (hd % 2) + 64)
                    for t in range(2):
                        last = pe.matmul(ps[4 + hd][:, 256 * t:256 * (t + 1)], qT[rows, hd // 2, 128 * t:128 * (t + 1)], kT[rows, hd // 2, :],
                                         start=True, stop=True)
                    last.then_inc(s["sc_ps"], 1)
                for q in range(2):
                    last = pe.transpose(ps[3][0:TS, 128 * q:128 * (q + 1)], qT[:, q, TP:T], ident[:, :])
                last.then_inc(s["qn_ps"], 1)
                for hd in range(4):
                    pe.wait_ge(s["sc_prob"], 4 * l + hd + 1)
                    for m in range(2):
                        for t in range(2):
                            last = pe.transpose(ps[4 + hd][:, 256 * m + 128 * t:256 * m + 128 * (t + 1)], P[:, hd, t, 128 * m:128 * (m + 1)], ident[:, :])
                    last.then_inc(s["pT_ps"], 1)
                for hd in range(4):
                    pe.wait_ge(s["pT"], 4 * l + hd + 1)
                    rows = slice(64 * (hd % 2), 64 * (hd % 2) + 64)
                    for m in range(2):
                        last = pe.matmul(ps[2][rows, 256 * (hd // 2):256 * (hd // 2 + 1)], kvn[:, m, MEMW + 64 * hd:MEMW + 64 * (hd + 1)], PT[:, hd, m, :],
                                         start=(m == 0), stop=(m == 1))
                last.then_inc(s["at_ps"], 1)
                pe.wait_ge(s["qn"], l * 7 + 1)
                for b in range(TS):
                    last = pe.matmul(ps[4 + b // 2][:, 256 * (b % 2):256 * (b % 2 + 1)], sel[:, b, :], qs[0:TS, :], start=True, stop=True)
                last.then_inc(s["qb_ps"], 1)
                pe.wait_ge(s["s_score"], l + 1)
                for m in range(2):
                    last = pe.transpose(ps[3][0:32, 128 * m:128 * (m + 1)], sc_s[:, 32 * m:32 * (m + 1)], ident[:, :])
                last.then_inc(s["sT_ps"], 1)
                pe.wait_ge(s["s_prob"], l + 1)
                for m in range(2):
                    last = pe.transpose(ps[3][:, 32 * m:32 * (m + 1)], sp_s[0:32, 128 * m:128 * (m + 1)], ident[0:32, 0:32])
                last.then_inc(s["spT_ps"], 1)
                pe.wait_ge(s["spT"], l + 1)
                pe.wait_ge(s["cache_v"], 32 * (l + 1))
                pe.wait_ge(s["at_out"], l + 1)
                for hp in range(2):
                    for b in range(TS):
                        for m in range(2):
                            last = pe.matmul(ps[2][:, 32 * hp + 4 * b:32 * hp + 4 * b + 4], VC[:, m, b, 128 * hp:128 * (hp + 1)],
                                             spT[:, 32 * m + 4 * b:32 * m + 4 * b + 4], start=(m == 0), stop=(m == 1))
                last.then_inc(s["sat_ps"], 1)

            def output(l):
                for c0, w in W_OUT[l]:
                    buf = chunk_in(1 + l)
                    for t, (c, m) in enumerate(TILES):
                        p = bank()
                        for n, (i, _, rows) in enumerate(wo_tiles[l]):
                            if l == 0:
                                wk = buf[0:rows, w * i:w * (i + 1)]
                            else:
                                wk = buf[0:rows, w * i:w * (i + 1)]
                            last = pe.matmul(p[0:m, 0:w], mixedT[0:rows, i, c:c + m], wk, start=(n == 0), stop=(n == len(wo_tiles[l]) - 1))
                        tile_done(last)

            def head_sums(src, n):
                for q in range(PAIRS):
                    last = pe.matmul(ps[2 + q][:, 0:T], block64[:, :], src[:, q, :], start=True, stop=True)
                last.then_inc(s["sum_ps"], 1)

            def mixer0():
                pe.wait_ge(s["shift_in"], 16)
                pe.wait_ge(s["sat_out"], 1)
                for k in range(KT):
                    last = pe.transpose(ps[7][:, TS * k:TS * (k + 1)], shn[0:TS, 128 * k:128 * (k + 1)], ident[0:TS, 0:TS])
                last.then_inc(s["shiftT_ps"], 1)
                n = 0
                for _, w in W_IN[0][1:]:
                    buf = k3(chunk_in()[:, 0:KT * w], KT)
                    for i in range(w // 128):
                        xi = n // PAIRS
                        pe.wait_ge(s["xj"], xi + 1)
                        product(lambda k: buf[:, k, 128 * i:128 * (i + 1)], 128, lambda k: TT[1 + xi % 2][:, k, :])
                        n += 1
                pe.wait_ge(s["lora_in"], 96)
                for xi, (w, m) in enumerate(((lw1, 64), (la1, 64), (lg1, 128))):
                    pe.wait_ge(s["xj"], xi + 4)
                    product(lambda k: w[:, k, :], m, lambda k: TT[1 + (xi + 3) % 2][:, k, :])
                base = tn[0]
                pe.wait_ge(s["lora_s"], 1)
                for q in range(PAIRS):
                    product(lambda k: lw2[0:64, 128 * q:128 * (q + 1)], 128, lambda k: w1o[0:64, :], kt=1)
                pe.wait_ge(s["pj_out"], base - 1)
                for q in range(PAIRS):
                    product(lambda k: la2[0:64, 128 * q:128 * (q + 1)], 128, lambda k: a1o[0:64, :], kt=1)
                pe.wait_ge(s["lora_s"], 2)
                for q in range(PAIRS):
                    product(lambda k: lg2[:, 128 * q:128 * (q + 1)], 128, lambda k: g1o, kt=1)
                pe.wait_ge(s["t_dve"], 1)
                head_sums(vL, 1)
                pe.wait_ge(s["t_dve"], 3)
                head_sums(TT[0], 2)
                pe.wait_ge(s["t_dve"], 5)
                for n, src in enumerate((vr, vk, vv, vkk, vb, TT[2])):
                    if n == 5:
                        pe.wait_ge(s["t_act"], 2)
                    if n >= 1:
                        pe.wait_ge(s["qn"], n + 1)
                    for q in range(PAIRS):
                        last = pe.transpose(ps[2 + q // 3][0:TS, 128 * (q % 3):128 * (q % 3 + 1)], src[:, q, TP:T], ident[:, :])
                    last.then_inc(s["qn_ps"], 1)

                def group(c, name, *mms, tr=False):
                    n = ORDER.index(name)
                    for hf in range(2):
                        for o in NEEDS.get(name, ()):
                            pe.wait_ge(s["c_" + dict(ROUNDS)[o]], c_at(c, o, hf))
                        g = len(ROUNDS) * c + n - 4
                        if g >= 0:
                            cc, nm = g // len(ROUNDS), ORDER[g % len(ROUNDS)]
                            pe.wait_ge(s["c_" + dict(ROUNDS)[nm]], c_at(cc, nm, hf))
                        b = ps[2 * (n % 4) + hf]
                        for q in range(3):
                            out = b[:, 128 * q:128 * (q + 1)]
                            for i, (lt, rh) in enumerate(mms):
                                if tr:
                                    last = pe.transpose(out, lt[:, 3 * hf + q, :], ident[:, :])
                                else:
                                    last = pe.matmul(out, lt[:, 3 * hf + q, :], rh[:, 3 * hf + q, :], start=(i == 0), stop=(i == len(mms) - 1))
                        last.then_inc(s["c_ps"], 1)

                assert len(ROUNDS) % 4 == 0
                for c in range(NCH):
                    pe.wait_ge(s["c_pool"], c + 1)
                    if c == 0:
                        pe.wait_ge(s["pj_out"], tn[0])
                        pe.wait_ge(s["qn"], 7)
                        pe.wait_ge(s["t_dve"], T_SCALED)
                    group(c, "N", (cAT, cBT))
                    group(c, "NT", (cBT, cAT))
                    group(c, "Bn", (cBT, None), tr=True)
                    group(c, "Kn", (cKT, None), tr=True)
                    group(c, "Vn", (cX4, None), tr=True)
                    group(c, "X2", (cN, cNT))
                    group(c, "X2T", (cNT, cN))
                    group(c, "MT", (cKT, cAT))
                    group(c, "U1", (cX2T, cUa))
                    group(c, "UT1", (cUa, cX2T))
                    group(c, "X4", (cX2T, cX2))
                    group(c, "X4T", (cX2, cX2T))
                    group(c, "PT", (cBT, cRT))
                    group(c, "U2", (cX4T, cUb))
                    group(c, "UT2", (cUb, cX4T))
                    group(c, "X8T", (cX4, cX4T))
                    group(c, "QT", (cKT, cRT))
                    group(c, "U3", (cX2T, cUa))
                    group(c, "UT3", (cUa, cX2T))
                    group(c, "W1", (cN1, cUb))
                    group(c, "U4", (cUTb, cX2))
                    group(c, "UT4", (cX2, cUTb))
                    group(c, "W2", (cN2, cUa))
                    group(c, "U5", (cUTa, cX4))
                    if c == 0:
                        pe.wait_ge(s["c_pool"], 1)
                    else:
                        for hf in range(2):
                            pe.wait_ge(s["c_dve"], c_at(c - 1, "Z", hf))
                    group(c, "RHS", (cAT, cZ), (cN, cVn))
                    group(c, "SA", (cUb, cX4T))
                    group(c, "Y", (cZ, cRT), (cX2T, cNT), (cVn, cQT))
                    group(c, "Z", (cBn, cX2T), (cKn, cVn))
                for hf in range(2):
                    pe.wait_ge(s["c_dve"], c_at(NCH - 1, "Z", hf))
                    pe.wait_ge(s["c_act"], c_at(NCH - 1, "Y", hf))
                for q in range(PAIRS):
                    last = pe.transpose(ps[2 + q // 3][:, 128 * (q % 3):128 * (q % 3 + 1)], cZ[:, q, :], ident[:, :])
                last.then_inc(s["qn_ps"], 1)
                pe.wait_ge(s["dec_y"], 32)
                for q in range(PAIRS):
                    last = pe.transpose(ps[4][:, TS * q:TS * (q + 1)], Dn[0][:, 128 * q:128 * (q + 1)], ident[0:TS, 0:TS])
                last.then_inc(s["qn_ps"], 1)
                pe.wait_ge(s["t_act"], T_STATE_OUT)
                pe.wait_ge(s["t_act"], 5)
                head_sums(vL, 3)
                pe.wait_ge(s["t_dve"], 8)
                head_sums(TT[1], 4)
                pe.wait_ge(s["t_dve"], 9)

            def mixer1():
                n = 0
                for _, w in W_IN[1][1:]:
                    buf = k3(chunk_in()[:, 0:KT * w], KT)
                    for i in range(w // 96):
                        product(lambda k: buf[:, k, 96 * i:96 * (i + 1)], 96, lambda k: hT[:, k, :])
                pe.wait_ge(s["lora_in"], 128)
                product(lambda k: ga1[:, k, :], 16, lambda k: hT[:, k, :])
                pe.wait_ge(s["pj_out"], tn[0])
                for i in range(4):
                    product(lambda k: ga2[0:16, 96 * i:96 * (i + 1)], 96, lambda k: ga1o[0:16, :], kt=1)
                pe.wait_ge(s["pj_out"], tn[0])
                for i in range(8):
                    last = pe.transpose(ps[2 + i // 4][0:TS, 96 * (i % 4):96 * (i % 4 + 1)], gv[0:96, i, TP:T], ident[0:96, 0:96])
                last.then_inc(s["qn_ps"], 1)
                pe.wait_ge(s["qn"], 9)
                for b in range(TS):
                    pe.wait_ge(s["dec_mul"], b + 1)
                    for u in range(2):
                        last = pe.matmul(ps[2 + 2 * (b % 2) + u][0:96, 0:384], sel[:, b, 0:96], gvs[0:TS, 384 * u:384 * (u + 1)], start=True, stop=True)
                    last.then_inc(s["qb_ps"], 1)
                pe.wait_ge(s["dec_sum"], 3)
                for b in range(TS):
                    for i in range(8):
                        last = pe.matmul(ps[6][0:96, TS * i + b:TS * i + b + 1], gS[0:96, b, i // 2, 96 * (i % 2):96 * (i % 2 + 1)],
                                         gq[0:96, i // 2, TP + b:TP + b + 1], start=True, stop=True)
                last.then_inc(s["sat_ps"], 1)
                pe.wait_ge(s["t_dve"], 14)
                for c in range(NCH):
                    cc = slice(C * c, C * (c + 1))
                    if c > 0:
                        pe.wait_ge(s["c_act"], C_ACT + 2 * c)
                    for i in range(8):
                        pe.transpose(ps[2 + i // 4][0:C, 96 * (i % 4):96 * (i % 4 + 1)], gv[0:96, i, cc], ident[0:96, 0:96])
                    for i in range(4):
                        last = pe.transpose(ps[4][0:C, 96 * i:96 * (i + 1)], gkh[0:96, i, cc], ident[0:96, 0:96])
                    last.then_inc(s["c_ps"], 1)
                    if c > 0:
                        pe.wait_ge(s["c_dve"], C_TOTAL + 2 * c)
                    for i in range(4):
                        last = pe.matmul(ps[5][0:C, C * i:C * (i + 1)], gk[0:96, i, cc], gq[0:96, i, cc], start=True, stop=True)
                    last.then_inc(s["c_ps"], 1)
                    pe.wait_ge(s["c_act"], C_ACT + 2 * c + 1)
                    pe.wait_ge(s["c_dve"], C_TOTAL + 2 * c + 1)
                    for i in range(8):
                        o = ps[6][0:96, C * i:C * (i + 1)]
                        pe.matmul(o, gvn[0:C, 96 * i:96 * (i + 1)], gatt[0:C, i // 2, :], start=True, stop=False)
                        last = pe.matmul(o, gZm[0:96, i // 2, 96 * (i % 2):96 * (i % 2 + 1)], gq[0:96, i // 2, cc], start=False, stop=True)
                    last.then_inc(s["c_ps"], 1)
                    for i in range(4):
                        last = pe.matmul(ps[7 if i < 2 else 5][0:96, 192 * (i % 2):192 * (i % 2 + 1)], gkn[0:C, 96 * i:96 * (i + 1)], gvn[0:C, 192 * i:192 * (i + 1)],
                                         start=True, stop=True)
                    last.then_inc(s["c_ps"], 1)
                pe.wait_ge(s["t_dve"], 15)
                for i in range(4):
                    for u in range(2):
                        last = pe.matmul(ps[2 + i][0:96, 0:T], ones[0:96, 0:96], gv[0:96, 2 * i + u, :], start=(u == 0), stop=(u == 1))
                last.then_inc(s["sum_ps"], 1)
                pe.wait_ge(s["t_dve"], 16)

            def gather(par, ks, s_done=None):
                for k in ks:
                    n = 0
                    for t, (_, m) in enumerate(TILES):
                        for part in hp:
                            last = pe.matmul(ps[par][:, k * CAP:(k + 1) * CAP], part[0:m, t, k * 128:(k + 1) * 128], G[par][0:m, t, :],
                                             start=(n == 0), stop=(n == 8))
                            n += 1
                if s_done is not None:
                    last.then_inc(s_done, 1)

            def up(par, sl, s_gate, s_up):
                for half, sd in ((0, s_gate), (1, s_up)):
                    for k in range(KT):
                        last = pe.matmul(ps[2 + half][0:CAP, :], xgT[par][:, k, :], wup[sl][:, k, half * FF:(half + 1) * FF],
                                         start=(k == 0), stop=(k == KT - 1))
                    last.then_inc(sd, 1)

            def act_T(s_done):
                for f in range(4):
                    last = pe.transpose(ps[5][:, f * 128:(f + 1) * 128], an[:, f * 128:(f + 1) * 128], ident[:, :])
                last.then_inc(s_done, 1)

            def down(sl, s_done):
                for half in range(2):
                    for f in range(4):
                        last = pe.matmul(ps[6 + half][0:CAP, :], actT[:, f, :], wdn[sl][:, f, half * FF:(half + 1) * FF],
                                         start=(f == 0), stop=(f == 3))
                last.then_inc(s_done, 1)

            pe.wait_ge(s["consts"], 1)
            pe.wait_ge(s["vec_in"], 16 * 8)
            pe.transpose(ps[7][:, 0:90], vraw[0:90, :], ident[0:90, 0:90]).then_inc(s["vecT_ps"], 1)
            for n, m in enumerate((mlow, moff1, moff2)):
                last = pe.transpose(ps[6][:, 128 * n:128 * (n + 1)], m[:, :], ident[:, :])
            last.then_inc(s["vecT_ps"], 1)
            for l in range(DEPTH):
                if l == 1:
                    pe.wait_ge(s["vec_in"], 16 * 10)
                    pe.transpose(ps[7][0:96, 0:6], vraw[0:6, 0:96], ident[0:6, 0:6]).then_inc(s["vecT_ps"], 1)
                attention(l)
                (mixer0, mixer1)[l]()
                output(l)
                transpose_h(2 * l + 2)
                pe.wait_ge(s["hT"], 8 * (2 * l + 2))
                pe.wait_ge(s["router_w"], 64 * (l + 1))
                for t, (c, m) in enumerate(TILES):
                    for k in range(KT):
                        last = pe.matmul(ps[2][0:m, t * 36:(t + 1) * 36], hT[:, k, c:c + m], wr[:, k, :], start=(k == 0), stop=(k == KT - 1))
                last.then_inc(s["logit_ps"], 1)
                pe.wait_ge(s["gates"], l + 1)
                for t, (c, m) in enumerate(TILES):
                    for u in range(t + 1):
                        mu = TILES[u][1]
                        last = pe.matmul(ps[3][:, t * NE:(t + 1) * NE], (before if u == t else ones)[0:mu, :], asum[0:mu, u, :],
                                         start=(u == 0), stop=(u == t))
                last.then_inc(s["rank_ps"], 1)
                pe.wait_ge(s["ranks"], l + 1)
                pe.transpose(ps[3][0:1, 256:384], flagf[:, 0:1], ident[:, :]).then_inc(s["flagT_ps"], 1)

                base, gb = NE * l, (NE + 1) * l
                pe.wait_ge(s["h_parts"], l + 1)
                pe.wait_ge(s["m_G"], gb + 1)
                gather(0, range(KT), s["m_xg_ps"])

                def pair(i, first):
                    for j in range(2):
                        it, g = base + 2 * i + j, gb + 2 * i + j
                        pe.wait_ge(s[f"wup{j}"], 16 * (NE // 2) * l + 16 * (i + 1))
                        pe.wait_ge(s["m_xgT"], g + 1)
                        up(j, j, s["m_gate_ps"], s["m_up_ps"])
                        pe.wait_ge(s["m_G"], g + 2)
                        if not (first and j == 0):
                            pe.wait_ge(s["m_xgT"], g)
                        gather(1 - j, range(0, 5))
                        pe.wait_ge(s["m_act"], it + 1)
                        act_T(s["m_actT_ps"])
                        gather(1 - j, range(5, KT), s["m_xg_ps"])
                        pe.wait_ge(s[f"wdn{j}"], 16 * (NE // 2) * l + 16 * (i + 1))
                        pe.wait_ge(s["m_actT"], it + 1)
                        if not (first and j == 0):
                            pe.wait_ge(s["m_nat"], it)
                        down(j, s["m_dn_ps"])

                pair(0, True)
                with pe.Fori(1, NE // 2) as i:
                    pair(i, False)

                pe.wait_ge(s["flag"], l + 1)
                more = pe.value_load(flag_i[0:1, 0:1], min_val=0, max_val=1)
                r = lambda n: s[f"r{n}{l}"]
                with pe.If(more > 0):
                    pe.wait_ge(s["m_nat"], NE * (l + 1))
                    pe.wait_ge(s["m_xgT"], (NE + 1) * (l + 1))
                    with pe.Fori(0, NE) as e:
                        pe.wait_ge(r("w"), 32 * (e + 1))
                        for b in range(STEPS_REST):
                            it = STEPS_REST * e + b
                            pe.wait_ge(r("G"), it + 1)
                            gather(b % 2, range(KT), r("xg"))
                            pe.wait_ge(r("xgT"), it + 1)
                            up(b % 2, 0, r("gate"), r("up"))
                            pe.wait_ge(r("act"), it + 1)
                            act_T(r("atps"))
                            pe.wait_ge(r("actT"), it + 1)
                            pe.wait_ge(r("nat"), it)
                            down(0, r("dn"))
                with pe.Else():
                    pe.nop()

        @block.scalar
        def _(act):
            link = chain(act, s["act_chain"])

            def norm_scale(n):
                for t, (_, m) in enumerate(TILES):
                    act.wait_ge(s["norm_ss"], 3 * (n - 1) + t + 1)
                    link(act.activation(st[0:m, 4 + t:5 + t], st[0:m, t:t + 1], ACT.Ln, scale=1.0 / D, bias=cst[0:m, 0:1]))
                    act.activation(st[0:m, 8 + t:9 + t], st[0:m, 4 + t:5 + t], ACT.Exp, scale=-0.5).then_inc(s["norm_rs"], 1)

            def copy_hT(n):
                for k in range(KT):
                    act.wait_ge(s["hT_ps"], 8 * (n - 1) + k + 1)
                    act.copy(hT[:, k, :], ps[k % 2][:, 0:T]).then_inc(s["hT"], 1)

            def xg_out(it, par, s_in, s_done):
                act.wait_ge(s_in, it + 1)
                act.copy(xgT[par].rearrange("p k n -> p (k n)"), ps[par][:, 0:KT * CAP]).then_inc(s_done, 1)

            def exp_gate(it, s_in, s_done):
                act.wait_ge(s_in, it + 1)
                act.activation(ex[0:CAP, :], ps[2][0:CAP, :], ACT.Exp, scale=-1.0).then_inc(s_done, 1)

            def actT_out(it, s_in, s_done):
                act.wait_ge(s_in, it + 1)
                act.copy(actT, ps[5][:, :].rearrange("p (f n) -> p f n", f=4)[:, :, 0:CAP]).then_inc(s_done, 1)

            tn = [0]

            def out(dst, m, n=T, func=ACT.Copy, **kw):
                act.wait_ge(s["pj_ps"], tn[0] + 1)
                act.activation(dst, ps[tn[0] % 2][0:m, 0:n], func, **kw).then_inc(s["pj_out"], 1)
                tn[0] += 1

            def attention(l):
                for m in range(2):
                    act.wait_ge(s["mm_ss"], 2 * l + m + 1)
                    link(act.activation(mm_st[:, 2 + m:3 + m], mm_st[:, m:m + 1], ACT.Ln, scale=1.0 / D, bias=cst[:, 0:1]))
                    act.activation(mm_st[:, 4 + m:5 + m], mm_st[:, 2 + m:3 + m], ACT.Exp, scale=-0.5).then_inc(s["mm_rs"], 1)
                norm_scale(2 * l + 1)
                for k in range(KT):
                    act.wait_ge(s["mm_T_ps"], KT * l + k + 1)
                    act.copy(memT[:, k, :], ps[2 + k % 2][:, 0:N_MEM]).then_inc(s["mm_T"], 1)
                for m in range(2):
                    out(kvn[:, m, :], 128, n=2 * MEMW)
                act.wait_ge(s["kT_ps"], l + 1)
                act.copy(kT, ps[2][:, :].rearrange("p (a b) -> p a b", a=2)).then_inc(s["kT"], 1)
                copy_hT(2 * l + 1)
                for q in range(2):
                    out(qT[:, q, :], 128)
                act.wait_ge(s["qn_ps"], 9 * l + 1)
                act.copy(qs[0:TS, :], ps[3][0:TS, 0:MEMW]).then_inc(s["qn"], 1)
                for hd in range(4):
                    act.wait_ge(s["sc_max"], 4 * l + hd + 1)
                    for t in range(2):
                        n = 2 * hd + t
                        last = act.activation(P[:, hd, t, :], ps[4 + hd][:, 256 * t:256 * (t + 1)], ACT.Exp, scale=0.125, bias=snx[:, n:n + 1],
                                              accum_out=ssm[:, n:n + 1])
                    last.then_inc(s["sc_exp"], 1)
                for hd in range(4):
                    act.wait_ge(s["pT_ps"], 4 * l + hd + 1)
                    act.copy(PT[:, hd].rearrange("p m t -> p (m t)"), ps[4 + hd][:, :]).then_inc(s["pT"], 1)
                m0 = KT - 2 if l == 0 else KT
                act.wait_ge(s["at_ps"], l + 1)
                act.copy(mixedT[:, m0:m0 + 2, 0:TP], ps[2][:, :].rearrange("p (a b) -> p a b", a=2)).then_inc(s["at_out"], 1)
                act.wait_ge(s["s_max"], l + 1)
                act.activation(sp_s[0:32, :], ps[3][0:32, 0:N_MEM], ACT.Exp, scale=0.125, bias=snx[0:32, 0:1], accum_out=ssm[0:32, 0:1]).then_inc(s["s_exp"], 1)
                act.wait_ge(s["spT_ps"], l + 1)
                act.copy(spT, ps[3][:, 0:64]).then_inc(s["spT"], 1)
                act.wait_ge(s["sat_ps"], l + 1)
                for hp in range(2):
                    for u in range(2):
                        rows = slice(64 * u, 64 * u + 64)
                        last = act.copy(mixedT[rows, m0 + hp, TP:T], ps[2][rows, 32 * hp + 2 * hp + u:32 * hp + 32:4])
                last.then_inc(s["sat_out"], 1)

            def mixer0():
                act.wait_ge(s["sat_out"], 1)
                for dst in (vr, vk, vv):
                    for q in range(PAIRS):
                        out(dst[:, q, :], 128)
                act.wait_ge(s["vecT"], 1)
                out(w1o[0:64, :], 64, func=ACT.Exp, scale=-2.0)
                out(a1o[0:64, :], 64)
                out(g1o, 128, func=ACT.Exp, scale=-1.0)
                for q in range(PAIRS):
                    out(vld[:, q, :], 128, func=ACT.Exp, scale=-1.0, bias=nvec[:, q:q + 1])
                for q in range(PAIRS):
                    out(vb[:, q, :], 128, func=ACT.Exp, scale=-1.0, bias=nvec[:, PAIRS + q:PAIRS + q + 1])
                for q in range(PAIRS):
                    out(vg[:, q, :], 128)
                act.wait_ge(s["t_dve"], 2)
                link(act.activation(vL, vL, ACT.Ln, scale=2.0 ** 32))
                act.activation(vL, vL, ACT.Exp, scale=-0.5, bias=cst[:, 3:4]).then_inc(s["t_act"], 1)
                act.wait_ge(s["t_dve"], 4)
                act.activation(TT[2][:, 0:PAIRS, TP:T], vld[:, :, TP:T], ACT.Exp)
                act.activation(TT[2][:, 0:PAIRS, 0:TP], TT[2][:, 0:PAIRS, 0:TP], ACT.Exp)
                act.activation(TT[1][:, 0:PAIRS, 0:TP], vL[:, :, 0:TP], ACT.Exp).then_inc(s["t_act"], 1)
                act.wait_ge(s["t_dve"], 5)
                act.activation(TT[0][:, 0:PAIRS, 0:TP], vL[:, :, 0:TP], ACT.Exp, scale=-1.0).then_inc(s["t_act"], 1)
                for n in range(6):
                    act.wait_ge(s["qn_ps"], n + 2)
                    if n >= 2:
                        act.wait_ge(s[f"dec_scr{n % 2}"], 16 * (n // 2))
                    for u in range(2):
                        last = act.copy(Dn[n % 2][:, 384 * u:384 * (u + 1)], ps[2 + u][0:TS, 0:384])
                    last.then_inc(s["qn"], 1)

                dst = {"Bn": cBn, "Kn": cKn, "Vn": cVn, "X2": cX2, "X2T": cX2T, "X4": cX4, "X4T": cX4T, "X8T": cX2T, "W1": cX2, "W2": cX4,
                       "RHS": cX4T, "SA": cX2T}
                act.wait_ge(s["c_pool"], 1)
                for c in range(NCH):
                    for name, e in ROUNDS:
                        if e != "act":
                            continue
                        for hf in range(2):
                            act.wait_ge(s["c_ps"], c_ps_at(c, name, hf))
                            b = ps[2 * (ORDER.index(name) % 4) + hf]
                            pairs = slice(3 * hf, 3 * hf + 3)
                            if name == "Y":
                                for u in range(2):
                                    rows = slice(64 * u, 64 * u + 64)
                                    last = act.copy(vL[rows, pairs, C * c:C * (c + 1)],
                                                    b[rows, 0:384].rearrange("p (q n) -> p q n", q=3)[:, :, 64 * u:64 * u + 64])
                            else:
                                last = act.copy(dst[name][:, pairs, :], b[:, 0:384].rearrange("p (q n) -> p q n", q=3))
                            last.then_inc(s["c_act"], 1)
                act.wait_ge(s["qn_ps"], 8)
                for u in range(2):
                    last = act.copy(cX2[:, 3 * u:3 * u + 3, :], ps[2 + u][:, 0:384].rearrange("p (q n) -> p q n", q=3))
                last.then_inc(s["t_act"], 1)
                act.wait_ge(s["qn_ps"], 9)
                act.copy(vL[:, :, TP:T], ps[4][:, 0:TS * PAIRS].rearrange("p (q b) -> p q b", q=PAIRS)).then_inc(s["t_act"], 1)
                act.wait_ge(s["sum_ps"], 4)
                for q in range(PAIRS):
                    link(act.activation(TT[1][:, q, :], ps[2 + q][:, 0:T], ACT.Ln, scale=1.0 / 64, bias=cst[:, 2:3]))
                act.activation(TT[1][:, 0:PAIRS, :], TT[1][:, 0:PAIRS, :], ACT.Exp, scale=-0.5).then_inc(s["t_act"], 1)

            def mixer1():
                act.wait_ge(s["sat_out"], 2)
                act.wait_ge(s["kv_stored"], 64)
                for i in range(4):
                    out(gq[0:96, i, :], 96, scale=96.0 ** -0.5)
                for i in range(4):
                    out(gk[0:96, i, :], 96)
                for i in range(8):
                    out(gv[0:96, i, :], 96)
                for i in range(8):
                    out(grt[0:96, i, :], 96)
                out(ga1o[0:16, :], 16)
                act.wait_ge(s["vecT"], 2)
                for i in range(4):
                    out(gl[0:96, i, :], 96, func=ACT.Identity, bias=vecT[0:96, i:i + 1])
                act.wait_ge(s["qn_ps"], 11)
                for u in range(2):
                    last = act.copy(gvs[0:TS, 384 * u:384 * (u + 1)], ps[2 + u][0:TS, 0:384])
                last.then_inc(s["qn"], 1)
                act.wait_ge(s["t_dve"], 10)
                link(act.activation(ge[0:96], ge[0:96], ACT.Exp, scale=-1.0))
                act.activation(ge[0:96], ge[0:96], ACT.Ln, bias=ones[0:96, 0:1]).then_inc(s["t_act"], 1)
                act.wait_ge(s["t_dve"], 11)
                act.activation(gkh[0:96, :, TP:T], gl[0:96, :, TP:T], ACT.Exp).then_inc(s["t_act"], 1)
                act.wait_ge(s["t_dve"], 12)
                act.activation(gem[0:96, :], gem[0:96, :], ACT.Exp)
                act.activation(gee[0:96, :], gee[0:96, :], ACT.Exp)
                g0, g1 = go[0:96, 0:4, 0:TP], go[0:96, 4:8, 0:TP]
                act.activation(gkh[0:96, :, 0:TP], g1, ACT.Exp).then_inc(s["t_act"], 1)
                act.wait_ge(s["t_dve"], 13)
                act.activation(g1, g0, ACT.Exp, scale=-1.0)
                link(act.activation(gl[0:96, :, 0:TP], g0, ACT.Exp))
                act.nop()
                act.sem_inc(s["t_act"], 1)
                act.wait_ge(s["sat_ps"], 3)
                act.wait_ge(s["t_dve"], 14)
                act.copy(go[0:96, :, TP:T], ps[6][0:96, 0:64].rearrange("p (i b) -> p i b", b=TS)).then_inc(s["sat_out"], 1)
                for c in range(NCH):
                    act.wait_ge(s["c_ps"], 2 * len(ROUNDS) * NCH + 4 * c + 1)
                    for u in range(2):
                        act.copy(gvn[0:C, 384 * u:384 * (u + 1)], ps[2 + u][0:C, 0:384])
                    act.copy(gkn[0:C, :], ps[4][0:C, 0:384]).then_inc(s["c_act"], 1)
                    act.wait_ge(s["c_ps"], 2 * len(ROUNDS) * NCH + 4 * c + 3)
                    act.copy(go[0:96, :, C * c:C * (c + 1)], ps[6][0:96, :].rearrange("p (i n) -> p i n", i=8)).then_inc(s["c_act"], 1)
                act.wait_ge(s["sum_ps"], 5)
                for i in range(4):
                    link(act.activation(ge[0:96, i, :], ps[2 + i][0:96, 0:T], ACT.Ln, scale=1.0 / 192, bias=cst[0:96, 0:1]))
                act.activation(ge[0:96], ge[0:96], ACT.Exp, scale=-0.5).then_inc(s["t_act"], 1)
                act.activation(gv[0:96], grt[0:96], ACT.Exp, scale=-1.0).then_inc(s["t_act"], 1)

            for l in range(DEPTH):
                if l == 0:
                    act.wait_ge(s["consts"], 1)
                attention(l)
                (mixer0, mixer1)[l]()
                tn[0] += 3 * len(W_OUT[l])
                norm_scale(2 * l + 2)
                copy_hT(2 * l + 2)
                act.wait_ge(s["logits"], l + 1)
                for t in range(3):
                    act.activation(gt[:, t, 0:4], gt[:, t, 0:4], ACT.Exp)
                act.activation(gt[:, :, 4], gt[:, :, 4], ACT.Exp).then_inc(s["gate_e"], 1)
                base, gb = NE * l, (NE + 1) * l
                xg_out(gb, 0, s["m_xg_ps"], s["m_xgT"])

                def pair(i, first):
                    for j in range(2):
                        it = base + 2 * i + j
                        exp_gate(it, s["m_gate_ps"], s["m_exp"])
                        actT_out(it, s["m_actT_ps"], s["m_actT"])
                        xg_out(gb + 2 * i + j + 1, 1 - j, s["m_xg_ps"], s["m_xgT"])

                pair(0, True)
                with act.Fori(1, NE // 2) as i:
                    pair(i, False)
                act.wait_ge(s["flag"], l + 1)
                more = act.value_load(flag_i[0:1, 0:1], min_val=0, max_val=1)
                r = lambda n: s[f"r{n}{l}"]
                with act.If(more > 0):
                    with act.Fori(0, NE) as e:
                        for b in range(STEPS_REST):
                            it = STEPS_REST * e + b
                            xg_out(it, b % 2, r("xg"), r("xgT"))
                            exp_gate(it, r("gate"), r("exp"))
                            actT_out(it, r("atps"), r("actT"))
                with act.Else():
                    act.nop()
            norm_scale(5)

        @block.vector
        def _(dve):
            link = chain(dve, s["dve_chain"])

            def norm(n, out):
                if n == 1:
                    dve.wait_ge(s["x_loaded"], 32)
                for t, (_, m) in enumerate(TILES):
                    dve.tensor_tensor_reduce(sq[0:m, :], x[0:m, t, :], x[0:m, t, :], 1.0, 0.0, ALU.mult, ALU.add, st[0:m, t:t + 1]).then_inc(s["norm_ss"], 1)
                    dve.wait_ge(s["norm_ss"], 3 * (n - 1) + t + 1)
                dve.wait_ge(s["gain_loaded"], 16 * n)
                for t, (_, m) in enumerate(TILES):
                    dve.wait_ge(s["norm_rs"], 3 * (n - 1) + t + 1)
                    dve.scalar_tensor_tensor(out=out[0:m, t, :], in0=x[0:m, t, :], scalar=st[0:m, 8 + t:9 + t], in1=gain[0:m, :],
                                             op0=ALU.mult, op1=ALU.mult).then_inc(s["norm_h"], 1)

            def route(l):
                link(dve.memset(lg, 0.0))
                link(dve.memset(g8, -BIG))
                dve.wait_ge(s["logit_ps"], l + 1)
                dve.wait_ge(s["router_w"], 64 * (l + 1))
                for t, (_, m) in enumerate(TILES):
                    link(dve.tensor_tensor(lg[0:m, t, :], ps[2][0:m, t * 36:(t + 1) * 36], br[0:m, :], ALU.add))
                link(dve.tensor_copy(g8[:, :, 0:4], lg[:, :, 0:4]))
                for t in range(3):
                    link(dve.max(m8[:, t, :], g8[:, t, :]))
                    link(dve.max_index(idx_u[:, t, :], m8[:, t, :], g8[:, t, :]))
                link(dve.tensor_copy(i8f, idx_u))
                link(dve.tensor_tensor(gt[:, :, 0:4], lg[:, :, 0:4], m8[:, :, 0:1].broadcast_to([128, 3, 4]), ALU.subtract))
                link(dve.tensor_tensor(tmp32, iota_g[:, :].unsqueeze(1).broadcast_to([128, 3, NE]), i8f[:, :, 0:1].broadcast_to([128, 3, NE]), ALU.is_equal))
                link(dve.tensor_scalar(tmp32, tmp32, -1.0, BIG, ALU.add, ALU.mult))
                link(dve.tensor_tensor(em, lg[:, :, 4:36], tmp32, ALU.add))
                for t in range(3):
                    link(dve.max(m8[:, t, :], em[:, t, :]))
                    link(dve.max_index(idx_u[:, t, :], m8[:, t, :], em[:, t, :]))
                link(dve.tensor_copy(i8f, idx_u))
                dve.tensor_tensor(gt[:, :, 4:5], m8[:, :, 1:2], m8[:, :, 0:1], ALU.subtract).then_inc(s["logits"], 1)
                for k, a in enumerate((a1, a2)):
                    link(dve.tensor_tensor(a, iota_e[:, :].unsqueeze(1).broadcast_to([128, 3, NE]), i8f[:, :, k:k + 1].broadcast_to([128, 3, NE]), ALU.is_equal))
                    link(dve.tensor_tensor(a, a, valid[:, :].unsqueeze(2).broadcast_to([128, 3, NE]), ALU.mult))
                dve.tensor_tensor(asum, a1, a2, ALU.add).then_inc(s["gates"], 1)
                dve.wait_ge(s["gate_e"], l + 1)
                link(dve.tensor_reduce(gt[:, :, 5:6], gt[:, :, 0:4], AXX, ALU.add))
                link(dve.tensor_scalar(gt[:, :, 6:7], gt[:, :, 4:5], 1.0, None, ALU.add))
                link(dve.tensor_tensor(gt[:, :, 5:6], gt[:, :, 5:6], gt[:, :, 6:7], ALU.mult))
                link(dve.reciprocal(gt[:, :, 6:7], gt[:, :, 5:6]))
                link(dve.tensor_tensor(gt[:, :, 7:8], gt[:, :, 6:7], gt[:, :, 4:5], ALU.mult))
                dve.wait_ge(s["rank_ps"], l + 1)
                link(dve.tensor_copy(rank, ps[3][:, 0:3 * NE].rearrange("p (t n) -> p t n", t=3)))
                for k, a in enumerate((a1, a2)):
                    link(dve.tensor_tensor(tmp32, rank, a, ALU.mult))
                    link(dve.tensor_reduce(rowf.rearrange("p (t n) -> p t n", t=3)[:, :, k:k + 1], tmp32, AXX, ALU.add))
                rank2 = rowf.rearrange("p (t n) -> p t n", t=3)
                v3 = lambda a: a[:, :].rearrange("p (t n) -> p t n", t=3)
                link(dve.tensor_scalar(in_rest[:, :], rowf, float(CAP), None, ALU.is_ge))
                link(dve.tensor_scalar(gr[:, :], rowf, float(CAP - 1), None, ALU.min))
                link(dve.scalar_tensor_tensor(out=v3(gr), in0=i8f[:, :, 0:2], scalar=float(CAP), in1=v3(gr), op0=ALU.mult, op1=ALU.add))
                link(dve.tensor_copy(rows_i[:, :], gr[:, :]))
                link(dve.tensor_scalar(gr[:, :], rowf, float(-CAP), 0.0, ALU.add, ALU.max))
                link(dve.scalar_tensor_tensor(out=v3(gr), in0=i8f[:, :, 0:2], scalar=float(RROWS), in1=v3(gr), op0=ALU.mult, op1=ALU.add))
                link(dve.tensor_copy(rows_r[:, :], gr[:, :]))
                link(dve.tensor_tensor(v3(gr), gt[:, :, 6:8], v3(in_rest), ALU.mult))
                link(dve.tensor_tensor(gt[:, :, 6:8], gt[:, :, 6:8], v3(gr), ALU.subtract))
                link(dve.memset(R, -1.0))
                link(dve.scalar_tensor_tensor(out=R[:, :, 0:NE], in0=rank, scalar=1.0, in1=asum, op0=ALU.add, op1=ALU.mult))
                link(dve.tensor_scalar(R[:, :, 0:NE], R[:, :, 0:NE], -1.0, None, ALU.add))
                dve.tensor_reduce(flagf[:, 0:1], R.rearrange("p t n -> p (t n)"), AXX, ALU.max).then_inc(s["ranks"], 1)
                dve.wait_ge(s["flagT_ps"], l + 1)
                link(dve.tensor_reduce(flagf[0:1, 1:2], ps[3][0:1, 256:384], AXX, ALU.max))
                link(dve.tensor_scalar(flagf[0:1, 2:3], flagf[0:1, 1:2], float(CAP), None, ALU.is_ge))
                dve.tensor_copy(flag_i[0:1, 0:1], flagf[0:1, 2:3]).then_inc(s["flag"], 1)

            def onehot(e, step, par, s_done):
                dve.tensor_tensor(G[par], iota_rank[:, CAP * step:CAP * (step + 1)].unsqueeze(1).broadcast_to([128, 3, CAP]),
                                  R[:, :, bass.ds(e, 1)].broadcast_to([128, 3, CAP]), ALU.is_equal).then_inc(s_done, 1)

            def swiglu(it, s_exp, s_up, s_done, s_chain, c0):
                dve.wait_ge(s_exp, it + 1)
                dve.tensor_scalar(ex[0:CAP, :], ex[0:CAP, :], 1.0, None, ALU.add).then_inc(s_chain, 1)
                dve.wait_ge(s_chain, c0 + 1)
                dve.reciprocal(rec[0:CAP, :], ex[0:CAP, :]).then_inc(s_chain, 1)
                dve.wait_ge(s_chain, c0 + 2)
                dve.tensor_tensor(sg[0:CAP, :], ps[2][0:CAP, :], rec[0:CAP, :], ALU.mult).then_inc(s_chain, 1)
                dve.wait_ge(s_chain, c0 + 3)
                dve.wait_ge(s_up, it + 1)
                dve.tensor_tensor(an[0:CAP, :], ps[3][0:CAP, :], sg[0:CAP, :], ALU.mult).then_inc(s_done, 1)

            def nat_out(it, par, s_in, s_done):
                dve.wait_ge(s_in, it + 1)
                dve.tensor_copy(ynat[par][0:CAP, 0:FF], ps[6][0:CAP, :])
                dve.tensor_copy(ynat[par][0:CAP, FF:D], ps[7][0:CAP, :]).then_inc(s_done, 1)

            def split_h():
                for t, (_, m) in enumerate(TILES):
                    a = h[0:m, t, :]
                    link(dve.tensor_copy(hp[0][0:m, t, :], a))
                    link(dve.tensor_tensor(sq[0:m, :], a, hp[0][0:m, t, :], ALU.subtract))
                    link(dve.tensor_copy(hp[1][0:m, t, :], sq[0:m, :]))
                    link(dve.tensor_tensor(sq[0:m, :], sq[0:m, :], hp[1][0:m, t, :], ALU.subtract))
                    last = link(dve.tensor_copy(hp[2][0:m, t, :], sq[0:m, :])) if t < 2 else dve.tensor_copy(hp[2][0:m, t, :], sq[0:m, :])
                last.then_inc(s["h_parts"], 1)

            def mark(ins, name, value):
                ins.then_inc(s[name], 1)
                dve.wait_ge(s[name], value)

            def setup():
                dve.wait_ge(s["vecT_ps"], 2)
                link(dve.tensor_copy(vecT[:, :], ps[7][:, 0:90]))
                link(dve.tensor_scalar(nvec[:, :], vecT[:, 48:60], -1.0, None, ALU.mult))
                for n, m in enumerate((mlow, moff1, moff2)):
                    link(dve.tensor_tensor(m[:, :], ps[6][:, 128 * n:128 * (n + 1)], m[:, :], ALU.is_equal))
                link(dve.tensor_copy(block64[:, :], moff2[:, :]))
                link(dve.tensor_tensor(mup[:, :], mlow[:, :], before[:, :], ALU.mult))
                link(dve.tensor_tensor(moff2[:, :], block64[:, :], moff1[:, :], ALU.subtract))
                link(dve.tensor_tensor(moff1[:, :], moff1[:, :], mlow[:, :], ALU.subtract))
                for m in (mlow, moff1, moff2):
                    link(dve.tensor_tensor(sq[:, 0:128], m[:, :], upto[:, :], ALU.mult))
                    link(dve.tensor_tensor(m[:, :], m[:, :], sq[:, 0:128], ALU.subtract))
                mark(dve.memset(sq[:, 0:1], 0.0), "vecT", 1)

            def attention(l):
                dve.wait_ge(s["mm_in"], 32 * (l + 1))
                for m in range(2):
                    mark(dve.tensor_tensor_reduce(sq, mem[:, m, :], mem[:, m, :], 1.0, 0.0, ALU.mult, ALU.add, mm_st[:, m:m + 1]), "mm_ss", 2 * l + m + 1)
                for m in range(2):
                    dve.wait_ge(s["mm_rs"], 2 * l + m + 1)
                    dve.scalar_tensor_tensor(out=mem[:, m, :], in0=mem[:, m, :], scalar=mm_st[:, 4 + m:5 + m], in1=gmem, op0=ALU.mult,
                                             op1=ALU.mult).then_inc(s["mm_h"], 1)
                norm(2 * l + 1, h)
                for hd in range(4):
                    dve.wait_ge(s["sc_ps"], 4 * l + hd + 1)
                    link(dve.tensor_reduce(smx[:, 2 * hd:2 * hd + 2], ps[4 + hd][:, :].rearrange("p (t m) -> p t m", t=2), AXX, ALU.max))
                    mark(dve.tensor_scalar(snx[:, 2 * hd:2 * hd + 2], smx[:, 2 * hd:2 * hd + 2], -0.125, None, ALU.mult), "sc_max", 4 * l + hd + 1)
                for hd in range(4):
                    dve.wait_ge(s["sc_exp"], 4 * l + hd + 1)
                    link(dve.reciprocal(srs[:, 2 * hd:2 * hd + 2], ssm[:, 2 * hd:2 * hd + 2]))
                    dve.tensor_tensor(P[:, hd], P[:, hd], srs[:, 2 * hd:2 * hd + 2].unsqueeze(2).broadcast_to([128, 2, N_MEM]),
                                      ALU.mult).then_inc(s["sc_prob"], 1)
                dve.wait_ge(s["qb_ps"], 1 if l == 0 else 2)
                dve.wait_ge(s["cache_k"], 32 * (l + 1))
                for m in range(2):
                    for b in range(0, TS, 2):
                        link(dve.tensor_tensor(KC[:, m, b:b + 2, :], KC[:, m, b:b + 2, :], ps[4 + b // 2][:, :].rearrange("p (b n) -> p b n", b=2), ALU.mult))
                mark(dve.tensor_reduce(sc_s, KC.rearrange("p m b (h d) -> p (m b h) d", d=64), AXX, ALU.add), "s_score", l + 1)
                dve.wait_ge(s["sT_ps"], l + 1)
                link(dve.tensor_reduce(smx[0:32, 0:1], ps[3][0:32, 0:N_MEM], AXX, ALU.max))
                mark(dve.tensor_scalar(snx[0:32, 0:1], smx[0:32, 0:1], -0.125, None, ALU.mult), "s_max", l + 1)
                dve.wait_ge(s["s_exp"], l + 1)
                link(dve.reciprocal(srs[0:32, 0:1], ssm[0:32, 0:1]))
                mark(dve.tensor_scalar(sp_s[0:32, :], sp_s[0:32, :], srs[0:32, 0:1], None, ALU.mult), "s_prob", l + 1)
                dve.wait_ge(s["sat_out"], l + 1)

            def output(l):
                n = tiles_through(CHUNKS[0] - 1 if l == 0 else sum(CHUNKS) - 1) - 3 * len(W_OUT[l])
                for c0, w in W_OUT[l]:
                    for t, (_, m) in enumerate(TILES):
                        dve.wait_ge(s["pj_ps"], n + 1)
                        mark(dve.tensor_tensor(x[0:m, t, c0:c0 + w], ps[n % 2][0:m, 0:w], x[0:m, t, c0:c0 + w], ALU.add), "pj_out", n + 1)
                        n += 1
                mark(dve.memset(sq[:, 0:1], 0.0), "x_out", l + 1)

            vec = lambda at: vecT[:, at:at + PAIRS].unsqueeze(2).broadcast_to([128, PAIRS, T])
            V_KK, V_KA, V_RK, V_LG, V_LB = 60, 66, 72, 78, 84

            def mixer0():
                T0, T1, T2 = (a[:, 0:PAIRS, :] for a in TT)
                xx = TT[0]
                dve.wait_ge(s["hT"], KT)
                dve.wait_ge(s["shiftT_ps"], 1)
                dve.tensor_tensor(xx[:, :, 1:TP], hT[:, :, 0:TP - 1], hT[:, :, 1:TP], ALU.subtract)
                dve.tensor_scalar(xx[:, :, 0:1], hT[:, :, 0:1], -1.0, None, ALU.mult)
                link(dve.tensor_tensor(xx[:, :, TP:T], ps[7][:, 0:KT * TS].rearrange("p (k b) -> p k b", k=KT), hT[:, :, TP:T], ALU.subtract))
                done = {2: 10, 3: 16, 4: 22, 5: 23}

                def blend(i, j):
                    if i in done:
                        dve.wait_ge(s["pj_ps"], done[i])
                    for k in range(KT):
                        last = dve.scalar_tensor_tensor(out=TT[1 + i % 2][:, k, :], in0=xx[:, k, :], scalar=vecT[:, 8 * j + k:8 * j + k + 1], in1=hT[:, k, :],
                                                        op0=ALU.mult, op1=ALU.add)
                    last.then_inc(s["xj"], 1)

                for i, j in enumerate((0, 2, 3, 1, 4)):
                    blend(i, j)
                    if i == 3:
                        dve.wait_ge(s["pj_out"], 16)
                        link(dve.tensor_tensor(vkk, vk, vec(V_KK), ALU.mult))
                        mark(dve.tensor_tensor(vL, vkk, vkk, ALU.mult), "t_dve", 1)
                dve.wait_ge(s["pj_out"], 23)
                link(dve.tensor_scalar(w1o[0:64, :], w1o[0:64, :], 1.0, None, ALU.add))
                link(dve.reciprocal(w1o[0:64, :], w1o[0:64, :]))
                mark(dve.tensor_scalar(w1o[0:64, :], w1o[0:64, :], 2.0, -1.0, ALU.mult, ALU.add), "lora_s", 1)
                blend(5, 5)
                dve.wait_ge(s["pj_out"], 25)
                link(dve.tensor_scalar(g1o, g1o, 1.0, None, ALU.add))
                mark(dve.reciprocal(g1o, g1o), "lora_s", 2)
                dve.wait_ge(s["sum_ps"], 1)
                for q in range(PAIRS):
                    link(dve.tensor_scalar(vL[:, q, :], ps[2 + q][:, 0:T], 1e-24, None, ALU.max))
                mark(dve.memset(sq[:, 0:1], 0.0), "t_dve", 2)
                dve.wait_ge(s["t_act"], 1)
                link(dve.tensor_tensor(vkk, vkk, vL, ALU.mult))
                dve.wait_ge(s["pj_out"], 31)
                link(dve.tensor_scalar(vld, vld, 1.0, None, ALU.add))
                link(dve.reciprocal(vL, vld))
                link(dve.tensor_scalar(vld, vL, -float(np.exp(-0.5)), None, ALU.mult))
                for q in range(PAIRS):
                    for c in range(NCH):
                        cc = slice(C * c, C * (c + 1))
                        last = dve.tensor_tensor_scan(vL[:, q, cc], ones[:, 0:C], vld[:, q, cc], 0.0, ALU.mult, ALU.add)
                link(last)
                dve.wait_ge(s["pj_out"], 37)
                link(dve.tensor_scalar(vb, vb, 1.0, None, ALU.add))
                link(dve.reciprocal(vb, vb))
                link(dve.tensor_scalar(T0, vb, -1.0, None, ALU.add))
                link(dve.tensor_tensor(T0, T0, vec(V_KA), ALU.mult))
                link(dve.scalar_tensor_tensor(out=vk, in0=T0, scalar=1.0, in1=vk, op0=ALU.add, op1=ALU.mult))
                link(dve.tensor_tensor(vb, vb, vkk, ALU.mult))
                link(dve.tensor_tensor(T0, vr, vk, ALU.mult))
                mark(dve.tensor_tensor(T0, T0, vec(V_RK), ALU.mult), "t_dve", 3)
                mark(dve.tensor_tensor(T2[:, :, 0:TP], vL[:, :, 0:TP], vld[:, :, 0:TP], ALU.subtract), "t_dve", 4)
                dve.wait_ge(s["sum_ps"], 2)
                dve.wait_ge(s["t_act"], 2)
                for q in range(PAIRS):
                    link(dve.tensor_tensor(vld[:, q, :], ps[2 + q][:, 0:T], vv[:, q, :], ALU.mult))
                mark(dve.memset(sq[:, 0:1], 0.0), "t_dve", 5)
                dve.wait_ge(s["t_act"], 3)
                pc = slice(0, TP)
                link(dve.tensor_copy(lam[:, :, :], T1[:, :, C - 1:TP:C]))
                link(dve.tensor_tensor(vr[:, :, pc], vr[:, :, pc], T1[:, :, pc], ALU.mult))
                link(dve.scalar_tensor_tensor(out=vkk[:, :, pc], in0=vkk[:, :, pc], scalar=-1.0, in1=T2[:, :, pc], op0=ALU.mult, op1=ALU.mult))
                link(dve.tensor_tensor(vk[:, :, pc], vk[:, :, pc], T0[:, :, pc], ALU.mult))
                dve.wait_ge(s["qn"], 7)
                mark(dve.tensor_tensor(vb[:, :, pc], vb[:, :, pc], T0[:, :, pc], ALU.mult), "t_dve", 6)

                I3 = ident[:, :].unsqueeze(1).broadcast_to([128, 3, 128])
                m3 = lambda m: m[:, :].unsqueeze(1).broadcast_to([128, 3, 128])
                adds = {"U1": (cUb, cUa), "UT1": (cUTb, cUTa), "U2": (cUa, cUb), "UT2": (cUTa, cUTb), "U3": (cUb, cUa), "UT3": (cUTb, cUTa),
                        "U4": (cUa, cUb), "UT4": (cUTa, cUTb), "U5": (cUb, cUa)}
                masks = {"MT": (cN, before), "PT": (cNT, upto), "QT": (cQT, upto)}
                dve.wait_ge(s["c_pool"], 1)
                for c in range(NCH):
                    for name, e in ROUNDS:
                        if e != "dve":
                            continue
                        for hf in range(2):
                            dve.wait_ge(s["c_ps"], c_ps_at(c, name, hf))
                            b = ps[2 * (ORDER.index(name) % 4) + hf][:, 0:384].rearrange("p (q n) -> p q n", q=3)
                            pp = slice(3 * hf, 3 * hf + 3)
                            tt = lambda o, a, b_, op: dve.tensor_tensor(o[:, pp, :], a, b_, op)
                            if name == "N":
                                link(tt(cN, b, m3(mlow), ALU.mult))
                                tt(cN1, b, m3(moff1), ALU.mult)
                                tt(cN2, b, m3(moff2), ALU.mult)
                                last = tt(cUTa, cN[:, pp, :], I3, ALU.add)
                            elif name == "NT":
                                link(tt(cNT, b, m3(mup), ALU.mult))
                                last = tt(cUa, cNT[:, pp, :], I3, ALU.add)
                            elif name in masks:
                                o, m = masks[name]
                                last = tt(o, b, m3(m), ALU.mult)
                            elif name == "Z":
                                link(tt(cZ, b, cZ[:, pp, :], ALU.add))
                                last = tt(cZ, cZ[:, pp, :], lam[:, pp, c:c + 1].broadcast_to([128, 3, 128]), ALU.mult)
                            else:
                                o, a = adds[name]
                                last = tt(o, b, a[:, pp, :], ALU.add)
                            mark(last, "c_dve", c_at(c, name, hf))
                dve.wait_ge(s["dec_in"], 32)
                row = lambda v: Dv[:, v, :].unsqueeze(1).broadcast_to([96, 64, 64])
                col = lambda a: a.unsqueeze(2).broadcast_to([96, 64, 64])
                link(dve.tensor_tensor(Dt, DS, row(3), ALU.mult))
                link(dve.tensor_reduce(Dsa, Dt, AXX, ALU.add))
                link(dve.tensor_tensor(DS, DS, row(5), ALU.mult))
                link(dve.tensor_tensor(Dt, row(4), col(Dsa), ALU.mult))
                link(dve.tensor_tensor(DS, DS, Dt, ALU.subtract))
                link(dve.tensor_tensor(Dt, row(1), col(Dv[:, 2, :]), ALU.mult))
                mark(dve.tensor_tensor(DS, DS, Dt, ALU.add), "dec_sum", 1)
                link(dve.tensor_tensor(Dt, DS, row(0), ALU.mult))
                mark(dve.tensor_reduce(Dy, Dt, AXX, ALU.add), "dec_sum", 2)
                dve.wait_ge(s["sum_ps"], 3)
                dve.wait_ge(s["dec_y"], 16)
                for q in range(PAIRS):
                    link(dve.scalar_tensor_tensor(out=T0[:, q, :], in0=ps[2 + q][:, 0:T], scalar=-1.0 / 64, in1=vL[:, q, :], op0=ALU.mult, op1=ALU.add))
                mark(dve.memset(sq[:, 0:1], 0.0), "t_dve", 7)
                mark(dve.tensor_tensor(T1, T0, T0, ALU.mult), "t_dve", 8)
                dve.wait_ge(s["t_act"], 6)
                link(dve.tensor_tensor(T0, T0, T1, ALU.mult))
                link(dve.tensor_tensor(T0, T0, vec(V_LG), ALU.mult))
                link(dve.tensor_tensor(T0, T0, vec(V_LB), ALU.add))
                link(dve.tensor_tensor(T0, T0, vld, ALU.add))
                mark(dve.tensor_tensor(mixedT[:, 0:PAIRS, :], T0, vg, ALU.mult), "t_dve", 9)

            def mixer1():
                g96 = lambda a: a[0:96]
                n = tiles_through(CHUNKS[0] + 7) + 5
                dve.wait_ge(s["pj_out"], n)
                mark(dve.scalar_tensor_tensor(out=g96(ge), in0=g96(gl), scalar=-1.0, in1=g96(gl), op0=ALU.mult, op1=ALU.max), "t_dve", 10)
                link(dve.tensor_scalar(g96(gl), g96(gl), 0.0, None, ALU.min))
                dve.wait_ge(s["t_act"], 7)
                link(dve.tensor_tensor(g96(gl), g96(gl), g96(ge), ALU.subtract))
                mark(dve.tensor_scalar(g96(gl), g96(gl), 1.0 / 16, None, ALU.mult), "t_dve", 11)
                for i in range(4):
                    for c in range(NCH):
                        cc = slice(C * c, C * (c + 1))
                        last = dve.tensor_tensor_scan(ge[0:96, i, cc], ones[0:96, 0:C], gl[0:96, i, cc], 0.0, ALU.mult, ALU.add)
                link(last)
                gep = ge[0:96, :, 0:TP]
                dve.tensor_copy(gem[0:96, :].rearrange("p (i c) -> p i c", i=4), ge[0:96, :, C // 2 - 1:TP:C])
                link(dve.tensor_copy(gee[0:96, :].rearrange("p (i c) -> p i c", i=4), ge[0:96, :, C - 1:TP:C]))
                g0, g1 = go[0:96, 0:4, 0:TP], go[0:96, 4:8, 0:TP]
                ic = lambda a: a.unsqueeze(2).broadcast_to([96, NCH, C])
                for i in range(4):
                    v4 = lambda a: a[:, i, :].rearrange("p (c n) -> p c n", c=NCH)
                    dve.tensor_tensor(v4(g1), ic(gee[0:96, NCH * i:NCH * (i + 1)]), v4(gep), ALU.subtract)
                    last = dve.tensor_tensor(v4(g0), v4(gep), ic(gem[0:96, NCH * i:NCH * (i + 1)]), ALU.subtract)
                mark(last, "t_dve", 12)
                dve.wait_ge(s["t_act"], 9)
                link(dve.tensor_tensor(gkh[0:96, :, 0:TP], gkh[0:96, :, 0:TP], gk[0:96, :, 0:TP], ALU.mult))
                mark(dve.memset(sq[:, 0:1], 0.0), "t_dve", 13)
                dve.wait_ge(s["t_act"], 10)
                link(dve.tensor_tensor(gq[0:96, :, 0:TP], gq[0:96, :, 0:TP], gl[0:96, :, 0:TP], ALU.mult))
                link(dve.tensor_tensor(gk[0:96, :, 0:TP], gk[0:96, :, 0:TP], g1, ALU.mult))
                dve.memset(gZ[0:96], 0.0)
                mark(dve.memset(gZm[0:96], 0.0), "t_dve", 14)
                dve.wait_ge(s["dec_in"], 48)
                for b in range(TS):
                    mark(dve.tensor_tensor(gS[0:96, b], gS[0:96, b], gkh[0:96, :, TP + b:TP + b + 1].broadcast_to([96, 4, 192]), ALU.mult), "dec_mul", b + 1)
                    if b > 0:
                        state_add(b - 1)
                state_add(TS - 1)
                mark(dve.memset(sq[:, 0:1], 0.0), "dec_sum", 3)
                cp = 2 * len(ROUNDS) * NCH
                for c in range(NCH):
                    dve.wait_ge(s["c_ps"], cp + 4 * c + 2)
                    mark(dve.tensor_tensor(gatt[0:C], ps[5][0:C, 0:4 * C].rearrange("p (i t) -> p i t", i=4),
                                           upto[0:C, 0:C].unsqueeze(1).broadcast_to([C, 4, C]), ALU.mult), "c_dve", C_TOTAL + 2 * c + 1)
                    dve.wait_ge(s["c_ps"], cp + 4 * c + 4)
                    for i in range(4):
                        link(dve.scalar_tensor_tensor(out=gZ[0:96, i, :], in0=gZ[0:96, i, :], scalar=gee[0:96, NCH * i + c:NCH * i + c + 1],
                                                      in1=ps[7 if i < 2 else 5][0:96, 192 * (i % 2):192 * (i % 2 + 1)], op0=ALU.mult, op1=ALU.add))
                        if c < NCH - 1:
                            link(dve.tensor_scalar(gZm[0:96, i, :], gZ[0:96, i, :], gem[0:96, NCH * i + c + 1:NCH * i + c + 2], None, ALU.mult))
                    mark(dve.memset(sq[:, 0:1], 0.0), "c_dve", C_TOTAL + 2 * c + 2)
                dve.wait_ge(s["c_act"], C_ACT + 2 * NCH)
                dve.wait_ge(s["sat_out"], 3)
                mark(dve.tensor_tensor(gv[0:96], go[0:96], go[0:96], ALU.mult), "t_dve", 15)
                dve.wait_ge(s["t_act"], 11)
                o4 = go[0:96].rearrange("p (i u) t -> p i u t", u=2)
                for i in range(4):
                    for u in range(2):
                        last = dve.scalar_tensor_tensor(out=o4[:, i, u, :], in0=o4[:, i, u, :], scalar=vecT[0:96, 4 + u:5 + u], in1=ge[0:96, i, :], op0=ALU.mult, op1=ALU.mult)
                link(last)
                dve.wait_ge(s["t_act"], 12)
                link(dve.tensor_scalar(gv[0:96], gv[0:96], 1.0, None, ALU.add))
                link(dve.reciprocal(gv[0:96], gv[0:96]))
                link(dve.tensor_tensor(grt[0:96], grt[0:96], gv[0:96], ALU.mult))
                mark(dve.tensor_tensor(mixedT[0:96, 0:8, :], go[0:96], grt[0:96], ALU.mult), "t_dve", 16)

            def state_add(b):
                dve.wait_ge(s["qb_ps"], 3 + b)
                for i in range(4):
                    last = dve.scalar_tensor_tensor(out=gS[0:96, b, i, :], in0=ps[2 + 2 * (b % 2) + i // 2][0:96, 192 * (i % 2):192 * (i % 2 + 1)],
                                                    scalar=gk[0:96, i, TP + b:TP + b + 1], in1=gS[0:96, b, i, :], op0=ALU.mult, op1=ALU.add)
                link(last)

            def add_rows(gate):
                for t, (_, m) in enumerate(TILES):
                    last = dve.scalar_tensor_tensor(out=x[0:m, t, :], in0=yg[0:m, t, :], scalar=gate(t, m), in1=x[0:m, t, :],
                                                    op0=ALU.mult, op1=ALU.add)
                return last

            dve.wait_ge(s["consts"], 1)
            setup()
            for l in range(DEPTH):
                if l == 1:
                    dve.wait_ge(s["vecT_ps"], 3)
                    mark(dve.tensor_copy(vecT[0:96, 0:6], ps[7][0:96, 0:6]), "vecT", 2)
                attention(l)
                (mixer0, mixer1)[l]()
                output(l)
                norm(2 * l + 2, h)
                route(l)
                link(dve.memset(an, 0.0))
                split_h()
                base, gb = NE * l, (NE + 1) * l
                onehot(0, 0, 0, s["m_G"])
                onehot(1, 0, 1, s["m_G"])
                cm = 3 * base

                def pair(i, first, final=False):
                    for j in range(2):
                        it, g = base + 2 * i + j, gb + 2 * i + j
                        swiglu(it, s["m_exp"], s["m_up_ps"], s["m_act"], s["m_swi"], 3 * it)
                        if not (final and j == 1):
                            dve.wait_ge(s["m_xg_ps"], g + 1)
                            onehot(2 * i + j + 2, 0, j, s["m_G"])
                        if not (first and l == 0):
                            dve.wait_ge(s[f"m_ywr{j}"], 16 * (base // 2 + i))
                        nat_out(it, j, s["m_dn_ps"], s["m_nat"])

                pair(0, True)
                with dve.Fori(1, NE // 2 - 1) as i:
                    pair(i, False)
                pair(NE // 2 - 1, False, final=True)
                dve.wait_ge(s["flag"], l + 1)
                more = dve.value_load(flag_i[0:1, 0:1], min_val=0, max_val=1)
                r = lambda n: s[f"r{n}{l}"]
                with dve.If(more > 0):
                    dve.wait_ge(s["m_xg_ps"], (NE + 1) * (l + 1))
                    for j in range(2):
                        dve.wait_ge(s[f"m_ywr{j}"], 8 * NE * (l + 1))
                    with dve.Fori(0, NE) as e:
                        for b in range(STEPS_REST):
                            it = STEPS_REST * e + b
                            onehot(e, b + 1, b % 2, r("G"))
                            swiglu(it, r("exp"), r("up"), r("act"), r("swi"), 3 * it)
                            dve.wait_ge(s[f"ryw{'ab'[b % 2]}{l}"], 16 * (STEPS_REST // 2 * e + b // 2))
                            nat_out(it, b % 2, r("dn"), r("nat"))
                    for k in range(2):
                        dve.wait_ge(s[f"rgath{l}"], 48 * (k + 1))
                        add_rows(lambda t, m: gr[0:m, 2 * t + k:2 * t + k + 1]).then_inc(s[f"rcomb{l}"], 1)
                        dve.wait_ge(s[f"rcomb{l}"], k + 1)
                with dve.Else():
                    dve.nop()
                for k in range(2):
                    dve.wait_ge(s["gathered"], 96 * l + 48 * (k + 1))
                    add_rows(lambda t, m: gt[0:m, t, 6 + k:7 + k]).then_inc(s["combined"], 1)
                    dve.wait_ge(s["combined"], 2 * l + k + 1)
            norm(5, h)


_OUTS = [("y_prompt", (1, 256, 1024)), ("y_sample", (8, 1, 1024)), ("prompt_rwkv_S", (1, 1, 12, 64, 64)), ("prompt_rwkv_shift", (1, 1, 1024)),
         ("prompt_gla_S", (1, 1, 4, 96, 192)), ("prompt_mem_k", (2, 1, 256, 4, 64)), ("prompt_mem_v", (2, 1, 256, 4, 64)),
         ("sample_rwkv_S", (1, 8, 12, 64, 64)), ("sample_rwkv_shift", (1, 8, 1024)), ("sample_gla_S", (1, 8, 4, 96, 192))]


def kernel(**inputs):
    import concourse.bacc as _bacc
    from concourse.bass_utils import run_bass_kernel_spmd as _run

    nc = _bacc.Bacc("TRN2", target_bir_lowering=False, num_devices=1)
    arrays, A, O = {}, {}, {}
    for name, v in inputs.items():
        a = np.ascontiguousarray(v)
        arrays[f"in_{name}"] = a
        A[name] = nc.dram_tensor(f"in_{name}", a.shape, mybir.dt.from_np(a.dtype), kind="ExternalInput").ap()
    for name, shape in _OUTS:
        O[name] = nc.dram_tensor(f"out_{name}", shape, F32, kind="ExternalOutput").ap()
    build(nc, A, O)
    r = _run(nc, [arrays], core_ids=[0])
    return tuple(r.results[0][f"out_{name}"] for name, _ in _OUTS)
```

```python
from contextlib import ExitStack

import numpy as np
import concourse.bass as bass
from concourse import mybir

ALU = mybir.AluOpType
ACT = mybir.ActivationFunctionType
F32 = mybir.dt.float32
F32R = mybir.dt.float32r
BF16 = mybir.dt.bfloat16
I32 = mybir.dt.int32
U32 = mybir.dt.uint32
AXX = mybir.AxisListType.X

D = 1024
KT = D // 128
TP = 256
TS = 8
T = TP + TS
TOK = 768
MEMW = 256
N_MEM = 256
C = 64
NCH = TP // C
PAIRS = TOK // 128
TILES = [(0, 128), (128, 128), (256, TS)]
DEPTH = 2
NE = 32
GROUPS = 4
FF = 512
CAP = 64
SLOT = D // 128 * D + FF // 128 * D
UNITS = D // 128 + FF // 128
UNITS_UP = D // 128
RING = 8
STEPS_REST = 4
RROWS = CAP * STEPS_REST
EPS = 1e-6
GN_EPS = 64e-5
LN2 = 0.6931471805599453
BIG = 1e30

W_IN = [[(2304, 256), (0, 512), (512, 512), (1024, 512), (1536, 512), (2048, 256)],
        [(2304, 256)] + [(384 * n, 384) for n in range(6)]]
W_OUT = [[(0, 512), (512, 512)], [(256 * n, 256) for n in range(4)]]
TILE_W = [128, 96]
LORA_TILES = [3 + 3 * PAIRS, 1 + 4]
CHUNKS = [1 + len(W_IN[l]) + len(W_OUT[l]) for l in range(2)]


def tiles_through(g):
    total, n = 0, 0
    for l in range(DEPTH):
        parts = [2, 2] + [w // TILE_W[l] for _, w in W_IN[l][1:]] + [3] * len(W_OUT[l])
        for i, m in enumerate(parts):
            if i == 1 + len(W_IN[l]):
                total += LORA_TILES[l]
            total += m
            if n == g:
                return total
            n += 1


ROUNDS = [("N", "dve"), ("NT", "dve"), ("Bn", "act"), ("Kn", "act"), ("Vn", "act"), ("X2", "act"), ("X2T", "act"),
          ("MT", "dve"), ("U1", "dve"), ("UT1", "dve"), ("X4", "act"), ("X4T", "act"), ("PT", "dve"), ("U2", "dve"),
          ("UT2", "dve"), ("X8T", "act"), ("QT", "dve"), ("U3", "dve"), ("UT3", "dve"), ("W1", "act"), ("U4", "dve"),
          ("UT4", "dve"), ("W2", "act"), ("U5", "dve"), ("RHS", "act"), ("SA", "act"), ("Y", "act"), ("Z", "dve")]
ORDER = [n for n, _ in ROUNDS]


def c_ps_at(c, name, half):
    return 2 * (len(ROUNDS) * c + ORDER.index(name)) + half + 1


def c_at(c, name, half):
    mine = [n for n, e in ROUNDS if e == dict(ROUNDS)[name]]
    return 2 * (len(mine) * c + mine.index(name)) + half + 1


C_TOTAL = 2 * NCH * sum(e == "dve" for _, e in ROUNDS)
C_ACT = 2 * NCH * sum(e == "act" for _, e in ROUNDS)
T_SCALED = 6
T_STATE_OUT = 4
REST = {"pe": ("xg", "up", "actT_ps", "down"), "act": ("xs_high", "gate_low", "up_low", "tanh", "actT_high", "y_low0", "y_low1"),
        "dve": ("G", "xs", "gate", "up", "q", "act", "actT", "nat")}


def rest_at(it, name):
    steps = next(v for v in REST.values() if name in v)
    return len(steps) * it + steps.index(name)


OUT_STORES = [3, 5]
SEMS = """consts x_loaded norm_ss norm_rs norm_h hT_ps hT gain_loaded router_w
logit_ps logits gate_e gates rank_ps ranks flagT_ps flag
wupa0 wupa1 wupb0 wupb1 wdn0 wdn1 m_wh m_wl m_used m_G m_xg_ps m_xh m_xs m_glo m_ulo m_g m_u m_tanh m_q m_act m_actT_ps m_ah
m_actT m_ylo m_nat h_parts m_ywr0 m_ywr1
rgath0 rgath1 rcomb0 rcomb1 rw0 r_pe0 r_act0 r_dve0 rywa0 rywb0
rw1 r_pe1 r_act1 r_dve1 rywa1 rywb1
gathered combined y_done stored out_stored
vec_in vecT_ps vecT masks lora_in chunk_in0 chunk_in1 chunk_in2 pj_ps pj_out shift_stored
mm_in mm_ss mm_rs mm_h mm_T_ps mm_T kv_stored
kT_ps kT sc_ps sc_max sc_exp sc_prob pT_ps pT at_ps at_out
cache_k cache_v qn_ps qn qb_ps s_score sT_ps s_max s_exp s_prob spT_ps spT sat_ps sat_out
shift_in shiftT_ps shiftT xj lora_e lora_s t_dve t_act sum_ps c_ps c_dve c_act c_pool
dec_scr0 dec_scr1 dec_in dec_mul dec_sum dec_y x_out act_chain dve_chain pool_chain""".split()


def build(nc, A, O, dbg=None):
    with ExitStack() as ctx:
        s = {n: ctx.enter_context(nc.semaphore(n)) for n in SEMS}

        def sb(name, cols, dt=F32, rows=128):
            return ctx.enter_context(nc.sbuf_tensor(name, [rows, cols], dt))

        WIDTHS = {"slot0": SLOT, "slot1": SLOT, "h": 3 * D, "hT": KT * T, "gain": D, "mixedT": (KT + 2) * T, "arena": 13600}
        with ExitStack() as names:
            split = {n: names.enter_context(nc.sbuf_tensor(f"{n}_split", [128, w], F32R)) for n, w in WIDTHS.items()}
        over = {n: sb(n, w) for n, w in WIDTHS.items()}
        slot = [over["slot0"], over["slot1"]]
        wup = [t[:, 0:8192].rearrange("p (k n) -> p k n", k=KT) for t in slot]
        wdn = [t[:, 8192:12288].rearrange("p (k n) -> p k n", k=FF // 128) for t in slot]
        x = sb("x", 3 * D)[:, :].rearrange("p (t d) -> p t d", t=3)
        h = over["h"][:, :].rearrange("p (t d) -> p t d", t=3)
        hT = over["hT"][:, :].rearrange("p (k t) -> p k t", k=KT)
        gain = over["gain"]
        ident = sb("ident", 128)
        before = sb("before", 128)
        ones = sb("ones", 128)
        iota_rank = sb("iota_rank", CAP + RROWS)
        iota_e = sb("iota_e", NE)
        iota_g = sb("iota_g", NE)
        valid = sb("valid", 3)
        cst = sb("cst", 8)
        vecT = sb("vecT", 90)
        mlow = sb("mlow", 128)
        mup = sb("mup", 128)
        moff1 = sb("moff1", 128)
        moff2 = sb("moff2", 128)
        upto = sb("upto", 128)
        block64 = sb("block64", 128)
        sel = sb("sel", TS * 128, rows=TS)[:, :].rearrange("k (b n) -> k b n", b=TS)
        mixedT = over["mixedT"][:, :].rearrange("p (k t) -> p k t", t=T)
        nvec = sb("nvec", 12)
        arena = over["arena"]
        pos = [0]

        def carve_split(n):
            a = split["arena"][:, pos[0]:pos[0] + n]
            pos[0] += n
            return a

        def carve(n):
            a = arena[:, pos[0]:pos[0] + n]
            pos[0] += n
            return a

        sq = carve(D)
        st = carve(16)
        mm_st = arena[:, 1024 + 8:1024 + 16]
        wr = carve(KT * 36).rearrange("p (k n) -> p k n", k=KT)
        br = carve(36)
        lg = carve(3 * 36).rearrange("p (t n) -> p t n", t=3)
        g8 = carve(3 * 8).rearrange("p (t n) -> p t n", t=3)
        m8 = carve(3 * 8).rearrange("p (t n) -> p t n", t=3)
        i8 = carve(3 * 8).rearrange("p (t n) -> p t n", t=3)
        i8f = carve(3 * 8).rearrange("p (t n) -> p t n", t=3)
        em = carve(3 * NE).rearrange("p (t n) -> p t n", t=3)
        tmp32 = carve(3 * NE).rearrange("p (t n) -> p t n", t=3)
        a1 = carve(3 * NE).rearrange("p (t n) -> p t n", t=3)
        a2 = carve(3 * NE).rearrange("p (t n) -> p t n", t=3)
        asum = carve(3 * NE).rearrange("p (t n) -> p t n", t=3)
        rank = carve(3 * NE).rearrange("p (t n) -> p t n", t=3)
        R = carve(3 * (NE + 2)).rearrange("p (t n) -> p t n", t=3)
        gt = carve(3 * 8).rearrange("p (t n) -> p t n", t=3)
        rowf = carve(6)
        rowi = carve(6)
        flagf = carve(4)
        bf = lambda n: carve(n // 2).bitcast(BF16)
        hp = [bf(3 * D).rearrange("p (t d) -> p t d", t=3) for _ in range(3)]
        G = [bf(3 * CAP).rearrange("p (t n) -> p t n", t=3) for _ in range(2)]
        xs = [carve_split(KT * 2 * CAP).rearrange("p (k v n) -> p k v n", k=KT, v=2) for _ in range(2)]
        actT = carve_split(4 * 2 * CAP).rearrange("p (f v n) -> p f v n", f=4, v=2)
        gate, ex = sq[:, 0:FF], sq[:, FF:D]
        upp = carve(FF)
        an = carve(FF)
        ynat = [carve(D) for _ in range(2)]
        ring = [split["h"][:, D * n:D * (n + 1)] for n in range(3)] + [split["hT"][:, D * n:D * (n + 1)] for n in range(2)] \
            + [split["mixedT"][:, D * n:D * (n + 1)] for n in range(2)] + [split["gain"][:, :]]
        assert UNITS * 2 % RING == 0 and len(ring) == RING
        yg = h
        rows_i = sb("rows_i", 6, I32)
        rows_r = sb("rows_r", 6, I32)
        in_rest = sb("in_rest", 6)
        gr = sb("gr", 6)
        flag_i = sb("flag_i", 2, I32)
        idx_u = sb("idx_u", 3 * 8, U32)[:, :].rearrange("p (t n) -> p t n", t=3)
        ps = [ctx.enter_context(nc.psum_tensor(f"bank{i}", [128, 512], F32)) for i in range(8)]
        wch = [slot[0][:, 4096 * n:4096 * (n + 1)] for n in range(3)]

        class Area:
            def __init__(self, ap, at=0):
                self.ap, self.at = ap, at

            def take(self, n):
                self.at += n
                return self.ap[:, self.at - n:self.at]
        k3 = lambda a, k: a.rearrange("p (k t) -> p k t", k=k)
        AR = 1040
        vraw = arena[:, AR:AR + 128]
        a_ = Area(arena, AR + 128)
        mem = k3(a_.take(2 * D), 2)
        gmem = a_.take(D)
        memT = k3(a_.take(KT * N_MEM), KT)
        kvn = k3(a_.take(2 * 2 * MEMW), 2)
        kT = k3(a_.take(2 * N_MEM), 2)
        qT = k3(a_.take(2 * T), 2)
        qs = a_.take(MEMW)
        smx = a_.take(8)
        snx = a_.take(8)
        ssm = a_.take(8)
        srs = a_.take(8)
        sc_s = a_.take(64)
        sp_s = a_.take(N_MEM)
        spT = a_.take(64)
        attention_end = a_.at
        b_ = Area(slot[1])
        KC = b_.take(4096).rearrange("p (m b n) -> p m b n", m=2, b=TS)
        VC = b_.take(4096).rearrange("p (m b n) -> p m b n", m=2, b=TS)
        P = b_.take(8 * N_MEM).rearrange("p (h t m) -> p h t m", h=4, t=2)
        PT = b_.take(4 * 2 * TP).rearrange("p (h m t) -> p h m t", h=4, m=2)
        a_ = Area(arena, AR + 128)
        Q = [k3(a_.take(PAIRS * T), PAIRS) for _ in range(5)]
        lw1, la1, lg1 = k3(a_.take(512), KT), k3(a_.take(512), KT), k3(a_.take(1024), KT)
        lw2, la2, lg2 = a_.take(TOK), a_.take(TOK), a_.take(TOK)
        lora_at = a_.at - (512 + 512 + 1024 + 3 * TOK)
        w1o, a1o, g1o = mixedT[:, 0, :], mixedT[:, 1, :], mixedT[:, 2, :]
        assert a_.at <= 13600, a_.at
        b_ = Area(slot[1])
        Q += [k3(b_.take(PAIRS * T), PAIRS) for _ in range(3)]
        t_at = b_.at
        TT = [k3(b_.take(KT * T), KT) for _ in range(3)]
        shn = b_.take(D)
        vr, vk, vv, vb, vkk, vL, vg, vld = Q
        b_ = Area(slot[1], t_at)
        c_ = Area(arena, lora_at)
        h_ = Area(h.rearrange("p t d -> p (t d)"))
        t_ = Area(hT.rearrange("p k t -> p (k t)"))
        mats = [k3(b_.take(768), PAIRS) for _ in range(9)] + [k3(c_.take(768), PAIRS) for _ in range(5)] \
            + [k3(h_.take(768), PAIRS) for _ in range(4)] + [k3(t_.take(768), PAIRS) for _ in range(2)] + [k3(gain[:, 0:768], PAIRS)]
        cAT, cBT, cKT, cRT, cN, cN1, cN2, cNT, cX2, cX2T, cX4, cX4T, cUa, cUb, cUTa, cUTb, cQT, cBn, cKn, cVn, cZ = mats
        lam = sb("lam", PAIRS * NCH)[:, :].rearrange("p (q c) -> p q c", c=NCH)
        DS = arena[0:96, lora_at:lora_at + 4096].rearrange("p (i j) -> p i j", i=64)
        Dt = slot[1][0:96, t_at:t_at + 4096].rearrange("p (i j) -> p i j", i=64)
        Dv = slot[1][0:96, t_at + 4096:t_at + 4096 + 6 * 64].rearrange("p (v j) -> p v j", v=6)
        Dsa = slot[1][0:96, t_at + 4500:t_at + 4564]
        Dy = slot[1][0:96, t_at + 4564:t_at + 4628]
        Dn = [mixedT.rearrange("p k t -> p (k t)")[0:TS, TOK * n:TOK * (n + 1)] for n in range(2)]
        dscr = nc.dram_tensor("sample_vectors", [6, TS * TOK], F32, kind="Internal").ap()
        yscr = nc.dram_tensor("sample_y", [TS * TOK], F32, kind="Internal").ap()
        a_ = Area(arena, AR + 128)
        b_ = Area(slot[1])
        gq, gk = k3(a_.take(4 * T), 4), k3(a_.take(4 * T), 4)
        gv, grt = k3(a_.take(8 * T), 8), k3(a_.take(8 * T), 8)
        gl, ge = k3(a_.take(4 * T), 4), k3(a_.take(4 * T), 4)
        gkh, gq2 = k3(a_.take(4 * T), 4), a_.take(0)
        ga1, ga2, ga1o = k3(a_.take(128), KT), a_.take(384), a_.take(T)
        assert a_.at <= 13600, a_.at
        gS = b_.take(TS * TOK).rearrange("p (b h e) -> p b h e", b=TS, h=4)
        go = k3(b_.take(8 * T), 8)
        gZ = k3(b_.take(TOK), 4)
        gZm = k3(b_.take(TOK), 4)
        gvn = b_.take(TOK)
        gkn = b_.take(384)
        gatt = k3(b_.take(4 * C), 4)
        gem = b_.take(4 * NCH)
        gee = b_.take(4 * NCH)
        gvs = b_.take(TOK)
        assert b_.at <= 12288, b_.at
        wo_tiles = [[(k, 128 * k, 128) for k in range(KT)],
                    [(k, 96 * k, 96) for k in range(8)] + [(8 + k, TOK + 128 * k, 128) for k in range(2)]]

        rows_first = [nc.dram_tensor(f"rows_first{l}", [NE * CAP, D], F32, kind="Internal").ap() for l in range(DEPTH)]
        rows_rest = [nc.dram_tensor(f"rows_rest{l}", [NE * RROWS, D], F32, kind="Internal").ap() for l in range(DEPTH)]

        def unit_of(j, u):
            return wup[j][:, u, :] if u < UNITS_UP else wdn[j][:, u - UNITS_UP, :]

        def low_of(j, u):
            return split[f"slot{j}"][:, D * u:D * (u + 1)]

        block = ctx.enter_context(nc.Block())

        def chain(eng, sem):
            n = [0]

            def link(ins):
                n[0] += 1
                ins.then_inc(sem, 1)
                eng.wait_ge(sem, n[0])
            return link

        def load_up(sp, e, sl, l, sa, sb_):
            for u, sem in enumerate((sa, sb_)):
                rows = slice(u * D // 2, (u + 1) * D // 2)
                sp.dma_start(wup[sl][:, u * KT // 2:(u + 1) * KT // 2, :],
                             A["exp_w_up"][l, bass.ds(e, 1), rows].rearrange("e (k p) n -> p (e k) n", p=128)).then_inc(sem, 16)

        def load_down(sp, e, sl, l, sem):
            sp.dma_start(wdn[sl], A["exp_w_down"][l, bass.ds(e, 1)].rearrange("e (k p) n -> p (e k) n", p=128)).then_inc(sem, 16)

        @block.sync
        def _(sp):
            sp.dma_start(x[:, 0:2, :], A["x_prompt"][0].rearrange("(t p) d -> p t d", p=128)).then_inc(s["x_loaded"], 16)
            sp.dma_start(x[0:TS, 2, :], A["x_sample"].rearrange("b q d -> (b q) d")).then_inc(s["x_loaded"], 16)
            sp.dma_start(vraw[0:48, :], A["rw_mu"][0].rearrange("j (k c) -> (j k) c", c=128)).then_inc(s["vec_in"], 16)
            for n, name in enumerate(("rw_w0", "rw_a0", "rw_k_k", "rw_k_a", "rw_r_k", "rw_ln_g", "rw_ln_b")):
                v = A[name][0].rearrange("(k c) -> k c", c=128) if name != "rw_r_k" else A[name][0].rearrange("(k u) c -> k (u c)", u=2)
                sp.dma_start(vraw[48 + 6 * n:54 + 6 * n, :], v).then_inc(s["vec_in"], 16)
            chunk = 0

            def load_chunk(dst, src):
                nonlocal chunk
                if chunk >= 3:
                    sp.wait_ge(s["pj_ps"], tiles_through(chunk - 3))
                for d, a in zip(dst(wch[chunk % 3]), src):
                    sp.dma_start(d, a).then_inc(s[f"chunk_in{chunk % 3}"], 16)
                chunk += 1

            for l in range(DEPTH):
                if l == 0:
                    sp.dma_start(gain[:, :], A["norm_mix_g"][0:1, :].broadcast_to([128, D])).then_inc(s["gain_loaded"], 16)
                else:
                    sp.wait_ge(s["m_used"], UNITS * NE)
                    sp.dma_start(gain[:, :], A["norm_mix_g"][1:2, :].broadcast_to([128, D])).then_inc(s["gain_loaded"], 16)
                    sp.wait_ge(s["combined"], 2)
                    sp.dma_start(vraw[0:4, 0:96], A["gla_ab"][0].rearrange("(k c) -> k c", c=96)).then_inc(s["vec_in"], 16)
                    sp.dma_start(vraw[4:6, 0:96], A["gla_norm_g"][0].rearrange("(k c) -> k c", c=96)).then_inc(s["vec_in"], 16)
                sp.dma_start(mem, A["mem_prompt"][0].rearrange("(m p) d -> p m d", p=128)).then_inc(s["mm_in"], 16)
                sp.dma_start(gmem, A["norm_mem_g"][l:l + 1, :].broadcast_to([128, D])).then_inc(s["mm_in"], 16)
                load_chunk(lambda b: [k3(b, KT)], [A["w_mem_kv"][l].rearrange("(k p) n -> p k n", p=128)])
                if l == 0:
                    sp.dma_start(lw1, A["rw_w1"][0].rearrange("(k p) n -> p k n", p=128)).then_inc(s["lora_in"], 16)
                    sp.dma_start(la1, A["rw_a1"][0].rearrange("(k p) n -> p k n", p=128)).then_inc(s["lora_in"], 16)
                    sp.dma_start(lg1, A["rw_g1"][0].rearrange("(k p) n -> p k n", p=128)).then_inc(s["lora_in"], 16)
                    sp.dma_start(lw2[0:64, :], A["rw_w2"][0]).then_inc(s["lora_in"], 16)
                    sp.dma_start(la2[0:64, :], A["rw_a2"][0]).then_inc(s["lora_in"], 16)
                    sp.dma_start(lg2, A["rw_g2"][0]).then_inc(s["lora_in"], 16)
                else:
                    sp.dma_start(ga1, A["gla_a1"][0].rearrange("(k p) n -> p k n", p=128)).then_inc(s["lora_in"], 16)
                    sp.dma_start(ga2[0:16, :], A["gla_a2"][0]).then_inc(s["lora_in"], 16)
                for m in range(2):
                    sp.dma_start(KC[:, m], A["cache_mem_k"][l].rearrange("b (m p) h d -> m p b (h d)", p=128)[m]).then_inc(s["cache_k"], 16)
                    sp.dma_start(VC[:, m], A["cache_mem_v"][l].rearrange("b (m p) h d -> m p b (h d)", p=128)[m]).then_inc(s["cache_v"], 16)
                for c0, w in W_IN[l]:
                    load_chunk(lambda b: [k3(b[:, 0:KT * w], KT)], [A["w_in"][l].rearrange("(k p) n -> p k n", p=128)[:, :, c0:c0 + w]])
                for c0, w in W_OUT[l]:
                    if l == 0:
                        load_chunk(lambda b: [k3(b[:, 0:KT * w], KT)], [A["w_out"][l].rearrange("(k p) n -> p k n", p=128)[:, :, c0:c0 + w]])
                    else:
                        load_chunk(lambda b: [k3(b[0:96, 0:8 * w], 8), k3(b[:, 8 * w:10 * w], 2)],
                                   [A["w_out"][l][0:TOK, c0:c0 + w].rearrange("(k p) n -> p k n", p=96),
                                    A["w_out"][l][TOK:D, c0:c0 + w].rearrange("(k p) n -> p k n", p=128)])
                sp.wait_ge(s["x_out"], l + 1)
                sp.wait_ge(s["out_stored"], 16 * OUT_STORES[l])
                sp.dma_start(wr[:, :, 0:4], A["router_wg"][l].rearrange("(k p) n -> p k n", p=128)).then_inc(s["router_w"], 16)
                sp.dma_start(wr[:, :, 4:36], A["router_we"][l].rearrange("(k p) n -> p k n", p=128)).then_inc(s["router_w"], 16)
                sp.dma_start(br[:, 0:4], A["router_bg"][l:l + 1, :].broadcast_to([128, 4])).then_inc(s["router_w"], 16)
                sp.dma_start(br[:, 4:36], A["router_be"][l:l + 1, :].broadcast_to([128, 32])).then_inc(s["router_w"], 16)
                sp.dma_start(gain[:, :], A["norm_ffn_g"][l:l + 1, :].broadcast_to([128, D])).then_inc(s["gain_loaded"], 16)
                for j in range(2):
                    load_up(sp, j, j, l, s[f"wupa{j}"], s[f"wupb{j}"])
                    load_down(sp, j, j, l, s[f"wdn{j}"])
                with sp.Fori(1, NE // 2) as i:
                    for j in range(2):
                        sp.wait_ge(s["m_used"], UNITS * (NE * l + 2 * i + j - 2) + UNITS_UP)
                        load_up(sp, 2 * i + j, j, l, s[f"wupa{j}"], s[f"wupb{j}"])
                        sp.wait_ge(s["m_used"], UNITS * (NE * l + 2 * i + j - 1))
                        load_down(sp, 2 * i + j, j, l, s[f"wdn{j}"])
                sp.wait_ge(s["flag"], l + 1)
                more = sp.value_load(flag_i[0:1, 0:1], min_val=0, max_val=1)
                with sp.If(more > 0):
                    sp.wait_ge(s["m_used"], UNITS * NE * (l + 1))
                    load_up(sp, 0, 0, l, s[f"rw{l}"], s[f"rw{l}"])
                    load_down(sp, 0, 0, l, s[f"rw{l}"])
                    with sp.Fori(1, NE) as e:
                        sp.wait_ge(s[f"r_pe{l}"], len(REST["pe"]) * STEPS_REST * e)
                        load_up(sp, e, 0, l, s[f"rw{l}"], s[f"rw{l}"])
                        load_down(sp, e, 0, l, s[f"rw{l}"])
                with sp.Else():
                    sp.nop()
            sp.wait_ge(s["m_used"], 2 * UNITS * NE)
            sp.dma_start(gain[:, :], A["norm_final_g"].rearrange("(a d) -> a d", a=1).broadcast_to([128, D])).then_inc(s["gain_loaded"], 16)
            sp.wait_ge(s["norm_h"], 15)
            sp.dma_start(O["y_prompt"][0].rearrange("(t p) d -> p t d", p=128), h[:, 0:2, :]).then_inc(s["stored"], 16)
            sp.dma_start(O["y_sample"].rearrange("b q d -> (b q) d"), h[0:TS, 2, :]).then_inc(s["stored"], 16)
            sp.wait_ge(s["stored"], 32)
            sp.wait_ge(s["kv_stored"], 64)
            sp.wait_ge(s["shift_stored"], 32)

        @block.gpsimd
        def _(pool):
            link = chain(pool, s["pool_chain"])
            link(pool.memset(ident[:, :], 0.0))
            link(pool.affine_select(out=ident[:, :], in_=ident[:, :], compare_op=ALU.not_equal, fill=1.0, base=0,
                                    pattern=[[-1, 128]], channel_multiplier=1))
            pool.memset(ones[:, :], 1.0)
            link(pool.memset(before[:, :], 1.0))
            link(pool.affine_select(out=before[:, :], in_=before[:, :], compare_op=ALU.is_gt, fill=0.0, base=0,
                                    pattern=[[1, 128]], channel_multiplier=-1))
            pool.iota(iota_rank[:, :], pattern=[[1, CAP + RROWS]], base=0, channel_multiplier=0, allow_small_or_imprecise_dtypes=True)
            pool.iota(iota_e[:, :], pattern=[[1, NE]], base=0, channel_multiplier=0, allow_small_or_imprecise_dtypes=True)
            pool.iota(iota_g[:, :], pattern=[[1, GROUPS], [0, NE // GROUPS]], base=0, channel_multiplier=0, allow_small_or_imprecise_dtypes=True)
            pool.memset(cst[:, 0:1], EPS)
            link(pool.memset(valid[:, :], 1.0))
            link(pool.affine_select(out=valid[:, 2:3], in_=valid[:, 2:3], compare_op=ALU.is_gt, fill=0.0, base=TS,
                                    pattern=[[0, 1]], channel_multiplier=-1))
            link(pool.memset(upto[:, :], 1.0))
            link(pool.affine_select(out=upto[:, :], in_=upto[:, :], compare_op=ALU.is_ge, fill=0.0, base=0,
                                    pattern=[[1, 128]], channel_multiplier=-1))
            pool.iota(mlow[:, :], pattern=[[1, 8], [0, 16]], base=0, channel_multiplier=0, allow_small_or_imprecise_dtypes=True)
            pool.iota(moff1[:, :], pattern=[[1, 4], [0, 32]], base=0, channel_multiplier=0, allow_small_or_imprecise_dtypes=True)
            pool.iota(moff2[:, :], pattern=[[1, 2], [0, 64]], base=0, channel_multiplier=0, allow_small_or_imprecise_dtypes=True)
            for b in range(TS):
                link(pool.tensor_copy(sel[:, b, :], ident[0:TS, b:b + 1].broadcast_to([TS, 128])))
            pool.memset(cst[:, 2:3], GN_EPS)
            pool.memset(cst[:, 3:4], 16 * LN2)
            pool.memset(cst[:, 1:2], 0.0).then_inc(s["consts"], 1)

            pool.wait_ge(s["consts"], 1)

            def mixer0():
                pool.wait_ge(s["norm_h"], 3)
                pool.dma_start(O["prompt_rwkv_shift"][0], h[127:128, 1, :]).then_inc(s["shift_stored"], 16)
                pool.dma_start(O["sample_rwkv_shift"][0], h[0:TS, 2, :]).then_inc(s["shift_stored"], 16)
                store_kv(0)
                pool.wait_ge(s["at_ps"], 1)
                pool.dma_start(shn[0:TS, :], A["state_rwkv_shift"][0]).then_inc(s["shift_in"], 16)
                for n in range(6):
                    pool.wait_ge(s["qn"], n + 2)
                    pool.dma_start(dscr[n].rearrange("(b c) -> b c", b=TS), Dn[n % 2]).then_inc(s[f"dec_scr{n % 2}"], 16)
                pool.wait_ge(s["t_dve"], T_SCALED)
                pool.wait_ge(s["shift_stored"], 32)
                for m in mats:
                    pool.memset(m, 0.0)
                link(pool.memset(cst[:, 4:5], 0.0))
                for c in range(NCH):
                    for i, (dst, src) in enumerate(((cAT, vkk), (cBT, vb), (cKT, vk), (cRT, vr), (cX4, vv))):
                        if c > 0 and i == 0:
                            pool.wait_ge(s["c_ps"], c_ps_at(c - 1, "Z", 1))
                            pool.wait_ge(s["c_dve"], c_at(c - 1, "Z", 1))
                        for u in range(2):
                            rows = slice(64 * u, 64 * u + 64)
                            last = pool.tensor_copy(dst[rows, :, 64 * u:64 * u + 64], src[rows, :, C * c:C * (c + 1)])
                    last.then_inc(s["c_pool"], 1)
                pool.wait_ge(s["t_act"], T_STATE_OUT)
                for u in range(2):
                    pool.dma_start(O["prompt_rwkv_S"][0, 0].rearrange("(q u) i j -> u i q j", u=2)[u], cX2[64 * u:64 * u + 64, :, 64 * u:64 * u + 64]).then_inc(s["out_stored"], 16)
                for n in range(2):
                    pool.wait_ge(s[f"dec_scr{n}"], 48)
                pool.dma_start(DS.rearrange("p i j -> p (i j)"), A["state_rwkv_S"][0].rearrange("b h i j -> (b h) (i j)")).then_inc(s["dec_in"], 16)
                pool.dma_start(Dv, dscr.rearrange("v (p j) -> p v j", j=64)).then_inc(s["dec_in"], 16)
                pool.wait_ge(s["dec_sum"], 1)
                pool.dma_start(O["sample_rwkv_S"][0].rearrange("b h i j -> (b h) (i j)"), DS.rearrange("p i j -> p (i j)")).then_inc(s["out_stored"], 16)
                pool.wait_ge(s["dec_sum"], 2)
                pool.dma_start(yscr.rearrange("(p i) -> p i", i=64), Dy).then_inc(s["dec_y"], 16)
                pool.wait_ge(s["dec_y"], 16)
                pool.dma_start(Dn[0], yscr.rearrange("(b c) -> b c", b=TS)).then_inc(s["dec_y"], 16)

            def mixer1():
                pool.wait_ge(s["combined"], 2)
                pool.wait_ge(s["sat_out"], 2)
                pool.dma_start(gS[0:96, :, :, :].rearrange("p b h e -> p (b h) e"), A["state_gla_S"][0].rearrange("b h d e -> d (b h) e")).then_inc(s["dec_in"], 16)
                store_kv(1)
                pool.wait_ge(s["dec_sum"], 3)
                pool.dma_start(O["sample_gla_S"][0].rearrange("b h d e -> d (b h) e"), gS[0:96, :, :, :].rearrange("p b h e -> p (b h) e")).then_inc(s["out_stored"], 16)
                pool.wait_ge(s["c_dve"], C_TOTAL + 2 * NCH)
                pool.dma_start(O["prompt_gla_S"][0, 0].rearrange("h d e -> d h e"), gZ[0:96]).then_inc(s["out_stored"], 16)

            def store_kv(l):
                pool.wait_ge(s["pj_out"], 2 + (tiles_through(CHUNKS[0] - 1) if l else 0))
                pool.dma_start(O["prompt_mem_k"][l, 0].rearrange("(m p) h d -> p m (h d)", p=128), kvn[:, :, 0:MEMW]).then_inc(s["kv_stored"], 16)
                pool.dma_start(O["prompt_mem_v"][l, 0].rearrange("(m p) h d -> p m (h d)", p=128), kvn[:, :, MEMW:2 * MEMW]).then_inc(s["kv_stored"], 16)

            def write_rows(dst, row, n, par, s_nat, s_wr):
                pool.wait_ge(s_nat, n + 1)
                pool.dma_start(dst[bass.ds(row, CAP), :], ynat[par][0:CAP, :]).then_inc(s_wr, 16)

            def gather_rows(src, index, k, s_done):
                for t, (_, n) in enumerate(TILES):
                    pool.indirect_dma_start(yg[0:n, t, :], None, src, bass.IndirectOffsetOnAxis(ap=index[0:n, 2 * t + k:2 * t + k + 1], axis=0)).then_inc(s_done, 16)

            for l in range(DEPTH):
                (mixer0, mixer1)[l]()
                with pool.Fori(0, NE // 2) as i:
                    for j in range(2):
                        write_rows(rows_first[l], (2 * i + j) * CAP, NE * l + 2 * i + j, j, s["m_nat"], s[f"m_ywr{j}"])
                pool.wait_ge(s["flag"], l + 1)
                more = pool.value_load(flag_i[0:1, 0:1], min_val=0, max_val=1)
                with pool.If(more > 0):
                    with pool.Fori(0, NE) as e:
                        for b in range(STEPS_REST):
                            write_rows(rows_rest[l], e * RROWS + CAP * b, rest_at(STEPS_REST * e + b, "nat"), b % 2, s[f"r_dve{l}"], s[f"ryw{'ab'[b % 2]}{l}"])
                    pool.wait_ge(s[f"rywa{l}"], 8 * STEPS_REST * NE)
                    pool.wait_ge(s[f"rywb{l}"], 8 * STEPS_REST * NE)
                    for k in range(2):
                        if k == 1 or l == 1:
                            pool.wait_ge(s["combined"], 2 * l)
                            pool.wait_ge(s[f"rcomb{l}"], k)
                        gather_rows(rows_rest[l], rows_r, k, s[f"rgath{l}"])
                    pool.wait_ge(s[f"rcomb{l}"], 2)
                with pool.Else():
                    pool.nop()
                for j in range(2):
                    pool.wait_ge(s[f"m_ywr{j}"], 8 * NE * (l + 1))
                for k in range(2):
                    if k == 1:
                        pool.wait_ge(s["combined"], 2 * l + 1)
                    elif l == 1:
                        pool.wait_ge(s["combined"], 2)
                    gather_rows(rows_first[l], rows_i, k, s["gathered"])

        NEEDS = {"X2": ("NT",), "X2T": ("NT",), "U1": ("X2T", "NT"), "UT1": ("X2T", "NT"), "X4": ("X2T",), "X4T": ("X2T",),
                 "U2": ("X4T", "UT1"), "UT2": ("X4T", "UT1"), "X8T": ("X4T",), "U3": ("X8T", "UT2"), "UT3": ("X8T", "UT2"),
                 "W1": ("U3",), "U4": ("W1", "UT3"), "UT4": ("W1", "UT3"), "W2": ("U4",), "U5": ("W2", "UT4"),
                 "RHS": ("Vn", "MT"), "SA": ("RHS", "U5"), "Y": ("SA", "QT"), "Z": ("SA",)}

        @block.tensor
        def _(pe):
            def transpose_h(n):
                pe.wait_ge(s["norm_h"], 3 * n)
                pe.wait_ge(s["pj_out"], tn[0])
                for k in range(KT):
                    if 8 * (n - 1) + k >= 2:
                        pe.wait_ge(s["hT"], 8 * (n - 1) + k - 1)
                    for t, (c, m) in enumerate(TILES):
                        last = pe.transpose(ps[k % 2][:, c:c + m], h[0:m, t, k * 128:(k + 1) * 128], ident[0:m, 0:m])
                    last.then_inc(s["hT_ps"], 1)

            tn = [0]

            def bank():
                if tn[0] >= 2:
                    pe.wait_ge(s["pj_out"], tn[0] - 1)
                return ps[tn[0] % 2]

            def tile_done(last):
                tn[0] += 1
                last.then_inc(s["pj_ps"], 1)

            wc = [0]

            def chunk_in(n_dmas=1):
                g = wc[0]
                wc[0] += 1
                b = g % 3
                got[b] += 16 * n_dmas
                pe.wait_ge(s[f"chunk_in{b}"], got[b])
                return wch[b]
            got = [0, 0, 0]

            def product(w, m, rhs, kt=KT, rows=128, n=T):
                p = bank()
                for k in range(kt):
                    last = pe.matmul(p[0:m, 0:n], w(k), rhs(k), start=(k == 0), stop=(k == kt - 1))
                tile_done(last)

            def attention(l):
                for k in range(KT):
                    pe.wait_ge(s["mm_h"], 2 * (l + 1))
                    if k >= 2:
                        pe.wait_ge(s["mm_T"], KT * l + k - 1)
                    for m in range(2):
                        last = pe.transpose(ps[2 + k % 2][:, 128 * m:128 * (m + 1)], mem[:, m, k * 128:(k + 1) * 128], ident[:, :])
                    last.then_inc(s["mm_T_ps"], 1)
                pe.wait_ge(s["mm_T"], KT * (l + 1))
                w = k3(chunk_in(), KT)
                for m in range(2):
                    product(lambda k: memT[:, k, 128 * m:128 * (m + 1)], 128, lambda k: w[:, k, :], n=2 * MEMW)
                pe.wait_ge(s["pj_out"], tn[0])
                for hp in range(2):
                    for m in range(2):
                        last = pe.transpose(ps[2][:, 256 * hp + 128 * m:256 * hp + 128 * (m + 1)], kvn[:, m, 128 * hp:128 * (hp + 1)], ident[:, :])
                last.then_inc(s["kT_ps"], 1)
                transpose_h(2 * l + 1)
                pe.wait_ge(s["hT"], KT * (2 * l + 1))
                w = k3(chunk_in()[:, 0:KT * 256], KT)
                for q in range(2):
                    product(lambda k: w[:, k, 128 * q:128 * (q + 1)], 128, lambda k: hT[:, k, :])
                pe.wait_ge(s["pj_out"], tn[0])
                pe.wait_ge(s["kT"], l + 1)
                pe.wait_ge(s["vecT"], l + 1)
                for hd in range(4):
                    rows = slice(64 * (hd % 2), 64 * (hd % 2) + 64)
                    for t in range(2):
                        last = pe.matmul(ps[4 + hd][:, 256 * t:256 * (t + 1)], qT[rows, hd // 2, 128 * t:128 * (t + 1)], kT[rows, hd // 2, :],
                                         start=True, stop=True)
                    last.then_inc(s["sc_ps"], 1)
                for q in range(2):
                    last = pe.transpose(ps[3][0:TS, 128 * q:128 * (q + 1)], qT[:, q, TP:T], ident[:, :])
                last.then_inc(s["qn_ps"], 1)
                for hd in range(4):
                    pe.wait_ge(s["sc_prob"], 4 * l + hd + 1)
                    for m in range(2):
                        for t in range(2):
                            last = pe.transpose(ps[4 + hd][:, 256 * m + 128 * t:256 * m + 128 * (t + 1)], P[:, hd, t, 128 * m:128 * (m + 1)], ident[:, :])
                    last.then_inc(s["pT_ps"], 1)
                for hd in range(4):
                    pe.wait_ge(s["pT"], 4 * l + hd + 1)
                    rows = slice(64 * (hd % 2), 64 * (hd % 2) + 64)
                    for m in range(2):
                        last = pe.matmul(ps[2][rows, 256 * (hd // 2):256 * (hd // 2 + 1)], kvn[:, m, MEMW + 64 * hd:MEMW + 64 * (hd + 1)], PT[:, hd, m, :],
                                         start=(m == 0), stop=(m == 1))
                last.then_inc(s["at_ps"], 1)
                pe.wait_ge(s["qn"], l * 7 + 1)
                for b in range(TS):
                    last = pe.matmul(ps[4 + b // 2][:, 256 * (b % 2):256 * (b % 2 + 1)], sel[:, b, :], qs[0:TS, :], start=True, stop=True)
                last.then_inc(s["qb_ps"], 1)
                pe.wait_ge(s["s_score"], l + 1)
                for m in range(2):
                    last = pe.transpose(ps[3][0:32, 128 * m:128 * (m + 1)], sc_s[:, 32 * m:32 * (m + 1)], ident[:, :])
                last.then_inc(s["sT_ps"], 1)
                pe.wait_ge(s["s_prob"], l + 1)
                for m in range(2):
                    last = pe.transpose(ps[3][:, 32 * m:32 * (m + 1)], sp_s[0:32, 128 * m:128 * (m + 1)], ident[0:32, 0:32])
                last.then_inc(s["spT_ps"], 1)
                pe.wait_ge(s["spT"], l + 1)
                pe.wait_ge(s["cache_v"], 32 * (l + 1))
                pe.wait_ge(s["at_out"], l + 1)
                for hp in range(2):
                    for b in range(TS):
                        for m in range(2):
                            last = pe.matmul(ps[2][:, 32 * hp + 4 * b:32 * hp + 4 * b + 4], VC[:, m, b, 128 * hp:128 * (hp + 1)],
                                             spT[:, 32 * m + 4 * b:32 * m + 4 * b + 4], start=(m == 0), stop=(m == 1))
                last.then_inc(s["sat_ps"], 1)

            def output(l):
                for c0, w in W_OUT[l]:
                    buf = chunk_in(1 + l)
                    for t, (c, m) in enumerate(TILES):
                        p = bank()
                        for n, (i, _, rows) in enumerate(wo_tiles[l]):
                            if l == 0:
                                wk = buf[0:rows, w * i:w * (i + 1)]
                            else:
                                wk = buf[0:rows, w * i:w * (i + 1)]
                            last = pe.matmul(p[0:m, 0:w], mixedT[0:rows, i, c:c + m], wk, start=(n == 0), stop=(n == len(wo_tiles[l]) - 1))
                        tile_done(last)

            def head_sums(src, n):
                for q in range(PAIRS):
                    last = pe.matmul(ps[2 + q][:, 0:T], block64[:, :], src[:, q, :], start=True, stop=True)
                last.then_inc(s["sum_ps"], 1)

            def mixer0():
                pe.wait_ge(s["shift_in"], 16)
                pe.wait_ge(s["sat_out"], 1)
                for k in range(KT):
                    last = pe.transpose(ps[7][:, TS * k:TS * (k + 1)], shn[0:TS, 128 * k:128 * (k + 1)], ident[0:TS, 0:TS])
                last.then_inc(s["shiftT_ps"], 1)
                n = 0
                for _, w in W_IN[0][1:]:
                    buf = k3(chunk_in()[:, 0:KT * w], KT)
                    for i in range(w // 128):
                        xi = n // PAIRS
                        pe.wait_ge(s["xj"], xi + 1)
                        product(lambda k: buf[:, k, 128 * i:128 * (i + 1)], 128, lambda k: TT[1 + xi % 2][:, k, :])
                        n += 1
                pe.wait_ge(s["lora_in"], 96)
                for xi, (w, m) in enumerate(((lw1, 64), (la1, 64), (lg1, 128))):
                    pe.wait_ge(s["xj"], xi + 4)
                    product(lambda k: w[:, k, :], m, lambda k: TT[1 + (xi + 3) % 2][:, k, :])
                base = tn[0]
                pe.wait_ge(s["lora_s"], 1)
                for q in range(PAIRS):
                    product(lambda k: lw2[0:64, 128 * q:128 * (q + 1)], 128, lambda k: w1o[0:64, :], kt=1)
                pe.wait_ge(s["pj_out"], base - 1)
                for q in range(PAIRS):
                    product(lambda k: la2[0:64, 128 * q:128 * (q + 1)], 128, lambda k: a1o[0:64, :], kt=1)
                pe.wait_ge(s["lora_s"], 2)
                for q in range(PAIRS):
                    product(lambda k: lg2[:, 128 * q:128 * (q + 1)], 128, lambda k: g1o, kt=1)
                pe.wait_ge(s["t_dve"], 1)
                head_sums(vL, 1)
                pe.wait_ge(s["t_dve"], 3)
                head_sums(TT[0], 2)
                pe.wait_ge(s["t_dve"], 5)
                for n, src in enumerate((vr, vk, vv, vkk, vb, TT[2])):
                    if n == 5:
                        pe.wait_ge(s["t_act"], 2)
                    if n >= 1:
                        pe.wait_ge(s["qn"], n + 1)
                    for q in range(PAIRS):
                        last = pe.transpose(ps[2 + q // 3][0:TS, 128 * (q % 3):128 * (q % 3 + 1)], src[:, q, TP:T], ident[:, :])
                    last.then_inc(s["qn_ps"], 1)

                def group(c, name, *mms, tr=False):
                    n = ORDER.index(name)
                    for hf in range(2):
                        for o in NEEDS.get(name, ()):
                            pe.wait_ge(s["c_" + dict(ROUNDS)[o]], c_at(c, o, hf))
                        g = len(ROUNDS) * c + n - 4
                        if g >= 0:
                            cc, nm = g // len(ROUNDS), ORDER[g % len(ROUNDS)]
                            pe.wait_ge(s["c_" + dict(ROUNDS)[nm]], c_at(cc, nm, hf))
                        b = ps[2 * (n % 4) + hf]
                        for q in range(3):
                            out = b[:, 128 * q:128 * (q + 1)]
                            for i, (lt, rh) in enumerate(mms):
                                if tr:
                                    last = pe.transpose(out, lt[:, 3 * hf + q, :], ident[:, :])
                                else:
                                    last = pe.matmul(out, lt[:, 3 * hf + q, :], rh[:, 3 * hf + q, :], start=(i == 0), stop=(i == len(mms) - 1))
                        last.then_inc(s["c_ps"], 1)

                assert len(ROUNDS) % 4 == 0
                for c in range(NCH):
                    pe.wait_ge(s["c_pool"], c + 1)
                    if c == 0:
                        pe.wait_ge(s["pj_out"], tn[0])
                        pe.wait_ge(s["qn"], 7)
                        pe.wait_ge(s["t_dve"], T_SCALED)
                    group(c, "N", (cAT, cBT))
                    group(c, "NT", (cBT, cAT))
                    group(c, "Bn", (cBT, None), tr=True)
                    group(c, "Kn", (cKT, None), tr=True)
                    group(c, "Vn", (cX4, None), tr=True)
                    group(c, "X2", (cN, cNT))
                    group(c, "X2T", (cNT, cN))
                    group(c, "MT", (cKT, cAT))
                    group(c, "U1", (cX2T, cUa))
                    group(c, "UT1", (cUa, cX2T))
                    group(c, "X4", (cX2T, cX2))
                    group(c, "X4T", (cX2, cX2T))
                    group(c, "PT", (cBT, cRT))
                    group(c, "U2", (cX4T, cUb))
                    group(c, "UT2", (cUb, cX4T))
                    group(c, "X8T", (cX4, cX4T))
                    group(c, "QT", (cKT, cRT))
                    group(c, "U3", (cX2T, cUa))
                    group(c, "UT3", (cUa, cX2T))
                    group(c, "W1", (cN1, cUb))
                    group(c, "U4", (cUTb, cX2))
                    group(c, "UT4", (cX2, cUTb))
                    group(c, "W2", (cN2, cUa))
                    group(c, "U5", (cUTa, cX4))
                    if c == 0:
                        pe.wait_ge(s["c_pool"], 1)
                    else:
                        for hf in range(2):
                            pe.wait_ge(s["c_dve"], c_at(c - 1, "Z", hf))
                    group(c, "RHS", (cAT, cZ), (cN, cVn))
                    group(c, "SA", (cUb, cX4T))
                    group(c, "Y", (cZ, cRT), (cX2T, cNT), (cVn, cQT))
                    group(c, "Z", (cBn, cX2T), (cKn, cVn))
                for hf in range(2):
                    pe.wait_ge(s["c_dve"], c_at(NCH - 1, "Z", hf))
                    pe.wait_ge(s["c_act"], c_at(NCH - 1, "Y", hf))
                for q in range(PAIRS):
                    last = pe.transpose(ps[2 + q // 3][:, 128 * (q % 3):128 * (q % 3 + 1)], cZ[:, q, :], ident[:, :])
                last.then_inc(s["qn_ps"], 1)
                pe.wait_ge(s["dec_y"], 32)
                for q in range(PAIRS):
                    last = pe.transpose(ps[4][:, TS * q:TS * (q + 1)], Dn[0][:, 128 * q:128 * (q + 1)], ident[0:TS, 0:TS])
                last.then_inc(s["qn_ps"], 1)
                pe.wait_ge(s["t_act"], T_STATE_OUT)
                pe.wait_ge(s["t_act"], 5)
                head_sums(vL, 3)
                pe.wait_ge(s["t_dve"], 8)
                head_sums(TT[1], 4)
                pe.wait_ge(s["t_dve"], 9)

            def mixer1():
                n = 0
                for _, w in W_IN[1][1:]:
                    buf = k3(chunk_in()[:, 0:KT * w], KT)
                    for i in range(w // 96):
                        product(lambda k: buf[:, k, 96 * i:96 * (i + 1)], 96, lambda k: hT[:, k, :])
                pe.wait_ge(s["lora_in"], 128)
                product(lambda k: ga1[:, k, :], 16, lambda k: hT[:, k, :])
                pe.wait_ge(s["pj_out"], tn[0])
                for i in range(4):
                    product(lambda k: ga2[0:16, 96 * i:96 * (i + 1)], 96, lambda k: ga1o[0:16, :], kt=1)
                pe.wait_ge(s["pj_out"], tn[0])
                for i in range(8):
                    last = pe.transpose(ps[2 + i // 4][0:TS, 96 * (i % 4):96 * (i % 4 + 1)], gv[0:96, i, TP:T], ident[0:96, 0:96])
                last.then_inc(s["qn_ps"], 1)
                pe.wait_ge(s["qn"], 9)
                for b in range(TS):
                    pe.wait_ge(s["dec_mul"], b + 1)
                    for u in range(2):
                        last = pe.matmul(ps[2 + 2 * (b % 2) + u][0:96, 0:384], sel[:, b, 0:96], gvs[0:TS, 384 * u:384 * (u + 1)], start=True, stop=True)
                    last.then_inc(s["qb_ps"], 1)
                pe.wait_ge(s["dec_sum"], 3)
                for b in range(TS):
                    for i in range(8):
                        last = pe.matmul(ps[6][0:96, TS * i + b:TS * i + b + 1], gS[0:96, b, i // 2, 96 * (i % 2):96 * (i % 2 + 1)],
                                         gq[0:96, i // 2, TP + b:TP + b + 1], start=True, stop=True)
                last.then_inc(s["sat_ps"], 1)
                pe.wait_ge(s["t_dve"], 14)
                for c in range(NCH):
                    cc = slice(C * c, C * (c + 1))
                    if c > 0:
                        pe.wait_ge(s["c_act"], C_ACT + 2 * c)
                    for i in range(8):
                        pe.transpose(ps[2 + i // 4][0:C, 96 * (i % 4):96 * (i % 4 + 1)], gv[0:96, i, cc], ident[0:96, 0:96])
                    for i in range(4):
                        last = pe.transpose(ps[4][0:C, 96 * i:96 * (i + 1)], gkh[0:96, i, cc], ident[0:96, 0:96])
                    last.then_inc(s["c_ps"], 1)
                    if c > 0:
                        pe.wait_ge(s["c_dve"], C_TOTAL + 2 * c)
                    for i in range(4):
                        last = pe.matmul(ps[5][0:C, C * i:C * (i + 1)], gk[0:96, i, cc], gq[0:96, i, cc], start=True, stop=True)
                    last.then_inc(s["c_ps"], 1)
                    pe.wait_ge(s["c_act"], C_ACT + 2 * c + 1)
                    pe.wait_ge(s["c_dve"], C_TOTAL + 2 * c + 1)
                    for i in range(8):
                        o = ps[6][0:96, C * i:C * (i + 1)]
                        pe.matmul(o, gvn[0:C, 96 * i:96 * (i + 1)], gatt[0:C, i // 2, :], start=True, stop=False)
                        last = pe.matmul(o, gZm[0:96, i // 2, 96 * (i % 2):96 * (i % 2 + 1)], gq[0:96, i // 2, cc], start=False, stop=True)
                    last.then_inc(s["c_ps"], 1)
                    for i in range(4):
                        last = pe.matmul(ps[7 if i < 2 else 5][0:96, 192 * (i % 2):192 * (i % 2 + 1)], gkn[0:C, 96 * i:96 * (i + 1)], gvn[0:C, 192 * i:192 * (i + 1)],
                                         start=True, stop=True)
                    last.then_inc(s["c_ps"], 1)
                pe.wait_ge(s["t_dve"], 15)
                for i in range(4):
                    for u in range(2):
                        last = pe.matmul(ps[2 + i][0:96, 0:T], ones[0:96, 0:96], gv[0:96, 2 * i + u, :], start=(u == 0), stop=(u == 1))
                last.then_inc(s["sum_ps"], 1)
                pe.wait_ge(s["t_dve"], 16)

            def gather(par, ks, s_done=None):
                for k in ks:
                    n = 0
                    for t, (_, m) in enumerate(TILES):
                        for part in hp:
                            last = pe.matmul(ps[par][:, k * CAP:(k + 1) * CAP], part[0:m, t, k * 128:(k + 1) * 128], G[par][0:m, t, :],
                                             start=(n == 0), stop=(n == 8))
                            n += 1
                if s_done is not None:
                    last.then_inc(s_done, 1)

            def unit(j, u, it):
                pe.wait_ge(s["m_wl"], UNITS * it + u + 1)
                if u < UNITS_UP:
                    lhs, bank0, first, last_ = xs[j][:, u], 2, u == 0, u == UNITS_UP - 1
                else:
                    f = u - UNITS_UP
                    lhs, bank0, first, last_ = actT[:, f], 6, f == 0, f == FF // 128 - 1
                lhs = lhs.rearrange("p v n -> p (v n)")
                for half in range(2):
                    cols = slice(half * FF, (half + 1) * FF)
                    pe.matmul(ps[bank0 + half][:, :], lhs, ring[(UNITS * j + u) % RING][:, cols], start=first, stop=False)
                    last = pe.matmul(ps[bank0 + half][:, :], lhs, low_of(j, u)[:, cols], start=False, stop=last_)
                last.then_inc(s["m_used"], 1)

            def act_T(s_done):
                for f in range(4):
                    last = pe.transpose(ps[5][:, f * 128:(f + 1) * 128], an[:, f * 128:(f + 1) * 128], ident[:, :])
                last.then_inc(s_done, 1)

            def whole(lhs, w, bank0, s_done):
                n = lhs.shape[1]
                for half in range(2):
                    for k in range(n):
                        last = pe.matmul(ps[bank0 + half][:, :], lhs[:, k].rearrange("p v n -> p (v n)").bitcast(F32), w[:, k, half * FF:(half + 1) * FF],
                                         start=(k == 0), stop=(k == n - 1))
                last.then_inc(s_done, 1)

            pe.wait_ge(s["consts"], 1)
            pe.wait_ge(s["vec_in"], 16 * 8)
            pe.transpose(ps[7][:, 0:90], vraw[0:90, :], ident[0:90, 0:90]).then_inc(s["vecT_ps"], 1)
            for n, m in enumerate((mlow, moff1, moff2)):
                last = pe.transpose(ps[6][:, 128 * n:128 * (n + 1)], m[:, :], ident[:, :])
            last.then_inc(s["vecT_ps"], 1)
            for l in range(DEPTH):
                if l == 1:
                    pe.wait_ge(s["vec_in"], 16 * 10)
                    pe.transpose(ps[7][0:96, 0:6], vraw[0:6, 0:96], ident[0:6, 0:6]).then_inc(s["vecT_ps"], 1)
                attention(l)
                (mixer0, mixer1)[l]()
                output(l)
                transpose_h(2 * l + 2)
                pe.wait_ge(s["hT"], 8 * (2 * l + 2))
                pe.wait_ge(s["router_w"], 64 * (l + 1))
                for t, (c, m) in enumerate(TILES):
                    for k in range(KT):
                        last = pe.matmul(ps[2][0:m, t * 36:(t + 1) * 36], hT[:, k, c:c + m], wr[:, k, :], start=(k == 0), stop=(k == KT - 1))
                last.then_inc(s["logit_ps"], 1)
                pe.wait_ge(s["gates"], l + 1)
                for t, (c, m) in enumerate(TILES):
                    for u in range(t + 1):
                        mu = TILES[u][1]
                        last = pe.matmul(ps[3][:, t * NE:(t + 1) * NE], (before if u == t else ones)[0:mu, :], asum[0:mu, u, :],
                                         start=(u == 0), stop=(u == t))
                last.then_inc(s["rank_ps"], 1)
                pe.wait_ge(s["ranks"], l + 1)
                pe.transpose(ps[3][0:1, 256:384], flagf[:, 0:1], ident[:, :]).then_inc(s["flagT_ps"], 1)

                base, gb = NE * l, (NE + 1) * l
                pe.wait_ge(s["h_parts"], l + 1)
                pe.wait_ge(s["m_G"], gb + 1)
                gather(0, range(KT), s["m_xg_ps"])

                def pair(i, first):
                    for j in range(2):
                        it, g = base + 2 * i + j, gb + 2 * i + j
                        start = first and j == 0 and l == 0
                        pe.wait_ge(s["m_xs"], g + 1)
                        if not start:
                            pe.wait_ge(s["m_u"], it)
                        for u in range(UNITS_UP):
                            unit(j, u, it)
                        pe.wait_ge(s["m_G"], g + 2)
                        if not start:
                            pe.wait_ge(s["m_xs"], g)
                        gather(1 - j, range(KT), s["m_xg_ps"])
                        pe.wait_ge(s["m_act"], it + 1)
                        act_T(s["m_actT_ps"])
                        pe.wait_ge(s["m_actT"], it + 1)
                        if not start:
                            pe.wait_ge(s["m_nat"], it)
                        for u in range(UNITS_UP, UNITS):
                            unit(j, u, it)

                pair(0, True)
                with pe.Fori(1, NE // 2) as i:
                    pair(i, False)

                pe.wait_ge(s["flag"], l + 1)
                more = pe.value_load(flag_i[0:1, 0:1], min_val=0, max_val=1)
                r = lambda n: s[f"r_{n}{l}"]
                with pe.If(more > 0):
                    pe.wait_ge(s["m_nat"], NE * (l + 1))
                    pe.wait_ge(s["m_xs"], (NE + 1) * (l + 1))
                    with pe.Fori(0, NE) as e:
                        pe.wait_ge(s[f"rw{l}"], 48 * (e + 1))
                        for b in range(STEPS_REST):
                            it = STEPS_REST * e + b
                            pe.wait_ge(r("dve"), rest_at(it, "G") + 1)
                            gather(b % 2, range(KT), r("pe"))
                            pe.wait_ge(r("dve"), rest_at(it, "xs") + 1)
                            whole(xs[b % 2], wup[0], 2, r("pe"))
                            pe.wait_ge(r("dve"), rest_at(it, "act") + 1)
                            act_T(r("pe"))
                            pe.wait_ge(r("dve"), rest_at(it, "actT") + 1)
                            whole(actT, wdn[0], 6, r("pe"))
                with pe.Else():
                    pe.nop()

        @block.scalar
        def _(act):
            link = chain(act, s["act_chain"])

            def norm_scale(n):
                for t, (_, m) in enumerate(TILES):
                    act.wait_ge(s["norm_ss"], 3 * (n - 1) + t + 1)
                    link(act.activation(st[0:m, 4 + t:5 + t], st[0:m, t:t + 1], ACT.Ln, scale=1.0 / D, bias=cst[0:m, 0:1]))
                    act.activation(st[0:m, 8 + t:9 + t], st[0:m, 4 + t:5 + t], ACT.Exp, scale=-0.5).then_inc(s["norm_rs"], 1)

            def copy_hT(n):
                for k in range(KT):
                    act.wait_ge(s["hT_ps"], 8 * (n - 1) + k + 1)
                    act.copy(hT[:, k, :], ps[k % 2][:, 0:T]).then_inc(s["hT"], 1)

            def xs_high(it, par, s_in, s_done):
                act.wait_ge(s_in, it + 1)
                act.copy(xs[par][:, :, 0, :], ps[par][:, 0:KT * CAP].rearrange("p (k n) -> p k n", k=KT)).then_inc(s_done, 1)

            def low_rows(dst, bank, s_done):
                act.copy(dst[0:CAP, :], ps[bank][CAP:2 * CAP, :]).then_inc(s_done, 1)

            def tanh_gate(n_in, s_in, s_done):
                act.wait_ge(s_in, n_in + 1)
                act.activation(ex[0:CAP, :], gate[0:CAP, :], ACT.Tanh, scale=0.5).then_inc(s_done, 1)

            def actT_high(it, s_in, s_done):
                act.wait_ge(s_in, it + 1)
                act.copy(actT[:, :, 0, :], ps[5][:, :].rearrange("p (f n) -> p f n", f=4)[:, :, 0:CAP]).then_inc(s_done, 1)

            tn = [0]

            def out(dst, m, n=T, func=ACT.Copy, **kw):
                act.wait_ge(s["pj_ps"], tn[0] + 1)
                act.activation(dst, ps[tn[0] % 2][0:m, 0:n], func, **kw).then_inc(s["pj_out"], 1)
                tn[0] += 1

            def attention(l):
                for m in range(2):
                    act.wait_ge(s["mm_ss"], 2 * l + m + 1)
                    link(act.activation(mm_st[:, 2 + m:3 + m], mm_st[:, m:m + 1], ACT.Ln, scale=1.0 / D, bias=cst[:, 0:1]))
                    act.activation(mm_st[:, 4 + m:5 + m], mm_st[:, 2 + m:3 + m], ACT.Exp, scale=-0.5).then_inc(s["mm_rs"], 1)
                norm_scale(2 * l + 1)
                for k in range(KT):
                    act.wait_ge(s["mm_T_ps"], KT * l + k + 1)
                    act.copy(memT[:, k, :], ps[2 + k % 2][:, 0:N_MEM]).then_inc(s["mm_T"], 1)
                for m in range(2):
                    out(kvn[:, m, :], 128, n=2 * MEMW)
                act.wait_ge(s["kT_ps"], l + 1)
                act.copy(kT, ps[2][:, :].rearrange("p (a b) -> p a b", a=2)).then_inc(s["kT"], 1)
                copy_hT(2 * l + 1)
                for q in range(2):
                    out(qT[:, q, :], 128)
                act.wait_ge(s["qn_ps"], 9 * l + 1)
                act.copy(qs[0:TS, :], ps[3][0:TS, 0:MEMW]).then_inc(s["qn"], 1)
                for hd in range(4):
                    act.wait_ge(s["sc_max"], 4 * l + hd + 1)
                    for t in range(2):
                        n = 2 * hd + t
                        last = act.activation(P[:, hd, t, :], ps[4 + hd][:, 256 * t:256 * (t + 1)], ACT.Exp, scale=0.125, bias=snx[:, n:n + 1],
                                              accum_out=ssm[:, n:n + 1])
                    last.then_inc(s["sc_exp"], 1)
                for hd in range(4):
                    act.wait_ge(s["pT_ps"], 4 * l + hd + 1)
                    act.copy(PT[:, hd].rearrange("p m t -> p (m t)"), ps[4 + hd][:, :]).then_inc(s["pT"], 1)
                m0 = KT - 2 if l == 0 else KT
                act.wait_ge(s["at_ps"], l + 1)
                act.copy(mixedT[:, m0:m0 + 2, 0:TP], ps[2][:, :].rearrange("p (a b) -> p a b", a=2)).then_inc(s["at_out"], 1)
                act.wait_ge(s["s_max"], l + 1)
                act.activation(sp_s[0:32, :], ps[3][0:32, 0:N_MEM], ACT.Exp, scale=0.125, bias=snx[0:32, 0:1], accum_out=ssm[0:32, 0:1]).then_inc(s["s_exp"], 1)
                act.wait_ge(s["spT_ps"], l + 1)
                act.copy(spT, ps[3][:, 0:64]).then_inc(s["spT"], 1)
                act.wait_ge(s["sat_ps"], l + 1)
                for hp in range(2):
                    for u in range(2):
                        rows = slice(64 * u, 64 * u + 64)
                        last = act.copy(mixedT[rows, m0 + hp, TP:T], ps[2][rows, 32 * hp + 2 * hp + u:32 * hp + 32:4])
                last.then_inc(s["sat_out"], 1)

            def mixer0():
                act.wait_ge(s["sat_out"], 1)
                for dst in (vr, vk, vv):
                    for q in range(PAIRS):
                        out(dst[:, q, :], 128)
                act.wait_ge(s["vecT"], 1)
                out(w1o[0:64, :], 64, func=ACT.Exp, scale=-2.0)
                out(a1o[0:64, :], 64)
                out(g1o, 128, func=ACT.Exp, scale=-1.0)
                for q in range(PAIRS):
                    out(vld[:, q, :], 128, func=ACT.Exp, scale=-1.0, bias=nvec[:, q:q + 1])
                for q in range(PAIRS):
                    out(vb[:, q, :], 128, func=ACT.Exp, scale=-1.0, bias=nvec[:, PAIRS + q:PAIRS + q + 1])
                for q in range(PAIRS):
                    out(vg[:, q, :], 128)
                act.wait_ge(s["t_dve"], 2)
                link(act.activation(vL, vL, ACT.Ln, scale=2.0 ** 32))
                act.activation(vL, vL, ACT.Exp, scale=-0.5, bias=cst[:, 3:4]).then_inc(s["t_act"], 1)
                act.wait_ge(s["t_dve"], 4)
                act.activation(TT[2][:, 0:PAIRS, TP:T], vld[:, :, TP:T], ACT.Exp)
                act.activation(TT[2][:, 0:PAIRS, 0:TP], TT[2][:, 0:PAIRS, 0:TP], ACT.Exp)
                act.activation(TT[1][:, 0:PAIRS, 0:TP], vL[:, :, 0:TP], ACT.Exp).then_inc(s["t_act"], 1)
                act.wait_ge(s["t_dve"], 5)
                act.activation(TT[0][:, 0:PAIRS, 0:TP], vL[:, :, 0:TP], ACT.Exp, scale=-1.0).then_inc(s["t_act"], 1)
                for n in range(6):
                    act.wait_ge(s["qn_ps"], n + 2)
                    if n >= 2:
                        act.wait_ge(s[f"dec_scr{n % 2}"], 16 * (n // 2))
                    for u in range(2):
                        last = act.copy(Dn[n % 2][:, 384 * u:384 * (u + 1)], ps[2 + u][0:TS, 0:384])
                    last.then_inc(s["qn"], 1)

                dst = {"Bn": cBn, "Kn": cKn, "Vn": cVn, "X2": cX2, "X2T": cX2T, "X4": cX4, "X4T": cX4T, "X8T": cX2T, "W1": cX2, "W2": cX4,
                       "RHS": cX4T, "SA": cX2T}
                act.wait_ge(s["c_pool"], 1)
                for c in range(NCH):
                    for name, e in ROUNDS:
                        if e != "act":
                            continue
                        for hf in range(2):
                            act.wait_ge(s["c_ps"], c_ps_at(c, name, hf))
                            b = ps[2 * (ORDER.index(name) % 4) + hf]
                            pairs = slice(3 * hf, 3 * hf + 3)
                            if name == "Y":
                                for u in range(2):
                                    rows = slice(64 * u, 64 * u + 64)
                                    last = act.copy(vL[rows, pairs, C * c:C * (c + 1)],
                                                    b[rows, 0:384].rearrange("p (q n) -> p q n", q=3)[:, :, 64 * u:64 * u + 64])
                            else:
                                last = act.copy(dst[name][:, pairs, :], b[:, 0:384].rearrange("p (q n) -> p q n", q=3))
                            last.then_inc(s["c_act"], 1)
                act.wait_ge(s["qn_ps"], 8)
                for u in range(2):
                    last = act.copy(cX2[:, 3 * u:3 * u + 3, :], ps[2 + u][:, 0:384].rearrange("p (q n) -> p q n", q=3))
                last.then_inc(s["t_act"], 1)
                act.wait_ge(s["qn_ps"], 9)
                act.copy(vL[:, :, TP:T], ps[4][:, 0:TS * PAIRS].rearrange("p (q b) -> p q b", q=PAIRS)).then_inc(s["t_act"], 1)
                act.wait_ge(s["sum_ps"], 4)
                for q in range(PAIRS):
                    link(act.activation(TT[1][:, q, :], ps[2 + q][:, 0:T], ACT.Ln, scale=1.0 / 64, bias=cst[:, 2:3]))
                act.activation(TT[1][:, 0:PAIRS, :], TT[1][:, 0:PAIRS, :], ACT.Exp, scale=-0.5).then_inc(s["t_act"], 1)

            def mixer1():
                act.wait_ge(s["sat_out"], 2)
                act.wait_ge(s["kv_stored"], 64)
                for i in range(4):
                    out(gq[0:96, i, :], 96, scale=96.0 ** -0.5)
                for i in range(4):
                    out(gk[0:96, i, :], 96)
                for i in range(8):
                    out(gv[0:96, i, :], 96)
                for i in range(8):
                    out(grt[0:96, i, :], 96)
                out(ga1o[0:16, :], 16)
                act.wait_ge(s["vecT"], 2)
                for i in range(4):
                    out(gl[0:96, i, :], 96, func=ACT.Identity, bias=vecT[0:96, i:i + 1])
                act.wait_ge(s["qn_ps"], 11)
                for u in range(2):
                    last = act.copy(gvs[0:TS, 384 * u:384 * (u + 1)], ps[2 + u][0:TS, 0:384])
                last.then_inc(s["qn"], 1)
                act.wait_ge(s["t_dve"], 10)
                link(act.activation(ge[0:96], ge[0:96], ACT.Exp, scale=-1.0))
                act.activation(ge[0:96], ge[0:96], ACT.Ln, bias=ones[0:96, 0:1]).then_inc(s["t_act"], 1)
                act.wait_ge(s["t_dve"], 11)
                act.activation(gkh[0:96, :, TP:T], gl[0:96, :, TP:T], ACT.Exp).then_inc(s["t_act"], 1)
                act.wait_ge(s["t_dve"], 12)
                act.activation(gem[0:96, :], gem[0:96, :], ACT.Exp)
                act.activation(gee[0:96, :], gee[0:96, :], ACT.Exp)
                g0, g1 = go[0:96, 0:4, 0:TP], go[0:96, 4:8, 0:TP]
                act.activation(gkh[0:96, :, 0:TP], g1, ACT.Exp).then_inc(s["t_act"], 1)
                act.wait_ge(s["t_dve"], 13)
                act.activation(g1, g0, ACT.Exp, scale=-1.0)
                link(act.activation(gl[0:96, :, 0:TP], g0, ACT.Exp))
                act.nop()
                act.sem_inc(s["t_act"], 1)
                act.wait_ge(s["sat_ps"], 3)
                act.wait_ge(s["t_dve"], 14)
                act.copy(go[0:96, :, TP:T], ps[6][0:96, 0:64].rearrange("p (i b) -> p i b", b=TS)).then_inc(s["sat_out"], 1)
                for c in range(NCH):
                    act.wait_ge(s["c_ps"], 2 * len(ROUNDS) * NCH + 4 * c + 1)
                    for u in range(2):
                        act.copy(gvn[0:C, 384 * u:384 * (u + 1)], ps[2 + u][0:C, 0:384])
                    act.copy(gkn[0:C, :], ps[4][0:C, 0:384]).then_inc(s["c_act"], 1)
                    act.wait_ge(s["c_ps"], 2 * len(ROUNDS) * NCH + 4 * c + 3)
                    act.copy(go[0:96, :, C * c:C * (c + 1)], ps[6][0:96, :].rearrange("p (i n) -> p i n", i=8)).then_inc(s["c_act"], 1)
                act.wait_ge(s["sum_ps"], 5)
                for i in range(4):
                    link(act.activation(ge[0:96, i, :], ps[2 + i][0:96, 0:T], ACT.Ln, scale=1.0 / 192, bias=cst[0:96, 0:1]))
                act.activation(ge[0:96], ge[0:96], ACT.Exp, scale=-0.5).then_inc(s["t_act"], 1)
                act.activation(gv[0:96], grt[0:96], ACT.Exp, scale=-1.0).then_inc(s["t_act"], 1)

            for l in range(DEPTH):
                if l == 0:
                    act.wait_ge(s["consts"], 1)
                attention(l)
                (mixer0, mixer1)[l]()
                tn[0] += 3 * len(W_OUT[l])
                norm_scale(2 * l + 2)
                copy_hT(2 * l + 2)
                act.wait_ge(s["logits"], l + 1)
                for t in range(3):
                    act.activation(gt[:, t, 0:4], gt[:, t, 0:4], ACT.Exp)
                act.activation(gt[:, :, 4], gt[:, :, 4], ACT.Exp).then_inc(s["gate_e"], 1)
                base, gb = NE * l, (NE + 1) * l
                xs_high(gb, 0, s["m_xg_ps"], s["m_xh"])

                def convert_units(i, j, units, waits=True):
                    for u in units:
                        if u == 0:
                            act.wait_ge(s[f"wupa{j}"], 16 * (NE // 2) * l + 16 * (i + 1))
                        if u == UNITS_UP // 2:
                            act.wait_ge(s[f"wupb{j}"], 16 * (NE // 2) * l + 16 * (i + 1))
                        if u == UNITS_UP:
                            act.wait_ge(s[f"wdn{j}"], 16 * (NE // 2) * l + 16 * (i + 1))
                        if waits:
                            act.wait_ge(s["m_used"], UNITS * (base + 2 * i + j) + u - RING + 1)
                        act.copy(ring[(UNITS * j + u) % RING], unit_of(j, u)).then_inc(s["m_wh"], 1)

                def pair(i, first=False, final=False):
                    for j in range(2):
                        it = base + 2 * i + j
                        ahead = not (final and j == 1)
                        nxt = (i, 1) if j == 0 else (i + 1, 0)
                        act.wait_ge(s["m_used"], UNITS * it + UNITS_UP)
                        low_rows(gate, 2, s["m_glo"])
                        low_rows(upp, 3, s["m_ulo"])
                        tanh_gate(it, s["m_g"], s["m_tanh"])
                        convert_units(i, j, (9, 10))
                        xs_high(gb + 2 * i + j + 1, 1 - j, s["m_xg_ps"], s["m_xh"])
                        actT_high(it, s["m_actT_ps"], s["m_ah"])
                        convert_units(i, j, (11,))
                        if ahead:
                            convert_units(*nxt, range(0, 6))
                        act.wait_ge(s["m_used"], UNITS * (it + 1))
                        if not (l == 0 and first):
                            act.wait_ge(s[f"m_ywr{j}"], 16 * (base // 2 + i))
                        low_rows(ynat[j][:, 0:FF], 6, s["m_ylo"])
                        low_rows(ynat[j][:, FF:D], 7, s["m_ylo"])
                        if ahead:
                            convert_units(*nxt, range(6, 9))

                act.wait_ge(s["h_parts"], l + 1)
                act.wait_ge(s["logit_ps"], l + 1)
                convert_units(0, 0, range(0, 8), waits=False)
                convert_units(0, 0, (8,))
                pair(0, first=True)
                with act.Fori(1, NE // 2 - 1) as i:
                    pair(i)
                pair(NE // 2 - 1, final=True)
                act.wait_ge(s["flag"], l + 1)
                more = act.value_load(flag_i[0:1, 0:1], min_val=0, max_val=1)
                r = lambda n: s[f"r_{n}{l}"]
                with act.If(more > 0):
                    with act.Fori(0, NE) as e:
                        for b in range(STEPS_REST):
                            it = STEPS_REST * e + b
                            xs_high(rest_at(it, "xg"), b % 2, r("pe"), r("act"))
                            act.wait_ge(r("pe"), rest_at(it, "up") + 1)
                            low_rows(gate, 2, r("act"))
                            low_rows(upp, 3, r("act"))
                            tanh_gate(rest_at(it, "gate"), r("dve"), r("act"))
                            actT_high(rest_at(it, "actT_ps"), r("pe"), r("act"))
                            act.wait_ge(r("pe"), rest_at(it, "down") + 1)
                            low_rows(ynat[b % 2][:, 0:FF], 6, r("act"))
                            low_rows(ynat[b % 2][:, FF:D], 7, r("act"))
                with act.Else():
                    act.nop()
            norm_scale(5)

        @block.vector
        def _(dve):
            link = chain(dve, s["dve_chain"])

            def norm(n, out):
                if n == 1:
                    dve.wait_ge(s["x_loaded"], 32)
                for t, (_, m) in enumerate(TILES):
                    dve.tensor_tensor_reduce(sq[0:m, :], x[0:m, t, :], x[0:m, t, :], 1.0, 0.0, ALU.mult, ALU.add, st[0:m, t:t + 1]).then_inc(s["norm_ss"], 1)
                    dve.wait_ge(s["norm_ss"], 3 * (n - 1) + t + 1)
                dve.wait_ge(s["gain_loaded"], 16 * n)
                for t, (_, m) in enumerate(TILES):
                    dve.wait_ge(s["norm_rs"], 3 * (n - 1) + t + 1)
                    dve.scalar_tensor_tensor(out=out[0:m, t, :], in0=x[0:m, t, :], scalar=st[0:m, 8 + t:9 + t], in1=gain[0:m, :],
                                             op0=ALU.mult, op1=ALU.mult).then_inc(s["norm_h"], 1)

            def route(l):
                link(dve.memset(lg, 0.0))
                link(dve.memset(g8, -BIG))
                dve.wait_ge(s["logit_ps"], l + 1)
                dve.wait_ge(s["router_w"], 64 * (l + 1))
                for t, (_, m) in enumerate(TILES):
                    link(dve.tensor_tensor(lg[0:m, t, :], ps[2][0:m, t * 36:(t + 1) * 36], br[0:m, :], ALU.add))
                link(dve.tensor_copy(g8[:, :, 0:4], lg[:, :, 0:4]))
                for t in range(3):
                    link(dve.max(m8[:, t, :], g8[:, t, :]))
                    link(dve.max_index(idx_u[:, t, :], m8[:, t, :], g8[:, t, :]))
                link(dve.tensor_copy(i8f, idx_u))
                link(dve.tensor_tensor(gt[:, :, 0:4], lg[:, :, 0:4], m8[:, :, 0:1].broadcast_to([128, 3, 4]), ALU.subtract))
                link(dve.tensor_tensor(tmp32, iota_g[:, :].unsqueeze(1).broadcast_to([128, 3, NE]), i8f[:, :, 0:1].broadcast_to([128, 3, NE]), ALU.is_equal))
                link(dve.tensor_scalar(tmp32, tmp32, -1.0, BIG, ALU.add, ALU.mult))
                link(dve.tensor_tensor(em, lg[:, :, 4:36], tmp32, ALU.add))
                for t in range(3):
                    link(dve.max(m8[:, t, :], em[:, t, :]))
                    link(dve.max_index(idx_u[:, t, :], m8[:, t, :], em[:, t, :]))
                link(dve.tensor_copy(i8f, idx_u))
                dve.tensor_tensor(gt[:, :, 4:5], m8[:, :, 1:2], m8[:, :, 0:1], ALU.subtract).then_inc(s["logits"], 1)
                for k, a in enumerate((a1, a2)):
                    link(dve.tensor_tensor(a, iota_e[:, :].unsqueeze(1).broadcast_to([128, 3, NE]), i8f[:, :, k:k + 1].broadcast_to([128, 3, NE]), ALU.is_equal))
                    link(dve.tensor_tensor(a, a, valid[:, :].unsqueeze(2).broadcast_to([128, 3, NE]), ALU.mult))
                dve.tensor_tensor(asum, a1, a2, ALU.add).then_inc(s["gates"], 1)
                dve.wait_ge(s["gate_e"], l + 1)
                link(dve.tensor_reduce(gt[:, :, 5:6], gt[:, :, 0:4], AXX, ALU.add))
                link(dve.tensor_scalar(gt[:, :, 6:7], gt[:, :, 4:5], 1.0, None, ALU.add))
                link(dve.tensor_tensor(gt[:, :, 5:6], gt[:, :, 5:6], gt[:, :, 6:7], ALU.mult))
                link(dve.reciprocal(gt[:, :, 6:7], gt[:, :, 5:6]))
                link(dve.tensor_tensor(gt[:, :, 7:8], gt[:, :, 6:7], gt[:, :, 4:5], ALU.mult))
                dve.wait_ge(s["rank_ps"], l + 1)
                link(dve.tensor_copy(rank, ps[3][:, 0:3 * NE].rearrange("p (t n) -> p t n", t=3)))
                for k, a in enumerate((a1, a2)):
                    link(dve.tensor_tensor(tmp32, rank, a, ALU.mult))
                    link(dve.tensor_reduce(rowf.rearrange("p (t n) -> p t n", t=3)[:, :, k:k + 1], tmp32, AXX, ALU.add))
                rank2 = rowf.rearrange("p (t n) -> p t n", t=3)
                v3 = lambda a: a[:, :].rearrange("p (t n) -> p t n", t=3)
                link(dve.tensor_scalar(in_rest[:, :], rowf, float(CAP), None, ALU.is_ge))
                link(dve.tensor_scalar(gr[:, :], rowf, float(CAP - 1), None, ALU.min))
                link(dve.scalar_tensor_tensor(out=v3(gr), in0=i8f[:, :, 0:2], scalar=float(CAP), in1=v3(gr), op0=ALU.mult, op1=ALU.add))
                link(dve.tensor_copy(rows_i[:, :], gr[:, :]))
                link(dve.tensor_scalar(gr[:, :], rowf, float(-CAP), 0.0, ALU.add, ALU.max))
                link(dve.scalar_tensor_tensor(out=v3(gr), in0=i8f[:, :, 0:2], scalar=float(RROWS), in1=v3(gr), op0=ALU.mult, op1=ALU.add))
                link(dve.tensor_copy(rows_r[:, :], gr[:, :]))
                link(dve.tensor_tensor(v3(gr), gt[:, :, 6:8], v3(in_rest), ALU.mult))
                link(dve.tensor_tensor(gt[:, :, 6:8], gt[:, :, 6:8], v3(gr), ALU.subtract))
                link(dve.memset(R, -1.0))
                link(dve.scalar_tensor_tensor(out=R[:, :, 0:NE], in0=rank, scalar=1.0, in1=asum, op0=ALU.add, op1=ALU.mult))
                link(dve.tensor_scalar(R[:, :, 0:NE], R[:, :, 0:NE], -1.0, None, ALU.add))
                dve.tensor_reduce(flagf[:, 0:1], R.rearrange("p t n -> p (t n)"), AXX, ALU.max).then_inc(s["ranks"], 1)
                dve.wait_ge(s["flagT_ps"], l + 1)
                link(dve.tensor_reduce(flagf[0:1, 1:2], ps[3][0:1, 256:384], AXX, ALU.max))
                link(dve.tensor_scalar(flagf[0:1, 2:3], flagf[0:1, 1:2], float(CAP), None, ALU.is_ge))
                dve.tensor_copy(flag_i[0:1, 0:1], flagf[0:1, 2:3]).then_inc(s["flag"], 1)

            def onehot(e, step, par, s_done):
                dve.tensor_tensor(G[par], iota_rank[:, CAP * step:CAP * (step + 1)].unsqueeze(1).broadcast_to([128, 3, CAP]),
                                  R[:, :, bass.ds(e, 1)].broadcast_to([128, 3, CAP]), ALU.is_equal).then_inc(s_done, 1)

            def xs_low(it, par, s_in, s_done):
                dve.wait_ge(s_in, it + 1)
                dve.tensor_tensor(xs[par][:, :, 1, :], ps[par][:, 0:KT * CAP].rearrange("p (k n) -> p k n", k=KT), xs[par][:, :, 0, :].bitcast(F32),
                                  ALU.subtract).then_inc(s_done, 1)

            def actT_low(it, s_in, s_done):
                dve.wait_ge(s_in, it + 1)
                dve.tensor_tensor(actT[:, :, 1, :], ps[5][:, :].rearrange("p (f n) -> p f n", f=4)[:, :, 0:CAP], actT[:, :, 0, :].bitcast(F32),
                                  ALU.subtract).then_inc(s_done, 1)

            def sum_rows(dst, bank, it, s_in, s_done):
                dve.wait_ge(s_in, it + 1)
                dve.tensor_tensor(dst[0:CAP, :], ps[bank][0:CAP, :], dst[0:CAP, :], ALU.add).then_inc(s_done, 1)

            def swiglu(tanh, up, q, s_done):
                dve.wait_ge(tanh[0], tanh[1] + 1)
                dve.scalar_tensor_tensor(out=ex[0:CAP, :], in0=ex[0:CAP, :], scalar=1.0, in1=gate[0:CAP, :], op0=ALU.add, op1=ALU.mult).then_inc(q[0], 1)
                dve.wait_ge(q[0], q[1] + 1)
                dve.wait_ge(up[0], up[1] + 1)
                dve.scalar_tensor_tensor(out=an[0:CAP, :], in0=ex[0:CAP, :], scalar=0.5, in1=upp[0:CAP, :], op0=ALU.mult, op1=ALU.mult).then_inc(s_done, 1)

            def nat_out(n, par, s_in, s_done):
                dve.wait_ge(s_in, n + 1)
                dve.tensor_tensor(ynat[par][0:CAP, 0:FF], ps[6][0:CAP, :], ynat[par][0:CAP, 0:FF], ALU.add)
                dve.wait_ge(s_in, n + 2)
                dve.tensor_tensor(ynat[par][0:CAP, FF:D], ps[7][0:CAP, :], ynat[par][0:CAP, FF:D], ALU.add).then_inc(s_done, 1)

            def split_h():
                for t, (_, m) in enumerate(TILES):
                    a = h[0:m, t, :]
                    link(dve.tensor_copy(hp[0][0:m, t, :], a))
                    link(dve.tensor_tensor(sq[0:m, :], a, hp[0][0:m, t, :], ALU.subtract))
                    link(dve.tensor_copy(hp[1][0:m, t, :], sq[0:m, :]))
                    link(dve.tensor_tensor(sq[0:m, :], sq[0:m, :], hp[1][0:m, t, :], ALU.subtract))
                    last = link(dve.tensor_copy(hp[2][0:m, t, :], sq[0:m, :])) if t < 2 else dve.tensor_copy(hp[2][0:m, t, :], sq[0:m, :])
                last.then_inc(s["h_parts"], 1)

            def mark(ins, name, value):
                ins.then_inc(s[name], 1)
                dve.wait_ge(s[name], value)

            def setup():
                dve.wait_ge(s["vecT_ps"], 2)
                link(dve.tensor_copy(vecT[:, :], ps[7][:, 0:90]))
                link(dve.tensor_scalar(nvec[:, :], vecT[:, 48:60], -1.0, None, ALU.mult))
                for n, m in enumerate((mlow, moff1, moff2)):
                    link(dve.tensor_tensor(m[:, :], ps[6][:, 128 * n:128 * (n + 1)], m[:, :], ALU.is_equal))
                link(dve.tensor_copy(block64[:, :], moff2[:, :]))
                link(dve.tensor_tensor(mup[:, :], mlow[:, :], before[:, :], ALU.mult))
                link(dve.tensor_tensor(moff2[:, :], block64[:, :], moff1[:, :], ALU.subtract))
                link(dve.tensor_tensor(moff1[:, :], moff1[:, :], mlow[:, :], ALU.subtract))
                for m in (mlow, moff1, moff2):
                    link(dve.tensor_tensor(sq[:, 0:128], m[:, :], upto[:, :], ALU.mult))
                    link(dve.tensor_tensor(m[:, :], m[:, :], sq[:, 0:128], ALU.subtract))
                mark(dve.memset(sq[:, 0:1], 0.0), "vecT", 1)

            def attention(l):
                dve.wait_ge(s["mm_in"], 32 * (l + 1))
                for m in range(2):
                    mark(dve.tensor_tensor_reduce(sq, mem[:, m, :], mem[:, m, :], 1.0, 0.0, ALU.mult, ALU.add, mm_st[:, m:m + 1]), "mm_ss", 2 * l + m + 1)
                for m in range(2):
                    dve.wait_ge(s["mm_rs"], 2 * l + m + 1)
                    dve.scalar_tensor_tensor(out=mem[:, m, :], in0=mem[:, m, :], scalar=mm_st[:, 4 + m:5 + m], in1=gmem, op0=ALU.mult,
                                             op1=ALU.mult).then_inc(s["mm_h"], 1)
                norm(2 * l + 1, h)
                for hd in range(4):
                    dve.wait_ge(s["sc_ps"], 4 * l + hd + 1)
                    link(dve.tensor_reduce(smx[:, 2 * hd:2 * hd + 2], ps[4 + hd][:, :].rearrange("p (t m) -> p t m", t=2), AXX, ALU.max))
                    mark(dve.tensor_scalar(snx[:, 2 * hd:2 * hd + 2], smx[:, 2 * hd:2 * hd + 2], -0.125, None, ALU.mult), "sc_max", 4 * l + hd + 1)
                for hd in range(4):
                    dve.wait_ge(s["sc_exp"], 4 * l + hd + 1)
                    link(dve.reciprocal(srs[:, 2 * hd:2 * hd + 2], ssm[:, 2 * hd:2 * hd + 2]))
                    dve.tensor_tensor(P[:, hd], P[:, hd], srs[:, 2 * hd:2 * hd + 2].unsqueeze(2).broadcast_to([128, 2, N_MEM]),
                                      ALU.mult).then_inc(s["sc_prob"], 1)
                dve.wait_ge(s["qb_ps"], 1 if l == 0 else 2)
                dve.wait_ge(s["cache_k"], 32 * (l + 1))
                for m in range(2):
                    for b in range(0, TS, 2):
                        link(dve.tensor_tensor(KC[:, m, b:b + 2, :], KC[:, m, b:b + 2, :], ps[4 + b // 2][:, :].rearrange("p (b n) -> p b n", b=2), ALU.mult))
                mark(dve.tensor_reduce(sc_s, KC.rearrange("p m b (h d) -> p (m b h) d", d=64), AXX, ALU.add), "s_score", l + 1)
                dve.wait_ge(s["sT_ps"], l + 1)
                link(dve.tensor_reduce(smx[0:32, 0:1], ps[3][0:32, 0:N_MEM], AXX, ALU.max))
                mark(dve.tensor_scalar(snx[0:32, 0:1], smx[0:32, 0:1], -0.125, None, ALU.mult), "s_max", l + 1)
                dve.wait_ge(s["s_exp"], l + 1)
                link(dve.reciprocal(srs[0:32, 0:1], ssm[0:32, 0:1]))
                mark(dve.tensor_scalar(sp_s[0:32, :], sp_s[0:32, :], srs[0:32, 0:1], None, ALU.mult), "s_prob", l + 1)
                dve.wait_ge(s["sat_out"], l + 1)

            def output(l):
                n = tiles_through(CHUNKS[0] - 1 if l == 0 else sum(CHUNKS) - 1) - 3 * len(W_OUT[l])
                for c0, w in W_OUT[l]:
                    for t, (_, m) in enumerate(TILES):
                        dve.wait_ge(s["pj_ps"], n + 1)
                        mark(dve.tensor_tensor(x[0:m, t, c0:c0 + w], ps[n % 2][0:m, 0:w], x[0:m, t, c0:c0 + w], ALU.add), "pj_out", n + 1)
                        n += 1
                mark(dve.memset(sq[:, 0:1], 0.0), "x_out", l + 1)

            vec = lambda at: vecT[:, at:at + PAIRS].unsqueeze(2).broadcast_to([128, PAIRS, T])
            V_KK, V_KA, V_RK, V_LG, V_LB = 60, 66, 72, 78, 84

            def mixer0():
                T0, T1, T2 = (a[:, 0:PAIRS, :] for a in TT)
                xx = TT[0]
                dve.wait_ge(s["hT"], KT)
                dve.wait_ge(s["shiftT_ps"], 1)
                dve.tensor_tensor(xx[:, :, 1:TP], hT[:, :, 0:TP - 1], hT[:, :, 1:TP], ALU.subtract)
                dve.tensor_scalar(xx[:, :, 0:1], hT[:, :, 0:1], -1.0, None, ALU.mult)
                link(dve.tensor_tensor(xx[:, :, TP:T], ps[7][:, 0:KT * TS].rearrange("p (k b) -> p k b", k=KT), hT[:, :, TP:T], ALU.subtract))
                done = {2: 10, 3: 16, 4: 22, 5: 23}

                def blend(i, j):
                    if i in done:
                        dve.wait_ge(s["pj_ps"], done[i])
                    for k in range(KT):
                        last = dve.scalar_tensor_tensor(out=TT[1 + i % 2][:, k, :], in0=xx[:, k, :], scalar=vecT[:, 8 * j + k:8 * j + k + 1], in1=hT[:, k, :],
                                                        op0=ALU.mult, op1=ALU.add)
                    last.then_inc(s["xj"], 1)

                for i, j in enumerate((0, 2, 3, 1, 4)):
                    blend(i, j)
                    if i == 3:
                        dve.wait_ge(s["pj_out"], 16)
                        link(dve.tensor_tensor(vkk, vk, vec(V_KK), ALU.mult))
                        mark(dve.tensor_tensor(vL, vkk, vkk, ALU.mult), "t_dve", 1)
                dve.wait_ge(s["pj_out"], 23)
                link(dve.tensor_scalar(w1o[0:64, :], w1o[0:64, :], 1.0, None, ALU.add))
                link(dve.reciprocal(w1o[0:64, :], w1o[0:64, :]))
                mark(dve.tensor_scalar(w1o[0:64, :], w1o[0:64, :], 2.0, -1.0, ALU.mult, ALU.add), "lora_s", 1)
                blend(5, 5)
                dve.wait_ge(s["pj_out"], 25)
                link(dve.tensor_scalar(g1o, g1o, 1.0, None, ALU.add))
                mark(dve.reciprocal(g1o, g1o), "lora_s", 2)
                dve.wait_ge(s["sum_ps"], 1)
                for q in range(PAIRS):
                    link(dve.tensor_scalar(vL[:, q, :], ps[2 + q][:, 0:T], 1e-24, None, ALU.max))
                mark(dve.memset(sq[:, 0:1], 0.0), "t_dve", 2)
                dve.wait_ge(s["t_act"], 1)
                link(dve.tensor_tensor(vkk, vkk, vL, ALU.mult))
                dve.wait_ge(s["pj_out"], 31)
                link(dve.tensor_scalar(vld, vld, 1.0, None, ALU.add))
                link(dve.reciprocal(vL, vld))
                link(dve.tensor_scalar(vld, vL, -float(np.exp(-0.5)), None, ALU.mult))
                for q in range(PAIRS):
                    for c in range(NCH):
                        cc = slice(C * c, C * (c + 1))
                        last = dve.tensor_tensor_scan(vL[:, q, cc], ones[:, 0:C], vld[:, q, cc], 0.0, ALU.mult, ALU.add)
                link(last)
                dve.wait_ge(s["pj_out"], 37)
                link(dve.tensor_scalar(vb, vb, 1.0, None, ALU.add))
                link(dve.reciprocal(vb, vb))
                link(dve.tensor_scalar(T0, vb, -1.0, None, ALU.add))
                link(dve.tensor_tensor(T0, T0, vec(V_KA), ALU.mult))
                link(dve.scalar_tensor_tensor(out=vk, in0=T0, scalar=1.0, in1=vk, op0=ALU.add, op1=ALU.mult))
                link(dve.tensor_tensor(vb, vb, vkk, ALU.mult))
                link(dve.tensor_tensor(T0, vr, vk, ALU.mult))
                mark(dve.tensor_tensor(T0, T0, vec(V_RK), ALU.mult), "t_dve", 3)
                mark(dve.tensor_tensor(T2[:, :, 0:TP], vL[:, :, 0:TP], vld[:, :, 0:TP], ALU.subtract), "t_dve", 4)
                dve.wait_ge(s["sum_ps"], 2)
                dve.wait_ge(s["t_act"], 2)
                for q in range(PAIRS):
                    link(dve.tensor_tensor(vld[:, q, :], ps[2 + q][:, 0:T], vv[:, q, :], ALU.mult))
                mark(dve.memset(sq[:, 0:1], 0.0), "t_dve", 5)
                dve.wait_ge(s["t_act"], 3)
                pc = slice(0, TP)
                link(dve.tensor_copy(lam[:, :, :], T1[:, :, C - 1:TP:C]))
                link(dve.tensor_tensor(vr[:, :, pc], vr[:, :, pc], T1[:, :, pc], ALU.mult))
                link(dve.scalar_tensor_tensor(out=vkk[:, :, pc], in0=vkk[:, :, pc], scalar=-1.0, in1=T2[:, :, pc], op0=ALU.mult, op1=ALU.mult))
                link(dve.tensor_tensor(vk[:, :, pc], vk[:, :, pc], T0[:, :, pc], ALU.mult))
                dve.wait_ge(s["qn"], 7)
                mark(dve.tensor_tensor(vb[:, :, pc], vb[:, :, pc], T0[:, :, pc], ALU.mult), "t_dve", 6)

                I3 = ident[:, :].unsqueeze(1).broadcast_to([128, 3, 128])
                m3 = lambda m: m[:, :].unsqueeze(1).broadcast_to([128, 3, 128])
                adds = {"U1": (cUb, cUa), "UT1": (cUTb, cUTa), "U2": (cUa, cUb), "UT2": (cUTa, cUTb), "U3": (cUb, cUa), "UT3": (cUTb, cUTa),
                        "U4": (cUa, cUb), "UT4": (cUTa, cUTb), "U5": (cUb, cUa)}
                masks = {"MT": (cN, before), "PT": (cNT, upto), "QT": (cQT, upto)}
                dve.wait_ge(s["c_pool"], 1)
                for c in range(NCH):
                    for name, e in ROUNDS:
                        if e != "dve":
                            continue
                        for hf in range(2):
                            dve.wait_ge(s["c_ps"], c_ps_at(c, name, hf))
                            b = ps[2 * (ORDER.index(name) % 4) + hf][:, 0:384].rearrange("p (q n) -> p q n", q=3)
                            pp = slice(3 * hf, 3 * hf + 3)
                            tt = lambda o, a, b_, op: dve.tensor_tensor(o[:, pp, :], a, b_, op)
                            if name == "N":
                                link(tt(cN, b, m3(mlow), ALU.mult))
                                tt(cN1, b, m3(moff1), ALU.mult)
                                tt(cN2, b, m3(moff2), ALU.mult)
                                last = tt(cUTa, cN[:, pp, :], I3, ALU.add)
                            elif name == "NT":
                                link(tt(cNT, b, m3(mup), ALU.mult))
                                last = tt(cUa, cNT[:, pp, :], I3, ALU.add)
                            elif name in masks:
                                o, m = masks[name]
                                last = tt(o, b, m3(m), ALU.mult)
                            elif name == "Z":
                                link(tt(cZ, b, cZ[:, pp, :], ALU.add))
                                last = tt(cZ, cZ[:, pp, :], lam[:, pp, c:c + 1].broadcast_to([128, 3, 128]), ALU.mult)
                            else:
                                o, a = adds[name]
                                last = tt(o, b, a[:, pp, :], ALU.add)
                            mark(last, "c_dve", c_at(c, name, hf))
                dve.wait_ge(s["dec_in"], 32)
                row = lambda v: Dv[:, v, :].unsqueeze(1).broadcast_to([96, 64, 64])
                col = lambda a: a.unsqueeze(2).broadcast_to([96, 64, 64])
                link(dve.tensor_tensor(Dt, DS, row(3), ALU.mult))
                link(dve.tensor_reduce(Dsa, Dt, AXX, ALU.add))
                link(dve.tensor_tensor(DS, DS, row(5), ALU.mult))
                link(dve.tensor_tensor(Dt, row(4), col(Dsa), ALU.mult))
                link(dve.tensor_tensor(DS, DS, Dt, ALU.subtract))
                link(dve.tensor_tensor(Dt, row(1), col(Dv[:, 2, :]), ALU.mult))
                mark(dve.tensor_tensor(DS, DS, Dt, ALU.add), "dec_sum", 1)
                link(dve.tensor_tensor(Dt, DS, row(0), ALU.mult))
                mark(dve.tensor_reduce(Dy, Dt, AXX, ALU.add), "dec_sum", 2)
                dve.wait_ge(s["sum_ps"], 3)
                dve.wait_ge(s["dec_y"], 16)
                for q in range(PAIRS):
                    link(dve.scalar_tensor_tensor(out=T0[:, q, :], in0=ps[2 + q][:, 0:T], scalar=-1.0 / 64, in1=vL[:, q, :], op0=ALU.mult, op1=ALU.add))
                mark(dve.memset(sq[:, 0:1], 0.0), "t_dve", 7)
                mark(dve.tensor_tensor(T1, T0, T0, ALU.mult), "t_dve", 8)
                dve.wait_ge(s["t_act"], 6)
                link(dve.tensor_tensor(T0, T0, T1, ALU.mult))
                link(dve.tensor_tensor(T0, T0, vec(V_LG), ALU.mult))
                link(dve.tensor_tensor(T0, T0, vec(V_LB), ALU.add))
                link(dve.tensor_tensor(T0, T0, vld, ALU.add))
                mark(dve.tensor_tensor(mixedT[:, 0:PAIRS, :], T0, vg, ALU.mult), "t_dve", 9)

            def mixer1():
                g96 = lambda a: a[0:96]
                n = tiles_through(CHUNKS[0] + 7) + 5
                dve.wait_ge(s["pj_out"], n)
                mark(dve.scalar_tensor_tensor(out=g96(ge), in0=g96(gl), scalar=-1.0, in1=g96(gl), op0=ALU.mult, op1=ALU.max), "t_dve", 10)
                link(dve.tensor_scalar(g96(gl), g96(gl), 0.0, None, ALU.min))
                dve.wait_ge(s["t_act"], 7)
                link(dve.tensor_tensor(g96(gl), g96(gl), g96(ge), ALU.subtract))
                mark(dve.tensor_scalar(g96(gl), g96(gl), 1.0 / 16, None, ALU.mult), "t_dve", 11)
                for i in range(4):
                    for c in range(NCH):
                        cc = slice(C * c, C * (c + 1))
                        last = dve.tensor_tensor_scan(ge[0:96, i, cc], ones[0:96, 0:C], gl[0:96, i, cc], 0.0, ALU.mult, ALU.add)
                link(last)
                gep = ge[0:96, :, 0:TP]
                dve.tensor_copy(gem[0:96, :].rearrange("p (i c) -> p i c", i=4), ge[0:96, :, C // 2 - 1:TP:C])
                link(dve.tensor_copy(gee[0:96, :].rearrange("p (i c) -> p i c", i=4), ge[0:96, :, C - 1:TP:C]))
                g0, g1 = go[0:96, 0:4, 0:TP], go[0:96, 4:8, 0:TP]
                ic = lambda a: a.unsqueeze(2).broadcast_to([96, NCH, C])
                for i in range(4):
                    v4 = lambda a: a[:, i, :].rearrange("p (c n) -> p c n", c=NCH)
                    dve.tensor_tensor(v4(g1), ic(gee[0:96, NCH * i:NCH * (i + 1)]), v4(gep), ALU.subtract)
                    last = dve.tensor_tensor(v4(g0), v4(gep), ic(gem[0:96, NCH * i:NCH * (i + 1)]), ALU.subtract)
                mark(last, "t_dve", 12)
                dve.wait_ge(s["t_act"], 9)
                link(dve.tensor_tensor(gkh[0:96, :, 0:TP], gkh[0:96, :, 0:TP], gk[0:96, :, 0:TP], ALU.mult))
                mark(dve.memset(sq[:, 0:1], 0.0), "t_dve", 13)
                dve.wait_ge(s["t_act"], 10)
                link(dve.tensor_tensor(gq[0:96, :, 0:TP], gq[0:96, :, 0:TP], gl[0:96, :, 0:TP], ALU.mult))
                link(dve.tensor_tensor(gk[0:96, :, 0:TP], gk[0:96, :, 0:TP], g1, ALU.mult))
                dve.memset(gZ[0:96], 0.0)
                mark(dve.memset(gZm[0:96], 0.0), "t_dve", 14)
                dve.wait_ge(s["dec_in"], 48)
                for b in range(TS):
                    mark(dve.tensor_tensor(gS[0:96, b], gS[0:96, b], gkh[0:96, :, TP + b:TP + b + 1].broadcast_to([96, 4, 192]), ALU.mult), "dec_mul", b + 1)
                    if b > 0:
                        state_add(b - 1)
                state_add(TS - 1)
                mark(dve.memset(sq[:, 0:1], 0.0), "dec_sum", 3)
                cp = 2 * len(ROUNDS) * NCH
                for c in range(NCH):
                    dve.wait_ge(s["c_ps"], cp + 4 * c + 2)
                    mark(dve.tensor_tensor(gatt[0:C], ps[5][0:C, 0:4 * C].rearrange("p (i t) -> p i t", i=4),
                                           upto[0:C, 0:C].unsqueeze(1).broadcast_to([C, 4, C]), ALU.mult), "c_dve", C_TOTAL + 2 * c + 1)
                    dve.wait_ge(s["c_ps"], cp + 4 * c + 4)
                    for i in range(4):
                        link(dve.scalar_tensor_tensor(out=gZ[0:96, i, :], in0=gZ[0:96, i, :], scalar=gee[0:96, NCH * i + c:NCH * i + c + 1],
                                                      in1=ps[7 if i < 2 else 5][0:96, 192 * (i % 2):192 * (i % 2 + 1)], op0=ALU.mult, op1=ALU.add))
                        if c < NCH - 1:
                            link(dve.tensor_scalar(gZm[0:96, i, :], gZ[0:96, i, :], gem[0:96, NCH * i + c + 1:NCH * i + c + 2], None, ALU.mult))
                    mark(dve.memset(sq[:, 0:1], 0.0), "c_dve", C_TOTAL + 2 * c + 2)
                dve.wait_ge(s["c_act"], C_ACT + 2 * NCH)
                dve.wait_ge(s["sat_out"], 3)
                mark(dve.tensor_tensor(gv[0:96], go[0:96], go[0:96], ALU.mult), "t_dve", 15)
                dve.wait_ge(s["t_act"], 11)
                o4 = go[0:96].rearrange("p (i u) t -> p i u t", u=2)
                for i in range(4):
                    for u in range(2):
                        last = dve.scalar_tensor_tensor(out=o4[:, i, u, :], in0=o4[:, i, u, :], scalar=vecT[0:96, 4 + u:5 + u], in1=ge[0:96, i, :], op0=ALU.mult, op1=ALU.mult)
                link(last)
                dve.wait_ge(s["t_act"], 12)
                link(dve.tensor_scalar(gv[0:96], gv[0:96], 1.0, None, ALU.add))
                link(dve.reciprocal(gv[0:96], gv[0:96]))
                link(dve.tensor_tensor(grt[0:96], grt[0:96], gv[0:96], ALU.mult))
                mark(dve.tensor_tensor(mixedT[0:96, 0:8, :], go[0:96], grt[0:96], ALU.mult), "t_dve", 16)

            def state_add(b):
                dve.wait_ge(s["qb_ps"], 3 + b)
                for i in range(4):
                    last = dve.scalar_tensor_tensor(out=gS[0:96, b, i, :], in0=ps[2 + 2 * (b % 2) + i // 2][0:96, 192 * (i % 2):192 * (i % 2 + 1)],
                                                    scalar=gk[0:96, i, TP + b:TP + b + 1], in1=gS[0:96, b, i, :], op0=ALU.mult, op1=ALU.add)
                link(last)

            def add_rows(gate):
                for t, (_, m) in enumerate(TILES):
                    last = dve.scalar_tensor_tensor(out=x[0:m, t, :], in0=yg[0:m, t, :], scalar=gate(t, m), in1=x[0:m, t, :],
                                                    op0=ALU.mult, op1=ALU.add)
                return last

            dve.wait_ge(s["consts"], 1)
            setup()
            for l in range(DEPTH):
                if l == 1:
                    dve.wait_ge(s["vecT_ps"], 3)
                    mark(dve.tensor_copy(vecT[0:96, 0:6], ps[7][0:96, 0:6]), "vecT", 2)
                attention(l)
                (mixer0, mixer1)[l]()
                output(l)
                norm(2 * l + 2, h)
                route(l)
                link(dve.memset(an, 0.0))
                split_h()
                base, gb = NE * l, (NE + 1) * l
                onehot(0, 0, 0, s["m_G"])
                onehot(1, 0, 1, s["m_G"])
                xs_low(gb, 0, s["m_xh"], s["m_xs"])

                def low_units(i, j, units):
                    for u in units:
                        dve.wait_ge(s["m_wh"], UNITS * (base + 2 * i + j) + u + 1)
                        dve.tensor_tensor(low_of(j, u), unit_of(j, u), ring[(UNITS * j + u) % RING].bitcast(F32), ALU.subtract).then_inc(s["m_wl"], 1)

                def pair(i, final=False):
                    for j in range(2):
                        it, g = base + 2 * i + j, gb + 2 * i + j
                        ahead = not (final and j == 1)
                        nxt = (i, 1) if j == 0 else (i + 1, 0)
                        sum_rows(gate, 2, it, s["m_glo"], s["m_g"])
                        sum_rows(upp, 3, it, s["m_ulo"], s["m_u"])
                        low_units(i, j, (9,))
                        swiglu((s["m_tanh"], it), (s["m_u"], it), (s["m_q"], it), s["m_act"])
                        low_units(i, j, (10,))
                        xs_low(g + 1, 1 - j, s["m_xh"], s["m_xs"])
                        actT_low(it, s["m_ah"], s["m_actT"])
                        low_units(i, j, (11,))
                        if ahead:
                            low_units(*nxt, range(0, 4))
                            onehot(2 * i + j + 2, 0, j, s["m_G"])
                            low_units(*nxt, range(4, 6))
                        nat_out(2 * it, j, s["m_ylo"], s["m_nat"])
                        if ahead:
                            low_units(*nxt, range(6, 9))

                low_units(0, 0, range(0, 9))
                pair(0)
                with dve.Fori(1, NE // 2 - 1) as i:
                    pair(i)
                pair(NE // 2 - 1, final=True)
                dve.wait_ge(s["flag"], l + 1)
                more = dve.value_load(flag_i[0:1, 0:1], min_val=0, max_val=1)
                r = lambda n: s[f"r_{n}{l}"]
                with dve.If(more > 0):
                    dve.wait_ge(s["m_xg_ps"], (NE + 1) * (l + 1))
                    for j in range(2):
                        dve.wait_ge(s[f"m_ywr{j}"], 8 * NE * (l + 1))
                    with dve.Fori(0, NE) as e:
                        for b in range(STEPS_REST):
                            it = STEPS_REST * e + b
                            onehot(e, b + 1, b % 2, r("dve"))
                            at = lambda name: rest_at(it, name)
                            xs_low(at("xs_high"), b % 2, r("act"), r("dve"))
                            sum_rows(gate, 2, at("gate_low"), r("act"), r("dve"))
                            sum_rows(upp, 3, at("up_low"), r("act"), r("dve"))
                            swiglu((r("act"), at("tanh")), (r("dve"), at("up")), (r("dve"), at("q")), r("dve"))
                            actT_low(at("actT_high"), r("act"), r("dve"))
                            nat_out(at("y_low0"), b % 2, r("act"), r("dve"))
                            dve.wait_ge(s[f"ryw{'ab'[b % 2]}{l}"], 16 * (STEPS_REST // 2 * e + b // 2 + 1))
                    for k in range(2):
                        dve.wait_ge(s[f"rgath{l}"], 48 * (k + 1))
                        add_rows(lambda t, m: gr[0:m, 2 * t + k:2 * t + k + 1]).then_inc(s[f"rcomb{l}"], 1)
                        dve.wait_ge(s[f"rcomb{l}"], k + 1)
                with dve.Else():
                    dve.nop()
                for k in range(2):
                    dve.wait_ge(s["gathered"], 96 * l + 48 * (k + 1))
                    add_rows(lambda t, m: gt[0:m, t, 6 + k:7 + k]).then_inc(s["combined"], 1)
                    dve.wait_ge(s["combined"], 2 * l + k + 1)
            norm(5, h)


_OUTS = [("y_prompt", (1, 256, 1024)), ("y_sample", (8, 1, 1024)), ("prompt_rwkv_S", (1, 1, 12, 64, 64)), ("prompt_rwkv_shift", (1, 1, 1024)),
         ("prompt_gla_S", (1, 1, 4, 96, 192)), ("prompt_mem_k", (2, 1, 256, 4, 64)), ("prompt_mem_v", (2, 1, 256, 4, 64)),
         ("sample_rwkv_S", (1, 8, 12, 64, 64)), ("sample_rwkv_shift", (1, 8, 1024)), ("sample_gla_S", (1, 8, 4, 96, 192))]


def kernel(**inputs):
    import concourse.bacc as _bacc
    from concourse.bass_utils import run_bass_kernel_spmd as _run

    nc = _bacc.Bacc("TRN2", target_bir_lowering=False, num_devices=1)
    arrays, A, O = {}, {}, {}
    for name, v in inputs.items():
        a = np.ascontiguousarray(v)
        arrays[f"in_{name}"] = a
        A[name] = nc.dram_tensor(f"in_{name}", a.shape, mybir.dt.from_np(a.dtype), kind="ExternalInput").ap()
    for name, shape in _OUTS:
        O[name] = nc.dram_tensor(f"out_{name}", shape, F32, kind="ExternalOutput").ap()
    build(nc, A, O)
    r = _run(nc, [arrays], core_ids=[0])
    return tuple(r.results[0][f"out_{name}"] for name, _ in _OUTS)
```

```python
from contextlib import ExitStack

import numpy as np
import concourse.bass as bass
from concourse import mybir

ALU = mybir.AluOpType
ACT = mybir.ActivationFunctionType
F32 = mybir.dt.float32
F32R = mybir.dt.float32r
BF16 = mybir.dt.bfloat16
I32 = mybir.dt.int32
U32 = mybir.dt.uint32
AXX = mybir.AxisListType.X

D = 1024
KT = D // 128
TP = 256
TS = 8
T = TP + TS
TOK = 768
MEMW = 256
N_MEM = 256
C = 64
NCH = TP // C
PAIRS = TOK // 128
TILES = [(0, 128), (128, 128), (256, TS)]
DEPTH = 2
NE = 32
GROUPS = 4
FF = 512
CAP = 64
SLOT = D // 128 * D + FF // 128 * D
UNITS = D // 128 + FF // 128
UNITS_UP = D // 128
RING = 8
STEPS_REST = 4
RROWS = CAP * STEPS_REST
EPS = 1e-6
GN_EPS = 64e-5
LN2 = 0.6931471805599453
BIG = 1e30

W_IN = [[(2304, 256), (768, 512), (1280, 256), (0, 512), (512, 256), (1536, 512), (2048, 256)],
        [(2304, 256)] + [(384 * n, 384) for n in range(6)]]
W_OUT = [[(0, 512), (512, 512)], [(256 * n, 256) for n in range(4)]]
TILE_W = [128, 96]
LORA_TILES = [{2: 3, 4: 3 * PAIRS}, {2: 1, 3: 4}]
CHUNKS = [1 + len(W_IN[l]) + len(W_OUT[l]) for l in range(2)]


def tiles_through(g):
    total, n = 0, 0
    for l in range(DEPTH):
        parts = [2, 2] + [w // TILE_W[l] for _, w in W_IN[l][1:]] + [w // 128 for _, w in W_OUT[l]]
        for i, m in enumerate(parts):
            total += LORA_TILES[l].get(i, 0)
            total += m
            if n == g:
                return total
            n += 1


ROUNDS = [("N", "dve"), ("NT", "dve"), ("Bn", "act"), ("Kn", "act"), ("Vn", "act"), ("X2", "act"), ("X2T", "act"),
          ("MT", "dve"), ("U1", "dve"), ("UT1", "dve"), ("X4", "act"), ("X4T", "act"), ("PT", "dve"), ("U2", "dve"),
          ("UT2", "dve"), ("X8T", "act"), ("QT", "dve"), ("U3", "dve"), ("UT3", "dve"), ("W1", "act"), ("U4", "dve"),
          ("UT4", "dve"), ("W2", "act"), ("U5", "dve"), ("RHS", "act"), ("SA", "act"), ("Y", "act"), ("Z", "dve")]
ORDER = [n for n, _ in ROUNDS]


def c_ps_at(c, name, half):
    return 2 * (len(ROUNDS) * c + ORDER.index(name)) + half + 1


def c_at(c, name, half):
    mine = [n for n, e in ROUNDS if e == dict(ROUNDS)[name]]
    return 2 * (len(mine) * c + mine.index(name)) + half + 1


C_TOTAL = 2 * NCH * sum(e == "dve" for _, e in ROUNDS)
C_ACT = 2 * NCH * sum(e == "act" for _, e in ROUNDS)
T_SCALED = 6
T_STATE_OUT = 4
REST = {"pe": ("xg", "up", "actT_ps", "down"), "act": ("xs_high", "gate_low", "up_low", "tanh", "actT_high", "y_low0", "y_low1"),
        "dve": ("G", "xs", "gate", "up", "q", "act", "actT", "nat")}


def rest_at(it, name):
    steps = next(v for v in REST.values() if name in v)
    return len(steps) * it + steps.index(name)


T_MIXED = [9, 16]
OUT_STORES = [2, 4]
SEMS = """consts x_loaded norm_ss norm_rs norm_h hT_ps hT gain_loaded router_w
logit_ps logits gate_e gates rank_ps ranks flagT_ps flag
wupa0 wupa1 wupb0 wupb1 wdn0 wdn1 m_wh m_wl m_used m_G m_xg_ps m_xh m_xs m_glo m_ulo m_g m_u m_tanh m_q m_act m_actT_ps m_ah
m_actT m_ylo m_nat h_parts m_ywr0 m_ywr1
rgath0 rgath1 rcomb0 rcomb1 rw0 r_pe0 r_act0 r_dve0 rywa0 rywb0
rw1 r_pe1 r_act1 r_dve1 rywa1 rywb1
gathered combined stored out_stored
vec_in vecT_ps vecT lora_in chunk_in0 chunk_in1 chunk_in2 pj_ps pj_out shift_stored
mm_in mm_ss mm_rs mm_h mm_T_ps mm_T kv_stored
kT_ps kT sc_ps sc_max sc_exp sc_prob pT_ps pT at_ps at_out
cache_k cache_v qn_ps qn qb_ps s_score sT_ps s_max s_exp s_prob spT_ps spT sat_ps sat_out
shift_in shiftT_ps xj lora_s t_dve t_act sum_ps c_ps c_dve c_act c_pool c_zero oT_ps o_x dec_out gath1 gla_in
dec_scr0 dec_scr1 dec_in dec_mul dec_sum dec_y x_out act_chain dve_chain pool_chain""".split()


def build(nc, A, O):
    with ExitStack() as ctx:
        s = {n: ctx.enter_context(nc.semaphore(n)) for n in SEMS}

        def sb(name, cols, dt=F32, rows=128):
            return ctx.enter_context(nc.sbuf_tensor(name, [rows, cols], dt))

        WIDTHS = {"slot0": SLOT, "slot1": SLOT, "h": 3 * D, "hT": KT * T, "gain": D, "mixedT": (KT + 2) * T, "arena": 13600}
        with ExitStack() as names:
            split = {n: names.enter_context(nc.sbuf_tensor(f"{n}_split", [128, w], F32R)) for n, w in WIDTHS.items()}
        over = {n: sb(n, w) for n, w in WIDTHS.items()}
        slot = [over["slot0"], over["slot1"]]
        wup = [t[:, 0:8192].rearrange("p (k n) -> p k n", k=KT) for t in slot[::-1]]
        wdn = [t[:, 8192:12288].rearrange("p (k n) -> p k n", k=FF // 128) for t in slot[::-1]]
        x = sb("x", 3 * D)[:, :].rearrange("p (t d) -> p t d", t=3)
        h = over["h"][:, :].rearrange("p (t d) -> p t d", t=3)
        hT = over["hT"][:, :].rearrange("p (k t) -> p k t", k=KT)
        gain = over["gain"]
        ident = sb("ident", 128)
        before = sb("before", 128)
        ones = sb("ones", 128)
        iota_rank = sb("iota_rank", CAP + RROWS)
        iota_e = sb("iota_e", NE)
        iota_g = sb("iota_g", NE)
        valid = sb("valid", 3)
        cst = sb("cst", 8)
        vecT = sb("vecT", 90)
        mlow = sb("mlow", 128)
        mup = sb("mup", 128)
        moff1 = sb("moff1", 128)
        moff2 = sb("moff2", 128)
        upto = sb("upto", 128)
        block64 = sb("block64", 128)
        sel = sb("sel", TS * 128, rows=TS)[:, :].rearrange("k (b n) -> k b n", b=TS)
        mixedT = over["mixedT"][:, :].rearrange("p (k t) -> p k t", t=T)
        nvec = sb("nvec", 12)
        arena = over["arena"]
        pos = [0]

        def carve_split(n):
            a = split["arena"][:, pos[0]:pos[0] + n]
            pos[0] += n
            return a

        def carve(n):
            a = arena[:, pos[0]:pos[0] + n]
            pos[0] += n
            return a

        sq = carve(D)
        st = carve(16)
        mm_st = arena[:, 1024 + 8:1024 + 16]
        wr = carve(KT * 36).rearrange("p (k n) -> p k n", k=KT)
        br = carve(36)
        lg = carve(3 * 36).rearrange("p (t n) -> p t n", t=3)
        g8 = carve(3 * 8).rearrange("p (t n) -> p t n", t=3)
        m8 = carve(3 * 8).rearrange("p (t n) -> p t n", t=3)
        i8 = carve(3 * 8).rearrange("p (t n) -> p t n", t=3)
        i8f = carve(3 * 8).rearrange("p (t n) -> p t n", t=3)
        em = carve(3 * NE).rearrange("p (t n) -> p t n", t=3)
        tmp32 = carve(3 * NE).rearrange("p (t n) -> p t n", t=3)
        a1 = carve(3 * NE).rearrange("p (t n) -> p t n", t=3)
        a2 = carve(3 * NE).rearrange("p (t n) -> p t n", t=3)
        asum = carve(3 * NE).rearrange("p (t n) -> p t n", t=3)
        rank = carve(3 * NE).rearrange("p (t n) -> p t n", t=3)
        R = carve(3 * (NE + 2)).rearrange("p (t n) -> p t n", t=3)
        gt = carve(3 * 8).rearrange("p (t n) -> p t n", t=3)
        rowf = carve(6)
        rowi = carve(6)
        flagf = carve(4)
        bf = lambda n: carve(n // 2).bitcast(BF16)
        hp = [bf(3 * D).rearrange("p (t d) -> p t d", t=3) for _ in range(3)]
        G = [bf(3 * CAP).rearrange("p (t n) -> p t n", t=3) for _ in range(2)]
        xs = [carve_split(KT * 2 * CAP).rearrange("p (k v n) -> p k v n", k=KT, v=2) for _ in range(2)]
        actT = carve_split(4 * 2 * CAP).rearrange("p (f v n) -> p f v n", f=4, v=2)
        gate, ex = sq[:, 0:FF], sq[:, FF:D]
        upp = carve(FF)
        an = carve(FF)
        ynat = [carve(D) for _ in range(2)]
        ring = [split[n][:, D * i:D * (i + 1)] for n, i in (("mixedT", 0), ("mixedT", 1), ("gain", 0), ("h", 0), ("h", 1), ("h", 2), ("hT", 0), ("hT", 1))]
        assert UNITS * 2 % RING == 0 and len(ring) == RING
        yg = [h, slot[1][:, 0:3 * D].rearrange("p (t d) -> p t d", t=3)]
        rows_i = sb("rows_i", 6, I32)
        rows_r = sb("rows_r", 6, I32)
        in_rest = sb("in_rest", 6)
        gr = sb("gr", 6)
        flag_i = sb("flag_i", 2, I32)
        idx_u = sb("idx_u", 3 * 8, U32)[:, :].rearrange("p (t n) -> p t n", t=3)
        ps = [ctx.enter_context(nc.psum_tensor(f"bank{i}", [128, 512], F32)) for i in range(8)]
        wch = [slot[0][:, 4096 * n:4096 * (n + 1)] for n in range(3)]

        class Area:
            def __init__(self, ap, at=0):
                self.ap, self.at = ap, at

            def take(self, n):
                self.at += n
                return self.ap[:, self.at - n:self.at]
        k3 = lambda a, k: a.rearrange("p (k t) -> p k t", k=k)
        AR = 1040
        vraw = arena[:, AR:AR + 128]
        a_ = Area(arena, AR + 128)
        mem = k3(a_.take(2 * D), 2)
        gmem = a_.take(D)
        memT = k3(a_.take(KT * N_MEM), KT)
        kvn = k3(a_.take(2 * 2 * MEMW), 2)
        kT = k3(a_.take(2 * N_MEM), 2)
        qT = k3(a_.take(2 * T), 2)
        qs = a_.take(MEMW)
        smx = a_.take(8)
        snx = a_.take(8)
        ssm = a_.take(8)
        srs = a_.take(8)
        sc_s = a_.take(64)
        sp_s = a_.take(N_MEM)
        spT = a_.take(64)
        b_ = Area(slot[1])
        KC = b_.take(4096).rearrange("p (m b n) -> p m b n", m=2, b=TS)
        VC = b_.take(4096).rearrange("p (m b n) -> p m b n", m=2, b=TS)
        P = b_.take(8 * N_MEM).rearrange("p (h t m) -> p h t m", h=4, t=2)
        PT = b_.take(4 * 2 * TP).rearrange("p (h m t) -> p h m t", h=4, m=2)
        a_ = Area(arena, AR + 128)
        Q = [k3(a_.take(PAIRS * T), PAIRS) for _ in range(5)]
        lw1, la1, lg1 = k3(a_.take(512), KT), k3(a_.take(512), KT), k3(a_.take(1024), KT)
        lw2, la2, lg2 = a_.take(TOK), a_.take(TOK), a_.take(TOK)
        lora_at = a_.at - (512 + 512 + 1024 + 3 * TOK)
        w1o, a1o, g1o = mixedT[:, 0, :], mixedT[:, 1, :], mixedT[:, 2, :]
        assert a_.at <= 13600, a_.at
        b_ = Area(slot[1])
        Q += [k3(b_.take(PAIRS * T), PAIRS) for _ in range(3)]
        t_at = b_.at
        TT = [k3(b_.take(KT * T), KT) for _ in range(3)]
        shn = b_.take(D)
        vr, vk, vv, vb, vkk, vL, vg, vld = Q
        b_ = Area(slot[1], t_at)
        c_ = Area(arena, lora_at)
        h_ = Area(h.rearrange("p t d -> p (t d)"))
        t_ = Area(hT.rearrange("p k t -> p (k t)"))
        cAT, cBT, cKT, cRT = (k3(h_.take(768), PAIRS) for _ in range(4))
        cX4, cX4T = (k3(t_.take(768), PAIRS) for _ in range(2))
        cN, cN1, cN2, cNT, cX2, cX2T, cBn, cKn, cVn = (k3(b_.take(768), PAIRS) for _ in range(9))
        cUa, cUb, cUTa, cUTb, cQT = (k3(c_.take(768), PAIRS) for _ in range(5))
        cZ = k3(gain[:, 0:768], PAIRS)
        lam = sb("lam", PAIRS * NCH)[:, :].rearrange("p (q c) -> p q c", c=NCH)
        DS = wch[1][0:96, :].rearrange("p (i j) -> p i j", i=64)
        Dt = wch[2][0:96, :].rearrange("p (i j) -> p i j", i=64)
        Dv = arena[0:96, 512:896].rearrange("p (v j) -> p v j", v=6)
        Dsa, Dy = arena[0:96, 896:960], arena[0:96, 960:1024]
        Dn = [mixedT.rearrange("p k t -> p (k t)")[0:TS, TOK * n:TOK * (n + 1)] for n in range(2)]
        dscr = nc.dram_tensor("sample_vectors", [6, TS * TOK], F32, kind="Internal").ap()
        yscr = nc.dram_tensor("sample_y", [TS * TOK], F32, kind="Internal").ap()
        a_ = Area(arena, AR + 128)
        b_ = Area(slot[1])
        gq, gk = k3(a_.take(4 * T), 4), k3(a_.take(4 * T), 4)
        gv, grt = k3(a_.take(8 * T), 8), k3(a_.take(8 * T), 8)
        gl, ge = k3(a_.take(4 * T), 4), k3(a_.take(4 * T), 4)
        gkh = k3(a_.take(4 * T), 4)
        ga1, ga2, ga1o = k3(a_.take(128), KT), a_.take(384), a_.take(T)
        assert a_.at <= 13600, a_.at
        gS = b_.take(TS * TOK).rearrange("p (b h e) -> p b h e", b=TS, h=4)
        go = k3(b_.take(8 * T), 8)
        gsl = k3(a_.take(8 * T), 8)
        assert a_.at <= 13600, a_.at
        gZ = k3(b_.take(TOK), 4)
        gZm = k3(b_.take(TOK), 4)
        gvn = b_.take(TOK)
        gkn = b_.take(384)
        gatt = k3(b_.take(4 * C), 4)
        gem = b_.take(4 * NCH)
        gee = b_.take(4 * NCH)
        gvs = b_.take(TOK)
        assert b_.at <= 12288, b_.at
        wo_tiles = [[(k, 128 * k, 128) for k in range(KT)],
                    [(k, 96 * k, 96) for k in range(8)] + [(8 + k, TOK + 128 * k, 128) for k in range(2)]]

        oT = [arena[:, AR + 128 + T * n:AR + 128 + T * (n + 1)] for n in range(2)]
        rows_first = [nc.dram_tensor(f"rows_first{l}", [NE * CAP, D], F32, kind="Internal").ap() for l in range(DEPTH)]
        rows_rest = [nc.dram_tensor(f"rows_rest{l}", [NE * RROWS, D], F32, kind="Internal").ap() for l in range(DEPTH)]

        def unit_of(j, u):
            return wup[j][:, u, :] if u < UNITS_UP else wdn[j][:, u - UNITS_UP, :]

        def low_of(j, u):
            return split[f"slot{1 - j}"][:, D * u:D * (u + 1)]

        block = ctx.enter_context(nc.Block())

        def chain(eng, sem):
            n = [0]

            def link(ins):
                n[0] += 1
                ins.then_inc(sem, 1)
                eng.wait_ge(sem, n[0])
            return link

        def load_up(sp, e, sl, l, sems):
            for u, sem in enumerate(sems):
                load_up_half(sp, e, sl, l, u, sem)

        def load_up_half(sp, e, sl, l, u, sem):
            rows = slice(u * D // 2, (u + 1) * D // 2)
            sp.dma_start(wup[sl][:, u * KT // 2:(u + 1) * KT // 2, :],
                         A["exp_w_up"][l, bass.ds(e, 1), rows].rearrange("e (k p) n -> p (e k) n", p=128)).then_inc(sem, 16)

        def load_down(sp, e, sl, l, sem):
            sp.dma_start(wdn[sl], A["exp_w_down"][l, bass.ds(e, 1)].rearrange("e (k p) n -> p (e k) n", p=128)).then_inc(sem, 16)

        @block.sync
        def _(sp):
            sp.dma_start(x[:, 0:2, :], A["x_prompt"][0].rearrange("(t p) d -> p t d", p=128)).then_inc(s["x_loaded"], 16)
            sp.dma_start(x[0:TS, 2, :], A["x_sample"].rearrange("b q d -> (b q) d")).then_inc(s["x_loaded"], 16)
            sp.dma_start(vraw[0:48, :], A["rw_mu"][0].rearrange("j (k c) -> (j k) c", c=128)).then_inc(s["vec_in"], 16)
            for n, name in enumerate(("rw_w0", "rw_a0", "rw_k_k", "rw_k_a", "rw_r_k", "rw_ln_g", "rw_ln_b")):
                v = A[name][0].rearrange("(k c) -> k c", c=128) if name != "rw_r_k" else A[name][0].rearrange("(k u) c -> k (u c)", u=2)
                sp.dma_start(vraw[48 + 6 * n:54 + 6 * n, :], v).then_inc(s["vec_in"], 16)
            chunk = 0

            def load_chunk(dst, src):
                nonlocal chunk
                if chunk >= 3:
                    sp.wait_ge(s["pj_ps"], tiles_through(chunk - 3))
                for d, a in zip(dst(wch[chunk % 3]), src):
                    sp.dma_start(d, a).then_inc(s[f"chunk_in{chunk % 3}"], 16)
                chunk += 1

            for l in range(DEPTH):
                if l == 0:
                    sp.dma_start(gain[:, :], A["norm_mix_g"][0:1, :].broadcast_to([128, D])).then_inc(s["gain_loaded"], 16)
                else:
                    sp.wait_ge(s["m_used"], UNITS * NE)
                    sp.dma_start(gain[:, :], A["norm_mix_g"][1:2, :].broadcast_to([128, D])).then_inc(s["gain_loaded"], 16)
                    sp.wait_ge(s["combined"], 2)
                    sp.dma_start(vraw[0:4, 0:96], A["gla_ab"][0].rearrange("(k c) -> k c", c=96)).then_inc(s["vec_in"], 16)
                    sp.dma_start(vraw[4:6, 0:96], A["gla_norm_g"][0].rearrange("(k c) -> k c", c=96)).then_inc(s["vec_in"], 16)
                sp.dma_start(mem, A["mem_prompt"][0].rearrange("(m p) d -> p m d", p=128)).then_inc(s["mm_in"], 16)
                sp.dma_start(gmem, A["norm_mem_g"][l:l + 1, :].broadcast_to([128, D])).then_inc(s["mm_in"], 16)
                load_chunk(lambda b: [k3(b, KT)], [A["w_mem_kv"][l].rearrange("(k p) n -> p k n", p=128)])
                if l == 0:
                    sp.dma_start(lw1, A["rw_w1"][0].rearrange("(k p) n -> p k n", p=128)).then_inc(s["lora_in"], 16)
                    sp.dma_start(la1, A["rw_a1"][0].rearrange("(k p) n -> p k n", p=128)).then_inc(s["lora_in"], 16)
                    sp.dma_start(lg1, A["rw_g1"][0].rearrange("(k p) n -> p k n", p=128)).then_inc(s["lora_in"], 16)
                    sp.dma_start(lw2[0:64, :], A["rw_w2"][0]).then_inc(s["lora_in"], 16)
                    sp.dma_start(la2[0:64, :], A["rw_a2"][0]).then_inc(s["lora_in"], 16)
                    sp.dma_start(lg2, A["rw_g2"][0]).then_inc(s["lora_in"], 16)
                else:
                    sp.dma_start(ga1, A["gla_a1"][0].rearrange("(k p) n -> p k n", p=128)).then_inc(s["lora_in"], 16)
                    sp.dma_start(ga2[0:16, :], A["gla_a2"][0]).then_inc(s["lora_in"], 16)
                for m in range(2):
                    sp.dma_start(KC[:, m], A["cache_mem_k"][l].rearrange("b (m p) h d -> m p b (h d)", p=128)[m]).then_inc(s["cache_k"], 16)
                    sp.dma_start(VC[:, m], A["cache_mem_v"][l].rearrange("b (m p) h d -> m p b (h d)", p=128)[m]).then_inc(s["cache_v"], 16)
                for c0, w in W_IN[l]:
                    load_chunk(lambda b: [k3(b[:, 0:KT * w], KT)], [A["w_in"][l].rearrange("(k p) n -> p k n", p=128)[:, :, c0:c0 + w]])
                if l == 0:
                    sp.wait_ge(s["pj_ps"], tiles_through(7))
                    for n in range(2):
                        sp.wait_ge(s[f"dec_scr{n}"], 48)
                    sp.dma_start(DS.rearrange("p i j -> p (i j)"), A["state_rwkv_S"][0].rearrange("b h i j -> (b h) (i j)")).then_inc(s["dec_in"], 16)
                    sp.dma_start(Dv, dscr.rearrange("v (p j) -> p v j", j=64)).then_inc(s["dec_in"], 16)
                    sp.wait_ge(s["dec_sum"], 3)
                    sp.dma_start(O["sample_rwkv_S"][0].rearrange("b h i j -> (b h) (i j)"), DS.rearrange("p i j -> p (i j)")).then_inc(s["dec_out"], 16)
                    sp.wait_ge(s["dec_sum"], 4)
                    sp.dma_start(yscr.rearrange("(p i) -> p i", i=64), Dy).then_inc(s["dec_y"], 16)
                    sp.wait_ge(s["dec_y"], 16)
                    sp.dma_start(Dn[0], yscr.rearrange("(b c) -> b c", b=TS)).then_inc(s["dec_y"], 16)
                for c0, w in W_OUT[l]:
                    if l == 0:
                        load_chunk(lambda b: [k3(b[:, 0:KT * w], KT)], [A["w_out"][l].rearrange("(k p) n -> p k n", p=128)[:, :, c0:c0 + w]])
                    else:
                        load_chunk(lambda b: [k3(b[0:96, 0:8 * w], 8), k3(b[:, 8 * w:10 * w], 2)],
                                   [A["w_out"][l][0:TOK, c0:c0 + w].rearrange("(k p) n -> p k n", p=96),
                                    A["w_out"][l][TOK:D, c0:c0 + w].rearrange("(k p) n -> p k n", p=128)])
                sp.wait_ge(s["t_dve"], T_MIXED[l])
                sp.wait_ge(s["out_stored"], 16 * OUT_STORES[l])
                load_up(sp, 0, 0, l, (s["wupa0"], s["wupb0"]))
                load_down(sp, 0, 0, l, s["wdn0"])
                sp.wait_ge(s["x_out"], l + 1)
                sp.dma_start(wr[:, :, 0:4], A["router_wg"][l].rearrange("(k p) n -> p k n", p=128)).then_inc(s["router_w"], 16)
                sp.dma_start(wr[:, :, 4:36], A["router_we"][l].rearrange("(k p) n -> p k n", p=128)).then_inc(s["router_w"], 16)
                sp.dma_start(br[:, 0:4], A["router_bg"][l:l + 1, :].broadcast_to([128, 4])).then_inc(s["router_w"], 16)
                sp.dma_start(br[:, 4:36], A["router_be"][l:l + 1, :].broadcast_to([128, 32])).then_inc(s["router_w"], 16)
                sp.dma_start(gain[:, :], A["norm_ffn_g"][l:l + 1, :].broadcast_to([128, D])).then_inc(s["gain_loaded"], 16)
                sp.wait_ge(s["dec_out"], 16)
                load_up(sp, 1, 1, l, (s["wupa1"], s["wupb1"]))
                load_down(sp, 1, 1, l, s["wdn1"])
                with sp.Fori(1, NE // 2) as i:
                    for j in range(2):
                        used = UNITS * (NE * l + 2 * i + j - 2)
                        for u in range(2):
                            sp.wait_ge(s["m_used"], used + (u + 1) * KT // 2)
                            load_up_half(sp, 2 * i + j, j, l, u, s[f"wup{'ab'[u]}{j}"])
                        sp.wait_ge(s["m_used"], used + UNITS)
                        load_down(sp, 2 * i + j, j, l, s[f"wdn{j}"])
                sp.wait_ge(s["flag"], l + 1)
                more = sp.value_load(flag_i[0:1, 0:1], min_val=0, max_val=1)
                with sp.If(more > 0):
                    sp.wait_ge(s["m_used"], UNITS * NE * (l + 1))
                    load_up(sp, 0, 0, l, (s[f"rw{l}"],) * 2)
                    load_down(sp, 0, 0, l, s[f"rw{l}"])
                    with sp.Fori(1, NE) as e:
                        sp.wait_ge(s[f"r_pe{l}"], len(REST["pe"]) * STEPS_REST * e)
                        load_up(sp, e, 0, l, (s[f"rw{l}"],) * 2)
                        load_down(sp, e, 0, l, s[f"rw{l}"])
                with sp.Else():
                    sp.nop()
            sp.wait_ge(s["m_used"], 2 * UNITS * NE)
            sp.dma_start(gain[:, :], A["norm_final_g"].rearrange("(a d) -> a d", a=1).broadcast_to([128, D])).then_inc(s["gain_loaded"], 16)
            sp.wait_ge(s["norm_h"], 15)
            sp.dma_start(O["y_prompt"][0].rearrange("(t p) d -> p t d", p=128), h[:, 0:2, :]).then_inc(s["stored"], 16)
            sp.dma_start(O["y_sample"].rearrange("b q d -> (b q) d"), h[0:TS, 2, :]).then_inc(s["stored"], 16)
            sp.wait_ge(s["stored"], 32)
            sp.wait_ge(s["kv_stored"], 64)
            sp.wait_ge(s["shift_stored"], 32)

        @block.gpsimd
        def _(pool):
            link = chain(pool, s["pool_chain"])
            link(pool.memset(ident[:, :], 0.0))
            link(pool.affine_select(out=ident[:, :], in_=ident[:, :], compare_op=ALU.not_equal, fill=1.0, base=0,
                                    pattern=[[-1, 128]], channel_multiplier=1))
            pool.memset(ones[:, :], 1.0)
            link(pool.memset(before[:, :], 1.0))
            link(pool.affine_select(out=before[:, :], in_=before[:, :], compare_op=ALU.is_gt, fill=0.0, base=0,
                                    pattern=[[1, 128]], channel_multiplier=-1))
            pool.iota(iota_rank[:, :], pattern=[[1, CAP + RROWS]], base=0, channel_multiplier=0, allow_small_or_imprecise_dtypes=True)
            pool.iota(iota_e[:, :], pattern=[[1, NE]], base=0, channel_multiplier=0, allow_small_or_imprecise_dtypes=True)
            pool.iota(iota_g[:, :], pattern=[[1, GROUPS], [0, NE // GROUPS]], base=0, channel_multiplier=0, allow_small_or_imprecise_dtypes=True)
            pool.memset(cst[:, 0:1], EPS)
            link(pool.memset(valid[:, :], 1.0))
            link(pool.affine_select(out=valid[:, 2:3], in_=valid[:, 2:3], compare_op=ALU.is_gt, fill=0.0, base=TS,
                                    pattern=[[0, 1]], channel_multiplier=-1))
            link(pool.memset(upto[:, :], 1.0))
            link(pool.affine_select(out=upto[:, :], in_=upto[:, :], compare_op=ALU.is_ge, fill=0.0, base=0,
                                    pattern=[[1, 128]], channel_multiplier=-1))
            pool.iota(mlow[:, :], pattern=[[1, 8], [0, 16]], base=0, channel_multiplier=0, allow_small_or_imprecise_dtypes=True)
            pool.iota(moff1[:, :], pattern=[[1, 4], [0, 32]], base=0, channel_multiplier=0, allow_small_or_imprecise_dtypes=True)
            pool.iota(moff2[:, :], pattern=[[1, 2], [0, 64]], base=0, channel_multiplier=0, allow_small_or_imprecise_dtypes=True)
            for b in range(TS):
                link(pool.tensor_copy(sel[:, b, :], ident[0:TS, b:b + 1].broadcast_to([TS, 128])))
            pool.memset(cst[:, 2:3], GN_EPS)
            pool.memset(cst[:, 3:4], 16 * LN2)
            pool.memset(cst[:, 1:2], 0.0).then_inc(s["consts"], 1)

            pool.wait_ge(s["consts"], 1)

            def mixer0():
                pool.wait_ge(s["norm_h"], 3)
                pool.dma_start(O["prompt_rwkv_shift"][0], h[127:128, 1, :]).then_inc(s["shift_stored"], 16)
                pool.dma_start(O["sample_rwkv_shift"][0], h[0:TS, 2, :]).then_inc(s["shift_stored"], 16)
                store_kv(0)
                pool.wait_ge(s["at_ps"], 1)
                pool.dma_start(shn[0:TS, :], A["state_rwkv_shift"][0]).then_inc(s["shift_in"], 16)
                for n in range(6):
                    pool.wait_ge(s["qn"], n + 2)
                    pool.dma_start(dscr[n].rearrange("(b c) -> b c", b=TS), Dn[n % 2]).then_inc(s[f"dec_scr{n % 2}"], 16)
                pool.wait_ge(s["shift_stored"], 32)
                pool.wait_ge(s["hT"], KT)
                for m in (cAT, cBT, cKT, cRT, cZ):
                    last = pool.memset(m, 0.0)
                last.then_inc(s["c_zero"], 1)
                pool.wait_ge(s["xj"], 6)
                pool.memset(cX4, 0.0).then_inc(s["c_zero"], 1)
                pool.wait_ge(s["c_zero"], 2)
                pool.wait_ge(s["t_dve"], T_SCALED)
                for c in range(1, NCH):
                    for dst, src, used in ((cBT, vb, "PT"), (cKT, vk, "QT"), (cX4, vv, "U5"), (cAT, vkk, "RHS"), (cRT, vr, "Y")):
                        pool.wait_ge(s["c_ps"], c_ps_at(c - 1, used, 1))
                        for u in range(2):
                            rows = slice(64 * u, 64 * u + 64)
                            last = pool.tensor_copy(dst[rows, :, 64 * u:64 * u + 64], src[rows, :, C * c:C * (c + 1)])
                        last.then_inc(s["c_pool"], 1)
                pool.wait_ge(s["t_act"], T_STATE_OUT)
                for u in range(2):
                    pool.dma_start(O["prompt_rwkv_S"][0, 0].rearrange("(q u) i j -> u i q j", u=2)[u], cKn[64 * u:64 * u + 64, :, 64 * u:64 * u + 64]).then_inc(s["out_stored"], 16)

            def mixer1():
                pool.wait_ge(s["combined"], 2)
                pool.wait_ge(s["sat_out"], 2)
                pool.dma_start(gS[0:96, :, :, :].rearrange("p b h e -> p (b h) e"), A["state_gla_S"][0].rearrange("b h d e -> d (b h) e")).then_inc(s["gla_in"], 16)
                store_kv(1)
                pool.wait_ge(s["dec_sum"], 5)
                pool.dma_start(O["sample_gla_S"][0].rearrange("b h d e -> d (b h) e"), gS[0:96, :, :, :].rearrange("p b h e -> p (b h) e")).then_inc(s["out_stored"], 16)
                pool.wait_ge(s["c_dve"], C_TOTAL + 2 * NCH)
                pool.dma_start(O["prompt_gla_S"][0, 0].rearrange("h d e -> d h e"), gZ[0:96]).then_inc(s["out_stored"], 16)

            def store_kv(l):
                pool.wait_ge(s["pj_out"], 2 + (tiles_through(CHUNKS[0] - 1) if l else 0))
                pool.dma_start(O["prompt_mem_k"][l, 0].rearrange("(m p) h d -> p m (h d)", p=128), kvn[:, :, 0:MEMW]).then_inc(s["kv_stored"], 16)
                pool.dma_start(O["prompt_mem_v"][l, 0].rearrange("(m p) h d -> p m (h d)", p=128), kvn[:, :, MEMW:2 * MEMW]).then_inc(s["kv_stored"], 16)

            def write_rows(dst, row, n, par, s_nat, s_wr):
                pool.wait_ge(s_nat, n + 1)
                pool.dma_start(dst[bass.ds(row, CAP), :], ynat[par][0:CAP, :]).then_inc(s_wr, 16)

            def gather_rows(src, index, k, s_done, buf):
                for t, (_, n) in enumerate(TILES):
                    pool.indirect_dma_start(buf[0:n, t, :], None, src, bass.IndirectOffsetOnAxis(ap=index[0:n, 2 * t + k:2 * t + k + 1], axis=0)).then_inc(s_done, 16)

            for l in range(DEPTH):
                (mixer0, mixer1)[l]()
                with pool.Fori(0, NE // 2) as i:
                    for j in range(2):
                        write_rows(rows_first[l], (2 * i + j) * CAP, NE * l + 2 * i + j, j, s["m_nat"], s[f"m_ywr{j}"])
                pool.wait_ge(s["flag"], l + 1)
                more = pool.value_load(flag_i[0:1, 0:1], min_val=0, max_val=1)
                with pool.If(more > 0):
                    with pool.Fori(0, NE) as e:
                        for b in range(STEPS_REST):
                            write_rows(rows_rest[l], e * RROWS + CAP * b, rest_at(STEPS_REST * e + b, "nat"), b % 2, s[f"r_dve{l}"], s[f"ryw{'ab'[b % 2]}{l}"])
                    pool.wait_ge(s[f"rywa{l}"], 8 * STEPS_REST * NE)
                    pool.wait_ge(s[f"rywb{l}"], 8 * STEPS_REST * NE)
                    for k in range(2):
                        if k == 1 or l == 1:
                            pool.wait_ge(s["combined"], 2 * l)
                            pool.wait_ge(s[f"rcomb{l}"], k)
                        gather_rows(rows_rest[l], rows_r, k, s[f"rgath{l}"], yg[0])
                    pool.wait_ge(s[f"rcomb{l}"], 2)
                with pool.Else():
                    pool.nop()
                for j in range(2):
                    pool.wait_ge(s[f"m_ywr{j}"], 8 * NE * (l + 1))
                for k in range(2):
                    gather_rows(rows_first[l], rows_i, k, s[("gathered", "gath1")[k]], yg[k])

        NEEDS = {"X2": ("NT",), "X2T": ("NT",), "U1": ("X2T", "NT"), "UT1": ("X2T", "NT"), "X4": ("X2T",), "X4T": ("X2T",),
                 "U2": ("X4T", "UT1"), "UT2": ("X4T", "UT1"), "X8T": ("X4T",), "U3": ("X8T", "UT2"), "UT3": ("X8T", "UT2"),
                 "W1": ("U3",), "U4": ("W1", "UT3"), "UT4": ("W1", "UT3"), "W2": ("U4",), "U5": ("W2", "UT4"),
                 "RHS": ("Vn", "MT"), "SA": ("RHS", "U5"), "Y": ("SA", "QT"), "Z": ("SA",)}

        @block.tensor
        def _(pe):
            def transpose_h(n):
                pe.wait_ge(s["norm_h"], 3 * n)
                pe.wait_ge(s["pj_out"], tn[0])
                for k in range(KT):
                    if 8 * (n - 1) + k >= 2:
                        pe.wait_ge(s["hT"], 8 * (n - 1) + k - 1)
                    for t, (c, m) in enumerate(TILES):
                        last = pe.transpose(ps[k % 2][:, c:c + m], h[0:m, t, k * 128:(k + 1) * 128], ident[0:m, 0:m])
                    last.then_inc(s["hT_ps"], 1)

            tn = [0]

            def bank():
                if tn[0] >= 2:
                    pe.wait_ge(s["pj_out"], tn[0] - 1)
                return ps[tn[0] % 2]

            def tile_done(last):
                tn[0] += 1
                last.then_inc(s["pj_ps"], 1)

            wc = [0]

            def chunk_in(n_dmas=1):
                g = wc[0]
                wc[0] += 1
                b = g % 3
                got[b] += 16 * n_dmas
                pe.wait_ge(s[f"chunk_in{b}"], got[b])
                return wch[b]
            got = [0, 0, 0]

            def product(w, m, rhs, kt=KT, rows=128, n=T):
                p = bank()
                for k in range(kt):
                    last = pe.matmul(p[0:m, 0:n], w(k), rhs(k), start=(k == 0), stop=(k == kt - 1))
                tile_done(last)

            def attention(l):
                for k in range(KT):
                    pe.wait_ge(s["mm_h"], 2 * (l + 1))
                    if k >= 2:
                        pe.wait_ge(s["mm_T"], KT * l + k - 1)
                    for m in range(2):
                        last = pe.transpose(ps[2 + k % 2][:, 128 * m:128 * (m + 1)], mem[:, m, k * 128:(k + 1) * 128], ident[:, :])
                    last.then_inc(s["mm_T_ps"], 1)
                pe.wait_ge(s["mm_T"], KT * (l + 1))
                w = k3(chunk_in(), KT)
                for m in range(2):
                    product(lambda k: memT[:, k, 128 * m:128 * (m + 1)], 128, lambda k: w[:, k, :], n=2 * MEMW)
                pe.wait_ge(s["pj_out"], tn[0])
                for hp in range(2):
                    for m in range(2):
                        last = pe.transpose(ps[2][:, 256 * hp + 128 * m:256 * hp + 128 * (m + 1)], kvn[:, m, 128 * hp:128 * (hp + 1)], ident[:, :])
                last.then_inc(s["kT_ps"], 1)
                transpose_h(2 * l + 1)
                pe.wait_ge(s["hT"], KT * (2 * l + 1))
                w = k3(chunk_in()[:, 0:KT * 256], KT)
                for q in range(2):
                    product(lambda k: w[:, k, 128 * q:128 * (q + 1)], 128, lambda k: hT[:, k, :])
                pe.wait_ge(s["pj_out"], tn[0])
                pe.wait_ge(s["kT"], l + 1)
                pe.wait_ge(s["vecT"], l + 1)
                for hd in range(4):
                    rows = slice(64 * (hd % 2), 64 * (hd % 2) + 64)
                    for t in range(2):
                        last = pe.matmul(ps[4 + hd][:, 256 * t:256 * (t + 1)], qT[rows, hd // 2, 128 * t:128 * (t + 1)], kT[rows, hd // 2, :],
                                         start=True, stop=True)
                    last.then_inc(s["sc_ps"], 1)
                for q in range(2):
                    last = pe.transpose(ps[3][0:TS, 128 * q:128 * (q + 1)], qT[:, q, TP:T], ident[:, :])
                last.then_inc(s["qn_ps"], 1)
                for hd in range(4):
                    pe.wait_ge(s["sc_prob"], 4 * l + hd + 1)
                    for m in range(2):
                        for t in range(2):
                            last = pe.transpose(ps[4 + hd][:, 256 * m + 128 * t:256 * m + 128 * (t + 1)], P[:, hd, t, 128 * m:128 * (m + 1)], ident[:, :])
                    last.then_inc(s["pT_ps"], 1)
                for hd in range(4):
                    pe.wait_ge(s["pT"], 4 * l + hd + 1)
                    rows = slice(64 * (hd % 2), 64 * (hd % 2) + 64)
                    for m in range(2):
                        last = pe.matmul(ps[2][rows, 256 * (hd // 2):256 * (hd // 2 + 1)], kvn[:, m, MEMW + 64 * hd:MEMW + 64 * (hd + 1)], PT[:, hd, m, :],
                                         start=(m == 0), stop=(m == 1))
                last.then_inc(s["at_ps"], 1)
                pe.wait_ge(s["qn"], l * 7 + 1)
                for b in range(TS):
                    last = pe.matmul(ps[4 + b // 2][:, 256 * (b % 2):256 * (b % 2 + 1)], sel[:, b, :], qs[0:TS, :], start=True, stop=True)
                last.then_inc(s["qb_ps"], 1)
                pe.wait_ge(s["s_score"], l + 1)
                for m in range(2):
                    last = pe.transpose(ps[3][0:32, 128 * m:128 * (m + 1)], sc_s[:, 32 * m:32 * (m + 1)], ident[:, :])
                last.then_inc(s["sT_ps"], 1)
                pe.wait_ge(s["s_prob"], l + 1)
                for m in range(2):
                    last = pe.transpose(ps[3][:, 32 * m:32 * (m + 1)], sp_s[0:32, 128 * m:128 * (m + 1)], ident[0:32, 0:32])
                last.then_inc(s["spT_ps"], 1)
                pe.wait_ge(s["spT"], l + 1)
                pe.wait_ge(s["cache_v"], 32 * (l + 1))
                pe.wait_ge(s["at_out"], l + 1)
                for hp in range(2):
                    for b in range(TS):
                        for m in range(2):
                            last = pe.matmul(ps[2][:, 32 * hp + 4 * b:32 * hp + 4 * b + 4], VC[:, m, b, 128 * hp:128 * (hp + 1)],
                                             spT[:, 32 * m + 4 * b:32 * m + 4 * b + 4], start=(m == 0), stop=(m == 1))
                last.then_inc(s["sat_ps"], 1)

            def output(l):
                def transposed(n):
                    pe.wait_ge(s["pj_out"], tn[0] - (0 if n == KT - 1 else 1))
                    if KT * l + n >= 2:
                        pe.wait_ge(s["o_x"], KT * l + n - 1)
                    for t, (c, m) in enumerate(TILES):
                        last = pe.transpose(ps[2 + n % 2][0:m, 128 * t:128 * (t + 1)], oT[n % 2][:, c:c + m], ident[:, :])
                    last.then_inc(s["oT_ps"], 1)

                n = 0
                for c0, w in W_OUT[l]:
                    buf = chunk_in(1 + l)
                    for b in range(w // 128):
                        p = bank()
                        for i, _, rows in wo_tiles[l]:
                            last = pe.matmul(p[:, 0:T], buf[0:rows, w * i + 128 * b:w * i + 128 * (b + 1)], mixedT[0:rows, i, :],
                                             start=(i == 0), stop=(i == len(wo_tiles[l]) - 1))
                        tile_done(last)
                        if n > 0:
                            transposed(n - 1)
                        n += 1
                transposed(KT - 1)

            def head_sums(src, n):
                for q in range(PAIRS):
                    last = pe.matmul(ps[2 + q][:, 0:T], block64[:, :], src[:, q, :], start=True, stop=True)
                last.then_inc(s["sum_ps"], 1)

            def mixer0():
                pe.wait_ge(s["shift_in"], 16)
                pe.wait_ge(s["sat_out"], 1)
                for k in range(KT):
                    last = pe.transpose(ps[7][:, TS * k:TS * (k + 1)], shn[0:TS, 128 * k:128 * (k + 1)], ident[0:TS, 0:TS])
                last.then_inc(s["shiftT_ps"], 1)
                def columns(xi, chunks):
                    pe.wait_ge(s["xj"], xi + 1)
                    for w in chunks:
                        buf = k3(chunk_in()[:, 0:KT * w], KT)
                        for i in range(w // 128):
                            product(lambda k: buf[:, k, 128 * i:128 * (i + 1)], 128, lambda k: TT[1 + xi % 2][:, k, :])

                pe.wait_ge(s["lora_in"], 96)
                for xi, (w, m) in enumerate(((lw1, 64), (la1, 64), (lg1, 128))):
                    pe.wait_ge(s["xj"], xi + 1)
                    product(lambda k: w[:, k, :], m, lambda k: TT[1 + xi % 2][:, k, :])
                base = tn[0]
                columns(3, (512, 256))
                pe.wait_ge(s["lora_s"], 1)
                for q in range(PAIRS):
                    product(lambda k: lw2[0:64, 128 * q:128 * (q + 1)], 128, lambda k: w1o[0:64, :], kt=1)
                pe.wait_ge(s["pj_out"], base - 1)
                for q in range(PAIRS):
                    product(lambda k: la2[0:64, 128 * q:128 * (q + 1)], 128, lambda k: a1o[0:64, :], kt=1)
                pe.wait_ge(s["lora_s"], 2)
                for q in range(PAIRS):
                    product(lambda k: lg2[:, 128 * q:128 * (q + 1)], 128, lambda k: g1o, kt=1)
                pe.wait_ge(s["t_dve"], 1)
                head_sums(vL, 1)
                columns(4, (512, 256))
                columns(5, (512, 256))
                pe.wait_ge(s["t_dve"], 3)
                head_sums(TT[0], 2)
                pe.wait_ge(s["pj_out"], tn[0])
                for n, src in enumerate((vr, vk, vv, vkk, vb, TT[2])):
                    if n == 5:
                        pe.wait_ge(s["t_act"], 2)
                    if n >= 1:
                        pe.wait_ge(s["qn"], n + 1)
                    for q in range(PAIRS):
                        last = pe.transpose(ps[q // 3][0:TS, 128 * (q % 3):128 * (q % 3 + 1)], src[:, q, TP:T], ident[:, :])
                    last.then_inc(s["qn_ps"], 1)

                def group(c, name, *mms, tr=False):
                    n = ORDER.index(name)
                    for hf in range(2):
                        for o in NEEDS.get(name, ()):
                            pe.wait_ge(s["c_" + dict(ROUNDS)[o]], c_at(c, o, hf))
                        g = len(ROUNDS) * c + n - 4
                        if g >= 0:
                            cc, nm = g // len(ROUNDS), ORDER[g % len(ROUNDS)]
                            pe.wait_ge(s["c_" + dict(ROUNDS)[nm]], c_at(cc, nm, hf))
                        b = ps[2 * (n % 4) + hf]
                        for q in range(3):
                            out = b[:, 128 * q:128 * (q + 1)]
                            for i, (lt, rh) in enumerate(mms):
                                if tr:
                                    last = pe.transpose(out, lt[:, 3 * hf + q, :], ident[:, :])
                                else:
                                    last = pe.matmul(out, lt[:, 3 * hf + q, :], rh[:, 3 * hf + q, :], start=(i == 0), stop=(i == len(mms) - 1))
                        last.then_inc(s["c_ps"], 1)

                assert len(ROUNDS) % 4 == 0
                for c in range(NCH):
                    pe.wait_ge(s["c_pool"], 5 * c + 4)
                    if c == 0:
                        pe.wait_ge(s["pj_out"], tn[0])
                        pe.wait_ge(s["qn"], 7)
                        pe.wait_ge(s["t_dve"], T_SCALED)
                    group(c, "N", (cAT, cBT))
                    group(c, "NT", (cBT, cAT))
                    group(c, "Bn", (cBT, None), tr=True)
                    group(c, "Kn", (cKT, None), tr=True)
                    group(c, "Vn", (cX4, None), tr=True)
                    group(c, "X2", (cN, cNT))
                    group(c, "X2T", (cNT, cN))
                    group(c, "MT", (cKT, cAT))
                    group(c, "U1", (cX2T, cUa))
                    group(c, "UT1", (cUa, cX2T))
                    group(c, "X4", (cX2T, cX2))
                    group(c, "X4T", (cX2, cX2T))
                    pe.wait_ge(s["c_pool"], 5 * (c + 1))
                    group(c, "PT", (cBT, cRT))
                    group(c, "U2", (cX4T, cUb))
                    group(c, "UT2", (cUb, cX4T))
                    group(c, "X8T", (cX4, cX4T))
                    group(c, "QT", (cKT, cRT))
                    group(c, "U3", (cX2T, cUa))
                    group(c, "UT3", (cUa, cX2T))
                    group(c, "W1", (cN1, cUb))
                    group(c, "U4", (cUTb, cX2))
                    group(c, "UT4", (cX2, cUTb))
                    group(c, "W2", (cN2, cUa))
                    group(c, "U5", (cUTa, cX4))
                    if c == 0:
                        pe.wait_ge(s["c_pool"], 1)
                    else:
                        for hf in range(2):
                            pe.wait_ge(s["c_dve"], c_at(c - 1, "Z", hf))
                    group(c, "RHS", (cAT, cZ), (cN, cVn))
                    group(c, "SA", (cUb, cX4T))
                    group(c, "Y", (cZ, cRT), (cX2T, cNT), (cVn, cQT))
                    group(c, "Z", (cBn, cX2T), (cKn, cVn))
                for hf in range(2):
                    pe.wait_ge(s["c_dve"], c_at(NCH - 1, "Z", hf))
                    pe.wait_ge(s["c_act"], c_at(NCH - 1, "Y", hf))
                for q in range(PAIRS):
                    last = pe.transpose(ps[2 + q // 3][:, 128 * (q % 3):128 * (q % 3 + 1)], cZ[:, q, :], ident[:, :])
                last.then_inc(s["qn_ps"], 1)
                pe.wait_ge(s["dec_y"], 32)
                for q in range(PAIRS):
                    last = pe.transpose(ps[4][:, TS * q:TS * (q + 1)], Dn[0][:, 128 * q:128 * (q + 1)], ident[0:TS, 0:TS])
                last.then_inc(s["qn_ps"], 1)
                pe.wait_ge(s["t_act"], T_STATE_OUT)
                pe.wait_ge(s["t_act"], 5)
                head_sums(vL, 3)
                pe.wait_ge(s["t_dve"], 8)
                head_sums(TT[1], 4)
                pe.wait_ge(s["t_dve"], 9)

            def mixer1():
                def columns(w):
                    buf = k3(chunk_in()[:, 0:KT * w], KT)
                    for i in range(w // 96):
                        product(lambda k: buf[:, k, 96 * i:96 * (i + 1)], 96, lambda k: hT[:, k, :])

                pe.wait_ge(s["lora_in"], 128)
                product(lambda k: ga1[:, k, :], 16, lambda k: hT[:, k, :])
                base = tn[0]
                columns(W_IN[1][1][1])
                pe.wait_ge(s["pj_out"], base)
                for i in range(4):
                    product(lambda k: ga2[0:16, 96 * i:96 * (i + 1)], 96, lambda k: ga1o[0:16, :], kt=1)
                for _, w in W_IN[1][2:]:
                    columns(w)
                pe.wait_ge(s["pj_out"], tn[0])
                for i in range(8):
                    last = pe.transpose(ps[2 + i // 4][0:TS, 96 * (i % 4):96 * (i % 4 + 1)], gv[0:96, i, TP:T], ident[0:96, 0:96])
                last.then_inc(s["qn_ps"], 1)
                pe.wait_ge(s["qn"], 9)
                for b in range(TS):
                    pe.wait_ge(s["dec_mul"], b + 1)
                    for u in range(2):
                        last = pe.matmul(ps[2 + 2 * (b % 2) + u][0:96, 0:384], sel[:, b, 0:96], gvs[0:TS, 384 * u:384 * (u + 1)], start=True, stop=True)
                    last.then_inc(s["qb_ps"], 1)
                pe.wait_ge(s["dec_sum"], 5)
                for b in range(TS):
                    for i in range(8):
                        last = pe.matmul(ps[6][0:96, TS * i + b:TS * i + b + 1], gS[0:96, b, i // 2, 96 * (i % 2):96 * (i % 2 + 1)],
                                         gq[0:96, i // 2, TP + b:TP + b + 1], start=True, stop=True)
                last.then_inc(s["sat_ps"], 1)
                pe.wait_ge(s["t_dve"], 14)
                for c in range(NCH):
                    cc = slice(C * c, C * (c + 1))
                    if c > 0:
                        pe.wait_ge(s["c_act"], C_ACT + 2 * c)
                    for i in range(8):
                        pe.transpose(ps[2 + i // 4][0:C, 96 * (i % 4):96 * (i % 4 + 1)], gv[0:96, i, cc], ident[0:96, 0:96])
                    for i in range(4):
                        last = pe.transpose(ps[4][0:C, 96 * i:96 * (i + 1)], gkh[0:96, i, cc], ident[0:96, 0:96])
                    last.then_inc(s["c_ps"], 1)
                    if c > 0:
                        pe.wait_ge(s["c_dve"], C_TOTAL + 2 * c)
                    for i in range(4):
                        last = pe.matmul(ps[5][0:C, C * i:C * (i + 1)], gk[0:96, i, cc], gq[0:96, i, cc], start=True, stop=True)
                    last.then_inc(s["c_ps"], 1)
                    pe.wait_ge(s["c_act"], C_ACT + 2 * c + 1)
                    pe.wait_ge(s["c_dve"], C_TOTAL + 2 * c + 1)
                    for i in range(8):
                        o = ps[6][0:96, C * i:C * (i + 1)]
                        pe.matmul(o, gvn[0:C, 96 * i:96 * (i + 1)], gatt[0:C, i // 2, :], start=True, stop=False)
                        last = pe.matmul(o, gZm[0:96, i // 2, 96 * (i % 2):96 * (i % 2 + 1)], gq[0:96, i // 2, cc], start=False, stop=True)
                    last.then_inc(s["c_ps"], 1)
                    for i in range(4):
                        last = pe.matmul(ps[7 if i < 2 else 5][0:96, 192 * (i % 2):192 * (i % 2 + 1)], gkn[0:C, 96 * i:96 * (i + 1)], gvn[0:C, 192 * i:192 * (i + 1)],
                                         start=True, stop=True)
                    last.then_inc(s["c_ps"], 1)
                pe.wait_ge(s["t_dve"], 15)
                for i in range(4):
                    for u in range(2):
                        last = pe.matmul(ps[2 + i][0:96, 0:T], ones[0:96, 0:96], gv[0:96, 2 * i + u, :], start=(u == 0), stop=(u == 1))
                last.then_inc(s["sum_ps"], 1)
                pe.wait_ge(s["t_dve"], 16)

            def gather(par, ks, s_done=None):
                for k in ks:
                    n = 0
                    for t, (_, m) in enumerate(TILES):
                        for part in hp:
                            last = pe.matmul(ps[par][:, k * CAP:(k + 1) * CAP], part[0:m, t, k * 128:(k + 1) * 128], G[par][0:m, t, :],
                                             start=(n == 0), stop=(n == 8))
                            n += 1
                if s_done is not None:
                    last.then_inc(s_done, 1)

            def unit(j, u, it):
                pe.wait_ge(s["m_wl"], UNITS * it + u + 1)
                if u < UNITS_UP:
                    lhs, bank0, first, last_ = xs[j][:, u], 2, u == 0, u == UNITS_UP - 1
                else:
                    f = u - UNITS_UP
                    lhs, bank0, first, last_ = actT[:, f], 6, f == 0, f == FF // 128 - 1
                lhs = lhs.rearrange("p v n -> p (v n)")
                for half in range(2):
                    cols = slice(half * FF, (half + 1) * FF)
                    pe.matmul(ps[bank0 + half][:, :], lhs, ring[(UNITS * j + u) % RING][:, cols], start=first, stop=False)
                    last = pe.matmul(ps[bank0 + half][:, :], lhs, low_of(j, u)[:, cols], start=False, stop=last_)
                last.then_inc(s["m_used"], 1)

            def act_T(s_done):
                for f in range(4):
                    last = pe.transpose(ps[5][:, f * 128:(f + 1) * 128], an[:, f * 128:(f + 1) * 128], ident[:, :])
                last.then_inc(s_done, 1)

            def whole(lhs, w, bank0, s_done):
                n = lhs.shape[1]
                for half in range(2):
                    for k in range(n):
                        last = pe.matmul(ps[bank0 + half][:, :], lhs[:, k].rearrange("p v n -> p (v n)").bitcast(F32), w[:, k, half * FF:(half + 1) * FF],
                                         start=(k == 0), stop=(k == n - 1))
                last.then_inc(s_done, 1)

            pe.wait_ge(s["consts"], 1)
            pe.wait_ge(s["vec_in"], 16 * 8)
            pe.transpose(ps[7][:, 0:90], vraw[0:90, :], ident[0:90, 0:90]).then_inc(s["vecT_ps"], 1)
            for n, m in enumerate((mlow, moff1, moff2)):
                last = pe.transpose(ps[6][:, 128 * n:128 * (n + 1)], m[:, :], ident[:, :])
            last.then_inc(s["vecT_ps"], 1)
            for l in range(DEPTH):
                if l == 1:
                    pe.wait_ge(s["vec_in"], 16 * 10)
                    pe.transpose(ps[7][0:96, 0:6], vraw[0:6, 0:96], ident[0:6, 0:6]).then_inc(s["vecT_ps"], 1)
                attention(l)
                (mixer0, mixer1)[l]()
                output(l)
                transpose_h(2 * l + 2)
                pe.wait_ge(s["hT"], 8 * (2 * l + 2))
                pe.wait_ge(s["router_w"], 64 * (l + 1))
                for t, (c, m) in enumerate(TILES):
                    for k in range(KT):
                        last = pe.matmul(ps[2][0:m, t * 36:(t + 1) * 36], hT[:, k, c:c + m], wr[:, k, :], start=(k == 0), stop=(k == KT - 1))
                last.then_inc(s["logit_ps"], 1)
                pe.wait_ge(s["gates"], l + 1)
                for t, (c, m) in enumerate(TILES):
                    for u in range(t + 1):
                        mu = TILES[u][1]
                        last = pe.matmul(ps[3][:, t * NE:(t + 1) * NE], (before if u == t else ones)[0:mu, :], asum[0:mu, u, :],
                                         start=(u == 0), stop=(u == t))
                last.then_inc(s["rank_ps"], 1)
                pe.wait_ge(s["ranks"], l + 1)
                pe.transpose(ps[3][0:1, 256:384], flagf[:, 0:1], ident[:, :]).then_inc(s["flagT_ps"], 1)

                base, gb = NE * l, (NE + 1) * l
                pe.wait_ge(s["h_parts"], l + 1)
                pe.wait_ge(s["m_G"], gb + 1)
                gather(0, range(KT), s["m_xg_ps"])

                def pair(i, first):
                    for j in range(2):
                        it, g = base + 2 * i + j, gb + 2 * i + j
                        start = first and j == 0 and l == 0
                        pe.wait_ge(s["m_xs"], g + 1)
                        if not start:
                            pe.wait_ge(s["m_u"], it)
                        for u in range(UNITS_UP):
                            unit(j, u, it)
                        pe.wait_ge(s["m_G"], g + 2)
                        if not start:
                            pe.wait_ge(s["m_xs"], g)
                        gather(1 - j, range(KT), s["m_xg_ps"])
                        pe.wait_ge(s["m_act"], it + 1)
                        act_T(s["m_actT_ps"])
                        pe.wait_ge(s["m_actT"], it + 1)
                        if not start:
                            pe.wait_ge(s["m_nat"], it)
                        for u in range(UNITS_UP, UNITS):
                            unit(j, u, it)

                pair(0, True)
                with pe.Fori(1, NE // 2) as i:
                    pair(i, False)

                pe.wait_ge(s["flag"], l + 1)
                more = pe.value_load(flag_i[0:1, 0:1], min_val=0, max_val=1)
                r = lambda n: s[f"r_{n}{l}"]
                with pe.If(more > 0):
                    pe.wait_ge(s["m_nat"], NE * (l + 1))
                    pe.wait_ge(s["m_xs"], (NE + 1) * (l + 1))
                    with pe.Fori(0, NE) as e:
                        pe.wait_ge(s[f"rw{l}"], 48 * (e + 1))
                        for b in range(STEPS_REST):
                            it = STEPS_REST * e + b
                            pe.wait_ge(r("dve"), rest_at(it, "G") + 1)
                            gather(b % 2, range(KT), r("pe"))
                            pe.wait_ge(r("dve"), rest_at(it, "xs") + 1)
                            whole(xs[b % 2], wup[0], 2, r("pe"))
                            pe.wait_ge(r("dve"), rest_at(it, "act") + 1)
                            act_T(r("pe"))
                            pe.wait_ge(r("dve"), rest_at(it, "actT") + 1)
                            whole(actT, wdn[0], 6, r("pe"))
                with pe.Else():
                    pe.nop()

        @block.scalar
        def _(act):
            link = chain(act, s["act_chain"])

            def norm_scale(n):
                for t, (_, m) in enumerate(TILES):
                    act.wait_ge(s["norm_ss"], 3 * (n - 1) + t + 1)
                    link(act.activation(st[0:m, 4 + t:5 + t], st[0:m, t:t + 1], ACT.Ln, scale=1.0 / D, bias=cst[0:m, 0:1]))
                    act.activation(st[0:m, 8 + t:9 + t], st[0:m, 4 + t:5 + t], ACT.Exp, scale=-0.5).then_inc(s["norm_rs"], 1)

            def copy_hT(n):
                for k in range(KT):
                    act.wait_ge(s["hT_ps"], 8 * (n - 1) + k + 1)
                    act.copy(hT[:, k, :], ps[k % 2][:, 0:T]).then_inc(s["hT"], 1)

            def xs_high(it, par, s_in, s_done):
                act.wait_ge(s_in, it + 1)
                act.copy(xs[par][:, :, 0, :], ps[par][:, 0:KT * CAP].rearrange("p (k n) -> p k n", k=KT)).then_inc(s_done, 1)

            def low_rows(dst, bank, s_done):
                act.copy(dst[0:CAP, :], ps[bank][CAP:2 * CAP, :]).then_inc(s_done, 1)

            def tanh_gate(n_in, s_in, s_done):
                act.wait_ge(s_in, n_in + 1)
                act.activation(ex[0:CAP, :], gate[0:CAP, :], ACT.Tanh, scale=0.5).then_inc(s_done, 1)

            def actT_high(it, s_in, s_done):
                act.wait_ge(s_in, it + 1)
                act.copy(actT[:, :, 0, :], ps[5][:, :].rearrange("p (f n) -> p f n", f=4)[:, :, 0:CAP]).then_inc(s_done, 1)

            tn = [0]

            def out(dst, m, n=T, func=ACT.Copy, **kw):
                act.wait_ge(s["pj_ps"], tn[0] + 1)
                act.activation(dst, ps[tn[0] % 2][0:m, 0:n], func, **kw).then_inc(s["pj_out"], 1)
                tn[0] += 1

            def attention(l):
                for m in range(2):
                    act.wait_ge(s["mm_ss"], 2 * l + m + 1)
                    link(act.activation(mm_st[:, 2 + m:3 + m], mm_st[:, m:m + 1], ACT.Ln, scale=1.0 / D, bias=cst[:, 0:1]))
                    act.activation(mm_st[:, 4 + m:5 + m], mm_st[:, 2 + m:3 + m], ACT.Exp, scale=-0.5).then_inc(s["mm_rs"], 1)
                norm_scale(2 * l + 1)
                for k in range(KT):
                    act.wait_ge(s["mm_T_ps"], KT * l + k + 1)
                    act.copy(memT[:, k, :], ps[2 + k % 2][:, 0:N_MEM]).then_inc(s["mm_T"], 1)
                for m in range(2):
                    out(kvn[:, m, :], 128, n=2 * MEMW)
                act.wait_ge(s["kT_ps"], l + 1)
                act.copy(kT, ps[2][:, :].rearrange("p (a b) -> p a b", a=2)).then_inc(s["kT"], 1)
                copy_hT(2 * l + 1)
                for q in range(2):
                    out(qT[:, q, :], 128)
                act.wait_ge(s["qn_ps"], 9 * l + 1)
                act.copy(qs[0:TS, :], ps[3][0:TS, 0:MEMW]).then_inc(s["qn"], 1)
                for hd in range(4):
                    act.wait_ge(s["sc_max"], 4 * l + hd + 1)
                    for t in range(2):
                        n = 2 * hd + t
                        last = act.activation(P[:, hd, t, :], ps[4 + hd][:, 256 * t:256 * (t + 1)], ACT.Exp, scale=0.125, bias=snx[:, n:n + 1],
                                              accum_out=ssm[:, n:n + 1])
                    last.then_inc(s["sc_exp"], 1)
                for hd in range(4):
                    act.wait_ge(s["pT_ps"], 4 * l + hd + 1)
                    act.copy(PT[:, hd].rearrange("p m t -> p (m t)"), ps[4 + hd][:, :]).then_inc(s["pT"], 1)
                m0 = KT - 2 if l == 0 else KT
                act.wait_ge(s["at_ps"], l + 1)
                act.copy(mixedT[:, m0:m0 + 2, 0:TP], ps[2][:, :].rearrange("p (a b) -> p a b", a=2)).then_inc(s["at_out"], 1)
                act.wait_ge(s["s_max"], l + 1)
                act.activation(sp_s[0:32, :], ps[3][0:32, 0:N_MEM], ACT.Exp, scale=0.125, bias=snx[0:32, 0:1], accum_out=ssm[0:32, 0:1]).then_inc(s["s_exp"], 1)
                act.wait_ge(s["spT_ps"], l + 1)
                act.copy(spT, ps[3][:, 0:64]).then_inc(s["spT"], 1)
                act.wait_ge(s["sat_ps"], l + 1)
                for hp in range(2):
                    for u in range(2):
                        rows = slice(64 * u, 64 * u + 64)
                        last = act.copy(mixedT[rows, m0 + hp, TP:T], ps[2][rows, 32 * hp + 2 * hp + u:32 * hp + 32:4])
                last.then_inc(s["sat_out"], 1)

            def mixer0():
                act.wait_ge(s["sat_out"], 1)
                act.wait_ge(s["vecT"], 1)
                out(w1o[0:64, :], 64, func=ACT.Exp, scale=-2.0)
                out(a1o[0:64, :], 64)
                out(g1o, 128, func=ACT.Exp, scale=-1.0)
                for q in range(PAIRS):
                    out(vk[:, q, :], 128)
                for q in range(PAIRS):
                    out(vld[:, q, :], 128, func=ACT.Exp, scale=-1.0, bias=nvec[:, q:q + 1])
                for q in range(PAIRS):
                    out(vb[:, q, :], 128, func=ACT.Exp, scale=-1.0, bias=nvec[:, PAIRS + q:PAIRS + q + 1])
                for q in range(PAIRS):
                    out(vg[:, q, :], 128)
                act.wait_ge(s["t_dve"], 2)
                link(act.activation(vL, vL, ACT.Ln, scale=2.0 ** 32))
                act.activation(vL, vL, ACT.Exp, scale=-0.5, bias=cst[:, 3:4]).then_inc(s["t_act"], 1)
                for dst in (vr, vv):
                    for q in range(PAIRS):
                        out(dst[:, q, :], 128)
                act.wait_ge(s["t_dve"], 4)
                act.activation(TT[2][:, 0:PAIRS, TP:T], vld[:, :, TP:T], ACT.Exp)
                act.activation(TT[2][:, 0:PAIRS, 0:TP], TT[2][:, 0:PAIRS, 0:TP], ACT.Exp)
                act.activation(TT[1][:, 0:PAIRS, 0:TP], vL[:, :, 0:TP], ACT.Exp).then_inc(s["t_act"], 1)
                act.wait_ge(s["t_dve"], 5)
                act.activation(TT[0][:, 0:PAIRS, 0:TP], vL[:, :, 0:TP], ACT.Exp, scale=-1.0).then_inc(s["t_act"], 1)
                for n in range(6):
                    act.wait_ge(s["qn_ps"], n + 2)
                    if n >= 2:
                        act.wait_ge(s[f"dec_scr{n % 2}"], 16 * (n // 2))
                    for u in range(2):
                        last = act.copy(Dn[n % 2][:, 384 * u:384 * (u + 1)], ps[u][0:TS, 0:384])
                    last.then_inc(s["qn"], 1)

                dst = {"Bn": cBn, "Kn": cKn, "Vn": cVn, "X2": cX2, "X2T": cX2T, "X4": cX4, "X4T": cX4T, "X8T": cX2T, "W1": cX2, "W2": cX4,
                       "RHS": cX4T, "SA": cX2T}
                act.wait_ge(s["c_zero"], 2)
                act.wait_ge(s["t_dve"], T_SCALED)
                for m, src in ((cBT, vb), (cKT, vk), (cX4, vv), (cAT, vkk), (cRT, vr)):
                    for u in range(2):
                        rows = slice(64 * u, 64 * u + 64)
                        last = act.copy(m[rows, :, 64 * u:64 * u + 64], src[rows, :, 0:C])
                    last.then_inc(s["c_pool"], 1)
                for c in range(NCH):
                    for name, e in ROUNDS:
                        if e != "act":
                            continue
                        for hf in range(2):
                            act.wait_ge(s["c_ps"], c_ps_at(c, name, hf))
                            b = ps[2 * (ORDER.index(name) % 4) + hf]
                            pairs = slice(3 * hf, 3 * hf + 3)
                            if name == "Y":
                                for u in range(2):
                                    rows = slice(64 * u, 64 * u + 64)
                                    last = act.copy(vL[rows, pairs, C * c:C * (c + 1)],
                                                    b[rows, 0:384].rearrange("p (q n) -> p q n", q=3)[:, :, 64 * u:64 * u + 64])
                            else:
                                last = act.copy(dst[name][:, pairs, :], b[:, 0:384].rearrange("p (q n) -> p q n", q=3))
                            last.then_inc(s["c_act"], 1)
                act.wait_ge(s["qn_ps"], 8)
                for u in range(2):
                    last = act.copy(cKn[:, 3 * u:3 * u + 3, :], ps[2 + u][:, 0:384].rearrange("p (q n) -> p q n", q=3))
                last.then_inc(s["t_act"], 1)
                act.wait_ge(s["qn_ps"], 9)
                act.copy(vL[:, :, TP:T], ps[4][:, 0:TS * PAIRS].rearrange("p (q b) -> p q b", q=PAIRS)).then_inc(s["t_act"], 1)
                act.wait_ge(s["sum_ps"], 4)
                for q in range(PAIRS):
                    link(act.activation(TT[1][:, q, :], ps[2 + q][:, 0:T], ACT.Ln, scale=1.0 / 64, bias=cst[:, 2:3]))
                act.activation(TT[1][:, 0:PAIRS, :], TT[1][:, 0:PAIRS, :], ACT.Exp, scale=-0.5).then_inc(s["t_act"], 1)

            def mixer1():
                act.wait_ge(s["sat_out"], 2)
                act.wait_ge(s["kv_stored"], 64)
                out(ga1o[0:16, :], 16)
                act.wait_ge(s["vecT"], 2)
                for i in range(4):
                    out(gq[0:96, i, :], 96, scale=96.0 ** -0.5)
                for i in range(4):
                    out(gl[0:96, i, :], 96, func=ACT.Identity, bias=vecT[0:96, i:i + 1])
                for i in range(4):
                    out(gk[0:96, i, :], 96)
                act.wait_ge(s["t_dve"], 10)
                link(act.activation(ge[0:96], ge[0:96], ACT.Exp, scale=-1.0))
                act.activation(ge[0:96], ge[0:96], ACT.Ln, bias=ones[0:96, 0:1]).then_inc(s["t_act"], 1)
                for i in range(2):
                    out(gv[0:96, i, :], 96)
                act.wait_ge(s["t_dve"], 11)
                act.activation(gkh[0:96, :, TP:T], gl[0:96, :, TP:T], ACT.Exp).then_inc(s["t_act"], 1)
                for i in range(2, 6):
                    out(gv[0:96, i, :], 96)
                act.wait_ge(s["t_dve"], 12)
                act.activation(gem[0:96, :], gem[0:96, :], ACT.Exp)
                act.activation(gee[0:96, :], gee[0:96, :], ACT.Exp)
                g0, g1 = go[0:96, 0:4, 0:TP], go[0:96, 4:8, 0:TP]
                act.activation(gkh[0:96, :, 0:TP], g1, ACT.Exp).then_inc(s["t_act"], 1)
                for i in range(6, 8):
                    out(gv[0:96, i, :], 96)
                act.wait_ge(s["t_dve"], 13)
                act.activation(g1, g0, ACT.Exp, scale=-1.0)
                act.activation(gl[0:96, :, 0:TP], g0, ACT.Exp).then_inc(s["t_act"], 1)
                for i in range(8):
                    out(grt[0:96, i, :], 96)
                act.wait_ge(s["pj_out"], tn[0])
                act.activation(gsl[0:96], grt[0:96], ACT.Exp, scale=-1.0).then_inc(s["t_act"], 1)
                act.wait_ge(s["qn_ps"], 11)
                for u in range(2):
                    last = act.copy(gvs[0:TS, 384 * u:384 * (u + 1)], ps[2 + u][0:TS, 0:384])
                last.then_inc(s["qn"], 1)
                act.wait_ge(s["sat_ps"], 3)
                act.wait_ge(s["t_dve"], 14)
                act.copy(go[0:96, :, TP:T], ps[6][0:96, 0:64].rearrange("p (i b) -> p i b", b=TS)).then_inc(s["sat_out"], 1)
                for c in range(NCH):
                    act.wait_ge(s["c_ps"], 2 * len(ROUNDS) * NCH + 4 * c + 1)
                    for u in range(2):
                        act.copy(gvn[0:C, 384 * u:384 * (u + 1)], ps[2 + u][0:C, 0:384])
                    act.copy(gkn[0:C, :], ps[4][0:C, 0:384]).then_inc(s["c_act"], 1)
                    act.wait_ge(s["c_ps"], 2 * len(ROUNDS) * NCH + 4 * c + 3)
                    act.copy(go[0:96, :, C * c:C * (c + 1)], ps[6][0:96, :].rearrange("p (i n) -> p i n", i=8)).then_inc(s["c_act"], 1)
                act.wait_ge(s["sum_ps"], 5)
                for i in range(4):
                    link(act.activation(ge[0:96, i, :], ps[2 + i][0:96, 0:T], ACT.Ln, scale=1.0 / 192, bias=cst[0:96, 0:1]))
                act.activation(ge[0:96], ge[0:96], ACT.Exp, scale=-0.5).then_inc(s["t_act"], 1)

            for l in range(DEPTH):
                if l == 0:
                    act.wait_ge(s["consts"], 1)
                attention(l)
                (mixer0, mixer1)[l]()
                for n in range(KT):
                    if n >= 2:
                        act.wait_ge(s["oT_ps"], KT * l + n - 1)
                    out(oT[n % 2], 128)
                norm_scale(2 * l + 2)
                copy_hT(2 * l + 2)
                base, gb = NE * l, (NE + 1) * l

                def convert_units(i, j, units, waits=True):
                    for u in units:
                        if u == 0:
                            act.wait_ge(s[f"wupa{j}"], 16 * (NE // 2) * l + 16 * (i + 1))
                        if u == UNITS_UP // 2:
                            act.wait_ge(s[f"wupb{j}"], 16 * (NE // 2) * l + 16 * (i + 1))
                        if u == UNITS_UP:
                            act.wait_ge(s[f"wdn{j}"], 16 * (NE // 2) * l + 16 * (i + 1))
                        if waits:
                            act.wait_ge(s["m_used"], UNITS * (base + 2 * i + j) + u - RING + 1)
                        act.copy(ring[(UNITS * j + u) % RING], unit_of(j, u)).then_inc(s["m_wh"], 1)

                act.wait_ge(s["x_out"], l + 1)
                act.wait_ge(s["norm_h"], 6 * (l + 1))
                convert_units(0, 0, range(0, 3), waits=False)
                act.wait_ge(s["h_parts"], l + 1)
                act.wait_ge(s["hT"], KT * (2 * l + 2))
                convert_units(0, 0, range(3, 6), waits=False)
                act.wait_ge(s["logits"], l + 1)
                for t in range(3):
                    act.activation(gt[:, t, 0:4], gt[:, t, 0:4], ACT.Exp)
                act.activation(gt[:, :, 4], gt[:, :, 4], ACT.Exp).then_inc(s["gate_e"], 1)
                xs_high(gb, 0, s["m_xg_ps"], s["m_xh"])

                def pair(i, first=False, final=False):
                    for j in range(2):
                        it = base + 2 * i + j
                        ahead = not (final and j == 1)
                        nxt = (i, 1) if j == 0 else (i + 1, 0)
                        act.wait_ge(s["m_used"], UNITS * it + UNITS_UP)
                        low_rows(gate, 2, s["m_glo"])
                        low_rows(upp, 3, s["m_ulo"])
                        tanh_gate(it, s["m_g"], s["m_tanh"])
                        convert_units(i, j, (11,))
                        xs_high(gb + 2 * i + j + 1, 1 - j, s["m_xg_ps"], s["m_xh"])
                        actT_high(it, s["m_actT_ps"], s["m_ah"])
                        if ahead:
                            convert_units(*nxt, range(0, 6))
                        act.wait_ge(s["m_used"], UNITS * (it + 1))
                        if not (l == 0 and first):
                            act.wait_ge(s[f"m_ywr{j}"], 16 * (base // 2 + i))
                        low_rows(ynat[j][:, 0:FF], 6, s["m_ylo"])
                        low_rows(ynat[j][:, FF:D], 7, s["m_ylo"])
                        if ahead:
                            convert_units(*nxt, range(6, 11))

                convert_units(0, 0, range(6, 8), waits=False)
                convert_units(0, 0, (8, 9, 10))
                pair(0, first=True)
                with act.Fori(1, NE // 2 - 1) as i:
                    pair(i)
                pair(NE // 2 - 1, final=True)
                act.wait_ge(s["flag"], l + 1)
                more = act.value_load(flag_i[0:1, 0:1], min_val=0, max_val=1)
                r = lambda n: s[f"r_{n}{l}"]
                with act.If(more > 0):
                    with act.Fori(0, NE) as e:
                        for b in range(STEPS_REST):
                            it = STEPS_REST * e + b
                            xs_high(rest_at(it, "xg"), b % 2, r("pe"), r("act"))
                            act.wait_ge(r("pe"), rest_at(it, "up") + 1)
                            low_rows(gate, 2, r("act"))
                            low_rows(upp, 3, r("act"))
                            tanh_gate(rest_at(it, "gate"), r("dve"), r("act"))
                            actT_high(rest_at(it, "actT_ps"), r("pe"), r("act"))
                            act.wait_ge(r("pe"), rest_at(it, "down") + 1)
                            low_rows(ynat[b % 2][:, 0:FF], 6, r("act"))
                            low_rows(ynat[b % 2][:, FF:D], 7, r("act"))
                with act.Else():
                    act.nop()
            norm_scale(5)

        @block.vector
        def _(dve):
            link = chain(dve, s["dve_chain"])

            def norm(n, out):
                if n == 1:
                    dve.wait_ge(s["x_loaded"], 32)
                for t, (_, m) in enumerate(TILES):
                    dve.tensor_tensor_reduce(sq[0:m, :], x[0:m, t, :], x[0:m, t, :], 1.0, 0.0, ALU.mult, ALU.add, st[0:m, t:t + 1]).then_inc(s["norm_ss"], 1)
                    dve.wait_ge(s["norm_ss"], 3 * (n - 1) + t + 1)
                dve.wait_ge(s["gain_loaded"], 16 * n)
                for t, (_, m) in enumerate(TILES):
                    dve.wait_ge(s["norm_rs"], 3 * (n - 1) + t + 1)
                    dve.scalar_tensor_tensor(out=out[0:m, t, :], in0=x[0:m, t, :], scalar=st[0:m, 8 + t:9 + t], in1=gain[0:m, :],
                                             op0=ALU.mult, op1=ALU.mult).then_inc(s["norm_h"], 1)

            def route(l):
                link(dve.memset(lg, 0.0))
                link(dve.memset(g8, -BIG))
                dve.wait_ge(s["logit_ps"], l + 1)
                dve.wait_ge(s["router_w"], 64 * (l + 1))
                for t, (_, m) in enumerate(TILES):
                    link(dve.tensor_tensor(lg[0:m, t, :], ps[2][0:m, t * 36:(t + 1) * 36], br[0:m, :], ALU.add))
                link(dve.tensor_copy(g8[:, :, 0:4], lg[:, :, 0:4]))
                for t in range(3):
                    link(dve.max(m8[:, t, :], g8[:, t, :]))
                    link(dve.max_index(idx_u[:, t, :], m8[:, t, :], g8[:, t, :]))
                link(dve.tensor_copy(i8f, idx_u))
                link(dve.tensor_tensor(gt[:, :, 0:4], lg[:, :, 0:4], m8[:, :, 0:1].broadcast_to([128, 3, 4]), ALU.subtract))
                link(dve.tensor_tensor(tmp32, iota_g[:, :].unsqueeze(1).broadcast_to([128, 3, NE]), i8f[:, :, 0:1].broadcast_to([128, 3, NE]), ALU.is_equal))
                link(dve.tensor_scalar(tmp32, tmp32, -1.0, BIG, ALU.add, ALU.mult))
                link(dve.tensor_tensor(em, lg[:, :, 4:36], tmp32, ALU.add))
                for t in range(3):
                    link(dve.max(m8[:, t, :], em[:, t, :]))
                    link(dve.max_index(idx_u[:, t, :], m8[:, t, :], em[:, t, :]))
                link(dve.tensor_copy(i8f, idx_u))
                dve.tensor_tensor(gt[:, :, 4:5], m8[:, :, 1:2], m8[:, :, 0:1], ALU.subtract).then_inc(s["logits"], 1)
                for k, a in enumerate((a1, a2)):
                    link(dve.tensor_tensor(a, iota_e[:, :].unsqueeze(1).broadcast_to([128, 3, NE]), i8f[:, :, k:k + 1].broadcast_to([128, 3, NE]), ALU.is_equal))
                    link(dve.tensor_tensor(a, a, valid[:, :].unsqueeze(2).broadcast_to([128, 3, NE]), ALU.mult))
                dve.tensor_tensor(asum, a1, a2, ALU.add).then_inc(s["gates"], 1)
                dve.wait_ge(s["gate_e"], l + 1)
                link(dve.tensor_reduce(gt[:, :, 5:6], gt[:, :, 0:4], AXX, ALU.add))
                link(dve.tensor_scalar(gt[:, :, 6:7], gt[:, :, 4:5], 1.0, None, ALU.add))
                link(dve.tensor_tensor(gt[:, :, 5:6], gt[:, :, 5:6], gt[:, :, 6:7], ALU.mult))
                link(dve.reciprocal(gt[:, :, 6:7], gt[:, :, 5:6]))
                link(dve.tensor_tensor(gt[:, :, 7:8], gt[:, :, 6:7], gt[:, :, 4:5], ALU.mult))
                dve.wait_ge(s["rank_ps"], l + 1)
                link(dve.tensor_copy(rank, ps[3][:, 0:3 * NE].rearrange("p (t n) -> p t n", t=3)))
                for k, a in enumerate((a1, a2)):
                    link(dve.tensor_tensor(tmp32, rank, a, ALU.mult))
                    link(dve.tensor_reduce(rowf.rearrange("p (t n) -> p t n", t=3)[:, :, k:k + 1], tmp32, AXX, ALU.add))
                rank2 = rowf.rearrange("p (t n) -> p t n", t=3)
                v3 = lambda a: a[:, :].rearrange("p (t n) -> p t n", t=3)
                link(dve.tensor_scalar(in_rest[:, :], rowf, float(CAP), None, ALU.is_ge))
                link(dve.tensor_scalar(gr[:, :], rowf, float(CAP - 1), None, ALU.min))
                link(dve.scalar_tensor_tensor(out=v3(gr), in0=i8f[:, :, 0:2], scalar=float(CAP), in1=v3(gr), op0=ALU.mult, op1=ALU.add))
                link(dve.tensor_copy(rows_i[:, :], gr[:, :]))
                link(dve.tensor_scalar(gr[:, :], rowf, float(-CAP), 0.0, ALU.add, ALU.max))
                link(dve.scalar_tensor_tensor(out=v3(gr), in0=i8f[:, :, 0:2], scalar=float(RROWS), in1=v3(gr), op0=ALU.mult, op1=ALU.add))
                link(dve.tensor_copy(rows_r[:, :], gr[:, :]))
                link(dve.tensor_tensor(v3(gr), gt[:, :, 6:8], v3(in_rest), ALU.mult))
                link(dve.tensor_tensor(gt[:, :, 6:8], gt[:, :, 6:8], v3(gr), ALU.subtract))
                link(dve.memset(R, -1.0))
                link(dve.scalar_tensor_tensor(out=R[:, :, 0:NE], in0=rank, scalar=1.0, in1=asum, op0=ALU.add, op1=ALU.mult))
                link(dve.tensor_scalar(R[:, :, 0:NE], R[:, :, 0:NE], -1.0, None, ALU.add))
                dve.tensor_reduce(flagf[:, 0:1], R.rearrange("p t n -> p (t n)"), AXX, ALU.max).then_inc(s["ranks"], 1)
                dve.wait_ge(s["flagT_ps"], l + 1)
                link(dve.tensor_reduce(flagf[0:1, 1:2], ps[3][0:1, 256:384], AXX, ALU.max))
                link(dve.tensor_scalar(flagf[0:1, 2:3], flagf[0:1, 1:2], float(CAP), None, ALU.is_ge))
                dve.tensor_copy(flag_i[0:1, 0:1], flagf[0:1, 2:3]).then_inc(s["flag"], 1)

            def onehot(e, step, par, s_done):
                dve.tensor_tensor(G[par], iota_rank[:, CAP * step:CAP * (step + 1)].unsqueeze(1).broadcast_to([128, 3, CAP]),
                                  R[:, :, bass.ds(e, 1)].broadcast_to([128, 3, CAP]), ALU.is_equal).then_inc(s_done, 1)

            def xs_low(it, par, s_in, s_done):
                dve.wait_ge(s_in, it + 1)
                dve.tensor_tensor(xs[par][:, :, 1, :], ps[par][:, 0:KT * CAP].rearrange("p (k n) -> p k n", k=KT), xs[par][:, :, 0, :].bitcast(F32),
                                  ALU.subtract).then_inc(s_done, 1)

            def actT_low(it, s_in, s_done):
                dve.wait_ge(s_in, it + 1)
                dve.tensor_tensor(actT[:, :, 1, :], ps[5][:, :].rearrange("p (f n) -> p f n", f=4)[:, :, 0:CAP], actT[:, :, 0, :].bitcast(F32),
                                  ALU.subtract).then_inc(s_done, 1)

            def sum_rows(dst, bank, it, s_in, s_done):
                dve.wait_ge(s_in, it + 1)
                dve.tensor_tensor(dst[0:CAP, :], ps[bank][0:CAP, :], dst[0:CAP, :], ALU.add).then_inc(s_done, 1)

            def swiglu(tanh, up, q, s_done):
                dve.wait_ge(tanh[0], tanh[1] + 1)
                dve.scalar_tensor_tensor(out=ex[0:CAP, :], in0=ex[0:CAP, :], scalar=1.0, in1=gate[0:CAP, :], op0=ALU.add, op1=ALU.mult).then_inc(q[0], 1)
                dve.wait_ge(q[0], q[1] + 1)
                dve.wait_ge(up[0], up[1] + 1)
                dve.scalar_tensor_tensor(out=an[0:CAP, :], in0=ex[0:CAP, :], scalar=0.5, in1=upp[0:CAP, :], op0=ALU.mult, op1=ALU.mult).then_inc(s_done, 1)

            def nat_out(n, par, s_in, s_done):
                dve.wait_ge(s_in, n + 1)
                dve.tensor_tensor(ynat[par][0:CAP, 0:FF], ps[6][0:CAP, :], ynat[par][0:CAP, 0:FF], ALU.add)
                dve.wait_ge(s_in, n + 2)
                dve.tensor_tensor(ynat[par][0:CAP, FF:D], ps[7][0:CAP, :], ynat[par][0:CAP, FF:D], ALU.add).then_inc(s_done, 1)

            def split_h():
                for t, (_, m) in enumerate(TILES):
                    a = h[0:m, t, :]
                    link(dve.tensor_copy(hp[0][0:m, t, :], a))
                    link(dve.tensor_tensor(sq[0:m, :], a, hp[0][0:m, t, :], ALU.subtract))
                    link(dve.tensor_copy(hp[1][0:m, t, :], sq[0:m, :]))
                    link(dve.tensor_tensor(sq[0:m, :], sq[0:m, :], hp[1][0:m, t, :], ALU.subtract))
                    last = link(dve.tensor_copy(hp[2][0:m, t, :], sq[0:m, :])) if t < 2 else dve.tensor_copy(hp[2][0:m, t, :], sq[0:m, :])
                last.then_inc(s["h_parts"], 1)

            def mark(ins, name, value):
                ins.then_inc(s[name], 1)
                dve.wait_ge(s[name], value)

            def setup():
                dve.wait_ge(s["vecT_ps"], 2)
                link(dve.tensor_copy(vecT[:, :], ps[7][:, 0:90]))
                link(dve.tensor_scalar(nvec[:, :], vecT[:, 48:60], -1.0, None, ALU.mult))
                for n, m in enumerate((mlow, moff1, moff2)):
                    link(dve.tensor_tensor(m[:, :], ps[6][:, 128 * n:128 * (n + 1)], m[:, :], ALU.is_equal))
                link(dve.tensor_copy(block64[:, :], moff2[:, :]))
                link(dve.tensor_tensor(mup[:, :], mlow[:, :], before[:, :], ALU.mult))
                link(dve.tensor_tensor(moff2[:, :], block64[:, :], moff1[:, :], ALU.subtract))
                link(dve.tensor_tensor(moff1[:, :], moff1[:, :], mlow[:, :], ALU.subtract))
                for m in (mlow, moff1, moff2):
                    link(dve.tensor_tensor(sq[:, 0:128], m[:, :], upto[:, :], ALU.mult))
                    link(dve.tensor_tensor(m[:, :], m[:, :], sq[:, 0:128], ALU.subtract))
                mark(dve.memset(sq[:, 0:1], 0.0), "vecT", 1)

            def attention(l):
                dve.wait_ge(s["mm_in"], 32 * (l + 1))
                for m in range(2):
                    mark(dve.tensor_tensor_reduce(sq, mem[:, m, :], mem[:, m, :], 1.0, 0.0, ALU.mult, ALU.add, mm_st[:, m:m + 1]), "mm_ss", 2 * l + m + 1)
                for m in range(2):
                    dve.wait_ge(s["mm_rs"], 2 * l + m + 1)
                    dve.scalar_tensor_tensor(out=mem[:, m, :], in0=mem[:, m, :], scalar=mm_st[:, 4 + m:5 + m], in1=gmem, op0=ALU.mult,
                                             op1=ALU.mult).then_inc(s["mm_h"], 1)
                norm(2 * l + 1, h)
                for hd in range(4):
                    dve.wait_ge(s["sc_ps"], 4 * l + hd + 1)
                    link(dve.tensor_reduce(smx[:, 2 * hd:2 * hd + 2], ps[4 + hd][:, :].rearrange("p (t m) -> p t m", t=2), AXX, ALU.max))
                    mark(dve.tensor_scalar(snx[:, 2 * hd:2 * hd + 2], smx[:, 2 * hd:2 * hd + 2], -0.125, None, ALU.mult), "sc_max", 4 * l + hd + 1)
                for hd in range(4):
                    dve.wait_ge(s["sc_exp"], 4 * l + hd + 1)
                    link(dve.reciprocal(srs[:, 2 * hd:2 * hd + 2], ssm[:, 2 * hd:2 * hd + 2]))
                    dve.tensor_tensor(P[:, hd], P[:, hd], srs[:, 2 * hd:2 * hd + 2].unsqueeze(2).broadcast_to([128, 2, N_MEM]),
                                      ALU.mult).then_inc(s["sc_prob"], 1)
                dve.wait_ge(s["qb_ps"], 1 if l == 0 else 2)
                dve.wait_ge(s["cache_k"], 32 * (l + 1))
                for m in range(2):
                    for b in range(0, TS, 2):
                        link(dve.tensor_tensor(KC[:, m, b:b + 2, :], KC[:, m, b:b + 2, :], ps[4 + b // 2][:, :].rearrange("p (b n) -> p b n", b=2), ALU.mult))
                mark(dve.tensor_reduce(sc_s, KC.rearrange("p m b (h d) -> p (m b h) d", d=64), AXX, ALU.add), "s_score", l + 1)
                dve.wait_ge(s["sT_ps"], l + 1)
                link(dve.tensor_reduce(smx[0:32, 0:1], ps[3][0:32, 0:N_MEM], AXX, ALU.max))
                mark(dve.tensor_scalar(snx[0:32, 0:1], smx[0:32, 0:1], -0.125, None, ALU.mult), "s_max", l + 1)
                dve.wait_ge(s["s_exp"], l + 1)
                link(dve.reciprocal(srs[0:32, 0:1], ssm[0:32, 0:1]))
                mark(dve.tensor_scalar(sp_s[0:32, :], sp_s[0:32, :], srs[0:32, 0:1], None, ALU.mult), "s_prob", l + 1)
                dve.wait_ge(s["sat_out"], l + 1)

            def output(l):
                for n in range(KT):
                    dve.wait_ge(s["oT_ps"], KT * l + n + 1)
                    cols = slice(128 * n, 128 * (n + 1))
                    dve.tensor_tensor(x[:, 0:2, cols], ps[2 + n % 2][:, 0:256].rearrange("p (t d) -> p t d", t=2), x[:, 0:2, cols], ALU.add)
                    mark(dve.tensor_tensor(x[0:TS, 2, cols], ps[2 + n % 2][0:TS, 256:384], x[0:TS, 2, cols], ALU.add), "o_x", KT * l + n + 1)
                mark(dve.memset(sq[:, 0:1], 0.0), "x_out", l + 1)

            vec = lambda at: vecT[:, at:at + PAIRS].unsqueeze(2).broadcast_to([128, PAIRS, T])
            V_KK, V_KA, V_RK, V_LG, V_LB = 60, 66, 72, 78, 84

            def mixer0():
                T0, T1, T2 = (a[:, 0:PAIRS, :] for a in TT)
                xx = TT[0]
                dve.wait_ge(s["hT"], KT)
                dve.wait_ge(s["shiftT_ps"], 1)
                dve.tensor_tensor(xx[:, :, 1:TP], hT[:, :, 0:TP - 1], hT[:, :, 1:TP], ALU.subtract)
                dve.tensor_scalar(xx[:, :, 0:1], hT[:, :, 0:1], -1.0, None, ALU.mult)
                link(dve.tensor_tensor(xx[:, :, TP:T], ps[7][:, 0:KT * TS].rearrange("p (k b) -> p k b", k=KT), hT[:, :, TP:T], ALU.subtract))
                done = {2: 5, 3: 6, 4: 7, 5: 13}

                def blend(i, j):
                    if i in done:
                        dve.wait_ge(s["pj_ps"], done[i])
                    for k in range(KT):
                        last = dve.scalar_tensor_tensor(out=TT[1 + i % 2][:, k, :], in0=xx[:, k, :], scalar=vecT[:, 8 * j + k:8 * j + k + 1], in1=hT[:, k, :],
                                                        op0=ALU.mult, op1=ALU.add)
                    last.then_inc(s["xj"], 1)

                for i, j in enumerate((1, 4, 5, 2)):
                    blend(i, j)
                dve.wait_ge(s["pj_out"], 7)
                link(dve.tensor_scalar(w1o[0:64, :], w1o[0:64, :], 1.0, None, ALU.add))
                link(dve.reciprocal(w1o[0:64, :], w1o[0:64, :]))
                mark(dve.tensor_scalar(w1o[0:64, :], w1o[0:64, :], 2.0, -1.0, ALU.mult, ALU.add), "lora_s", 1)
                link(dve.tensor_scalar(g1o, g1o, 1.0, None, ALU.add))
                mark(dve.reciprocal(g1o, g1o), "lora_s", 2)
                blend(4, 0)
                dve.wait_ge(s["pj_out"], 13)
                link(dve.tensor_tensor(vkk, vk, vec(V_KK), ALU.mult))
                mark(dve.tensor_tensor(vL, vkk, vkk, ALU.mult), "t_dve", 1)
                blend(5, 3)
                dve.wait_ge(s["sum_ps"], 1)
                for q in range(PAIRS):
                    link(dve.tensor_scalar(vL[:, q, :], ps[2 + q][:, 0:T], 1e-24, None, ALU.max))
                mark(dve.memset(sq[:, 0:1], 0.0), "t_dve", 2)
                dve.wait_ge(s["t_act"], 1)
                link(dve.tensor_tensor(vkk, vkk, vL, ALU.mult))
                dve.wait_ge(s["pj_out"], 19)
                link(dve.tensor_scalar(vld, vld, 1.0, None, ALU.add))
                link(dve.reciprocal(vL, vld))
                link(dve.tensor_scalar(vld, vL, -float(np.exp(-0.5)), None, ALU.mult))
                for q in range(PAIRS):
                    for c in range(NCH):
                        cc = slice(C * c, C * (c + 1))
                        last = dve.tensor_tensor_scan(vL[:, q, cc], ones[:, 0:C], vld[:, q, cc], 0.0, ALU.mult, ALU.add)
                link(last)
                dve.wait_ge(s["pj_out"], 25)
                link(dve.tensor_scalar(vb, vb, 1.0, None, ALU.add))
                link(dve.reciprocal(vb, vb))
                dve.wait_ge(s["xj"], 6)
                link(dve.tensor_scalar(T0, vb, -1.0, None, ALU.add))
                link(dve.tensor_tensor(T0, T0, vec(V_KA), ALU.mult))
                link(dve.scalar_tensor_tensor(out=vk, in0=T0, scalar=1.0, in1=vk, op0=ALU.add, op1=ALU.mult))
                link(dve.tensor_tensor(vb, vb, vkk, ALU.mult))
                dve.wait_ge(s["pj_out"], 37)
                link(dve.tensor_tensor(T0, vr, vk, ALU.mult))
                mark(dve.tensor_tensor(T0, T0, vec(V_RK), ALU.mult), "t_dve", 3)
                dve.wait_ge(s["pj_out"], 43)
                mark(dve.tensor_tensor(T2[:, :, 0:TP], vL[:, :, 0:TP], vld[:, :, 0:TP], ALU.subtract), "t_dve", 4)
                dve.wait_ge(s["sum_ps"], 2)
                dve.wait_ge(s["t_act"], 2)
                for q in range(PAIRS):
                    link(dve.tensor_tensor(vld[:, q, :], ps[2 + q][:, 0:T], vv[:, q, :], ALU.mult))
                mark(dve.memset(sq[:, 0:1], 0.0), "t_dve", 5)
                dve.wait_ge(s["t_act"], 3)
                pc = slice(0, TP)
                link(dve.tensor_copy(lam[:, :, :], T1[:, :, C - 1:TP:C]))
                link(dve.tensor_tensor(vr[:, :, pc], vr[:, :, pc], T1[:, :, pc], ALU.mult))
                link(dve.scalar_tensor_tensor(out=vkk[:, :, pc], in0=vkk[:, :, pc], scalar=-1.0, in1=T2[:, :, pc], op0=ALU.mult, op1=ALU.mult))
                link(dve.tensor_tensor(vk[:, :, pc], vk[:, :, pc], T0[:, :, pc], ALU.mult))
                mark(dve.tensor_tensor(vb[:, :, pc], vb[:, :, pc], T0[:, :, pc], ALU.mult), "t_dve", 6)

                I3 = ident[:, :].unsqueeze(1).broadcast_to([128, 3, 128])
                m3 = lambda m: m[:, :].unsqueeze(1).broadcast_to([128, 3, 128])
                adds = {"U1": (cUb, cUa), "UT1": (cUTb, cUTa), "U2": (cUa, cUb), "UT2": (cUTa, cUTb), "U3": (cUb, cUa), "UT3": (cUTb, cUTa),
                        "U4": (cUa, cUb), "UT4": (cUTa, cUTb), "U5": (cUb, cUa)}
                masks = {"MT": (cN, before), "PT": (cNT, upto), "QT": (cQT, upto)}
                dve.wait_ge(s["c_pool"], 1)
                def sample_step(n):
                    half, part = divmod(n, 9)
                    i32 = slice(32 * half, 32 * half + 32)
                    S, P_ = DS[:, i32, :], Dt[:, i32, :]
                    row = lambda v: Dv[:, v, :].unsqueeze(1).broadcast_to([96, 32, 64])
                    col = lambda a: a[:, i32].unsqueeze(2).broadcast_to([96, 32, 64])
                    if part == 0:
                        if half == 0:
                            dve.wait_ge(s["dec_in"], 32)
                        link(dve.tensor_tensor(P_, S, row(3), ALU.mult))
                    elif part == 1:
                        link(dve.tensor_reduce(Dsa[:, i32], P_, AXX, ALU.add))
                    elif part == 2:
                        link(dve.tensor_tensor(S, S, row(5), ALU.mult))
                    elif part == 3:
                        link(dve.tensor_tensor(P_, row(4), col(Dsa), ALU.mult))
                    elif part == 4:
                        link(dve.tensor_tensor(S, S, P_, ALU.subtract))
                    elif part == 5:
                        link(dve.tensor_tensor(P_, row(1), col(Dv[:, 2, :]), ALU.mult))
                    elif part == 6:
                        mark(dve.tensor_tensor(S, S, P_, ALU.add), "dec_sum", 2 * half + 1)
                    elif part == 7:
                        link(dve.tensor_tensor(P_, S, row(0), ALU.mult))
                    else:
                        mark(dve.tensor_reduce(Dy[:, i32], P_, AXX, ALU.add), "dec_sum", 2 * half + 2)

                between = {(0, "UT1"): (0,), (0, "U5"): (1,), (1, "NT"): (2, 3, 4), (1, "UT1"): (5,), (1, "U5"): (6,), (2, "NT"): (7, 8, 9),
                           (2, "UT1"): (10,), (2, "U5"): (11,), (3, "NT"): (12, 13, 14, 15), (3, "UT1"): (16,), (3, "U5"): (17,)}
                for c in range(NCH):
                    for name, e in ROUNDS:
                        if e != "dve":
                            continue
                        for hf in range(2):
                            dve.wait_ge(s["c_ps"], c_ps_at(c, name, hf))
                            b = ps[2 * (ORDER.index(name) % 4) + hf][:, 0:384].rearrange("p (q n) -> p q n", q=3)
                            pp = slice(3 * hf, 3 * hf + 3)
                            tt = lambda o, a, b_, op: dve.tensor_tensor(o[:, pp, :], a, b_, op)
                            if name == "N":
                                link(tt(cN, b, m3(mlow), ALU.mult))
                                tt(cN1, b, m3(moff1), ALU.mult)
                                tt(cN2, b, m3(moff2), ALU.mult)
                                last = tt(cUTa, cN[:, pp, :], I3, ALU.add)
                            elif name == "NT":
                                link(tt(cNT, b, m3(mup), ALU.mult))
                                last = tt(cUa, cNT[:, pp, :], I3, ALU.add)
                            elif name in masks:
                                o, m = masks[name]
                                last = tt(o, b, m3(m), ALU.mult)
                            elif name == "Z":
                                link(tt(cZ, b, cZ[:, pp, :], ALU.add))
                                last = tt(cZ, cZ[:, pp, :], lam[:, pp, c:c + 1].broadcast_to([128, 3, 128]), ALU.mult)
                            else:
                                o, a = adds[name]
                                last = tt(o, b, a[:, pp, :], ALU.add)
                            mark(last, "c_dve", c_at(c, name, hf))
                        for n in between.get((c, name), ()):
                            sample_step(n)
                dve.wait_ge(s["sum_ps"], 3)
                for q in range(PAIRS):
                    link(dve.scalar_tensor_tensor(out=T0[:, q, :], in0=ps[2 + q][:, 0:T], scalar=-1.0 / 64, in1=vL[:, q, :], op0=ALU.mult, op1=ALU.add))
                mark(dve.memset(sq[:, 0:1], 0.0), "t_dve", 7)
                mark(dve.tensor_tensor(T1, T0, T0, ALU.mult), "t_dve", 8)
                dve.wait_ge(s["t_act"], 6)
                link(dve.tensor_tensor(T0, T0, T1, ALU.mult))
                link(dve.tensor_tensor(T0, T0, vec(V_LG), ALU.mult))
                link(dve.tensor_tensor(T0, T0, vec(V_LB), ALU.add))
                link(dve.tensor_tensor(T0, T0, vld, ALU.add))
                mark(dve.tensor_tensor(mixedT[:, 0:PAIRS, :], T0, vg, ALU.mult), "t_dve", 9)

            def mixer1():
                g96 = lambda a: a[0:96]
                n = tiles_through(CHUNKS[0] + 1) + 1 + 4 + 4
                dve.wait_ge(s["pj_out"], n)
                mark(dve.scalar_tensor_tensor(out=g96(ge), in0=g96(gl), scalar=-1.0, in1=g96(gl), op0=ALU.mult, op1=ALU.max), "t_dve", 10)
                link(dve.tensor_scalar(g96(gl), g96(gl), 0.0, None, ALU.min))
                dve.wait_ge(s["t_act"], 7)
                link(dve.tensor_tensor(g96(gl), g96(gl), g96(ge), ALU.subtract))
                mark(dve.tensor_scalar(g96(gl), g96(gl), 1.0 / 16, None, ALU.mult), "t_dve", 11)
                for i in range(4):
                    for c in range(NCH):
                        cc = slice(C * c, C * (c + 1))
                        last = dve.tensor_tensor_scan(ge[0:96, i, cc], ones[0:96, 0:C], gl[0:96, i, cc], 0.0, ALU.mult, ALU.add)
                link(last)
                gep = ge[0:96, :, 0:TP]
                dve.tensor_copy(gem[0:96, :].rearrange("p (i c) -> p i c", i=4), ge[0:96, :, C // 2 - 1:TP:C])
                link(dve.tensor_copy(gee[0:96, :].rearrange("p (i c) -> p i c", i=4), ge[0:96, :, C - 1:TP:C]))
                g0, g1 = go[0:96, 0:4, 0:TP], go[0:96, 4:8, 0:TP]
                ic = lambda a: a.unsqueeze(2).broadcast_to([96, NCH, C])
                for i in range(4):
                    v4 = lambda a: a[:, i, :].rearrange("p (c n) -> p c n", c=NCH)
                    dve.tensor_tensor(v4(g1), ic(gee[0:96, NCH * i:NCH * (i + 1)]), v4(gep), ALU.subtract)
                    last = dve.tensor_tensor(v4(g0), v4(gep), ic(gem[0:96, NCH * i:NCH * (i + 1)]), ALU.subtract)
                mark(last, "t_dve", 12)
                dve.wait_ge(s["t_act"], 9)
                dve.wait_ge(s["pj_out"], n + 4)
                link(dve.tensor_tensor(gkh[0:96, :, 0:TP], gkh[0:96, :, 0:TP], gk[0:96, :, 0:TP], ALU.mult))
                mark(dve.memset(sq[:, 0:1], 0.0), "t_dve", 13)
                dve.wait_ge(s["t_act"], 10)
                link(dve.tensor_tensor(gq[0:96, :, 0:TP], gq[0:96, :, 0:TP], gl[0:96, :, 0:TP], ALU.mult))
                link(dve.tensor_tensor(gk[0:96, :, 0:TP], gk[0:96, :, 0:TP], g1, ALU.mult))
                dve.memset(gZ[0:96], 0.0)
                mark(dve.memset(gZm[0:96], 0.0), "t_dve", 14)
                dve.wait_ge(s["gla_in"], 16)
                for b in range(TS):
                    mark(dve.tensor_tensor(gS[0:96, b], gS[0:96, b], gkh[0:96, :, TP + b:TP + b + 1].broadcast_to([96, 4, 192]), ALU.mult), "dec_mul", b + 1)
                    if b > 0:
                        state_add(b - 1)
                state_add(TS - 1)
                mark(dve.memset(sq[:, 0:1], 0.0), "dec_sum", 5)
                cp = 2 * len(ROUNDS) * NCH
                for c in range(NCH):
                    dve.wait_ge(s["c_ps"], cp + 4 * c + 2)
                    mark(dve.tensor_tensor(gatt[0:C], ps[5][0:C, 0:4 * C].rearrange("p (i t) -> p i t", i=4),
                                           upto[0:C, 0:C].unsqueeze(1).broadcast_to([C, 4, C]), ALU.mult), "c_dve", C_TOTAL + 2 * c + 1)
                    dve.wait_ge(s["c_ps"], cp + 4 * c + 4)
                    for i in range(4):
                        link(dve.scalar_tensor_tensor(out=gZ[0:96, i, :], in0=gZ[0:96, i, :], scalar=gee[0:96, NCH * i + c:NCH * i + c + 1],
                                                      in1=ps[7 if i < 2 else 5][0:96, 192 * (i % 2):192 * (i % 2 + 1)], op0=ALU.mult, op1=ALU.add))
                        if c < NCH - 1:
                            link(dve.tensor_scalar(gZm[0:96, i, :], gZ[0:96, i, :], gem[0:96, NCH * i + c + 1:NCH * i + c + 2], None, ALU.mult))
                    mark(dve.memset(sq[:, 0:1], 0.0), "c_dve", C_TOTAL + 2 * c + 2)
                    if c == 0:
                        dve.wait_ge(s["t_act"], 11)
                    part = slice(2 * c, 2 * c + 2)
                    link(dve.tensor_scalar(gsl[0:96, part], gsl[0:96, part], 1.0, None, ALU.add))
                    link(dve.reciprocal(gsl[0:96, part], gsl[0:96, part]))
                    link(dve.tensor_tensor(grt[0:96, part], grt[0:96, part], gsl[0:96, part], ALU.mult))
                dve.wait_ge(s["c_act"], C_ACT + 2 * NCH)
                dve.wait_ge(s["sat_out"], 3)
                mark(dve.tensor_tensor(gv[0:96], go[0:96], go[0:96], ALU.mult), "t_dve", 15)
                dve.wait_ge(s["t_act"], 12)
                o4 = go[0:96].rearrange("p (i u) t -> p i u t", u=2)
                for i in range(4):
                    for u in range(2):
                        last = dve.scalar_tensor_tensor(out=o4[:, i, u, :], in0=o4[:, i, u, :], scalar=vecT[0:96, 4 + u:5 + u], in1=ge[0:96, i, :], op0=ALU.mult, op1=ALU.mult)
                link(last)
                mark(dve.tensor_tensor(mixedT[0:96, 0:8, :], go[0:96], grt[0:96], ALU.mult), "t_dve", 16)

            def state_add(b):
                dve.wait_ge(s["qb_ps"], 3 + b)
                for i in range(4):
                    last = dve.scalar_tensor_tensor(out=gS[0:96, b, i, :], in0=ps[2 + 2 * (b % 2) + i // 2][0:96, 192 * (i % 2):192 * (i % 2 + 1)],
                                                    scalar=gk[0:96, i, TP + b:TP + b + 1], in1=gS[0:96, b, i, :], op0=ALU.mult, op1=ALU.add)
                link(last)

            def add_rows(gate, buf):
                for t, (_, m) in enumerate(TILES):
                    last = dve.scalar_tensor_tensor(out=x[0:m, t, :], in0=buf[0:m, t, :], scalar=gate(t, m), in1=x[0:m, t, :],
                                                    op0=ALU.mult, op1=ALU.add)
                return last

            dve.wait_ge(s["consts"], 1)
            setup()
            for l in range(DEPTH):
                if l == 1:
                    dve.wait_ge(s["vecT_ps"], 3)
                    mark(dve.tensor_copy(vecT[0:96, 0:6], ps[7][0:96, 0:6]), "vecT", 2)
                attention(l)
                (mixer0, mixer1)[l]()
                output(l)
                norm(2 * l + 2, h)
                dve.wait_ge(s["norm_h"], 6 * (l + 1))
                split_h()
                link(dve.memset(an, 0.0))
                base, gb = NE * l, (NE + 1) * l

                def low_units(i, j, units):
                    for u in units:
                        dve.wait_ge(s["m_wh"], UNITS * (base + 2 * i + j) + u + 1)
                        dve.tensor_tensor(low_of(j, u), unit_of(j, u), ring[(UNITS * j + u) % RING].bitcast(F32), ALU.subtract).then_inc(s["m_wl"], 1)

                low_units(0, 0, range(0, 3))
                route(l)
                onehot(0, 0, 0, s["m_G"])
                onehot(1, 0, 1, s["m_G"])
                low_units(0, 0, range(3, 6))
                xs_low(gb, 0, s["m_xh"], s["m_xs"])

                def pair(i, final=False):
                    for j in range(2):
                        it, g = base + 2 * i + j, gb + 2 * i + j
                        ahead = not (final and j == 1)
                        nxt = (i, 1) if j == 0 else (i + 1, 0)
                        sum_rows(gate, 2, it, s["m_glo"], s["m_g"])
                        sum_rows(upp, 3, it, s["m_ulo"], s["m_u"])
                        swiglu((s["m_tanh"], it), (s["m_u"], it), (s["m_q"], it), s["m_act"])
                        low_units(i, j, (10,))
                        xs_low(g + 1, 1 - j, s["m_xh"], s["m_xs"])
                        actT_low(it, s["m_ah"], s["m_actT"])
                        low_units(i, j, (11,))
                        if ahead:
                            low_units(*nxt, range(0, 4))
                            onehot(2 * i + j + 2, 0, j, s["m_G"])
                            low_units(*nxt, range(4, 6))
                        nat_out(2 * it, j, s["m_ylo"], s["m_nat"])
                        if ahead:
                            low_units(*nxt, range(6, 10))

                low_units(0, 0, range(6, 10))
                pair(0)
                with dve.Fori(1, NE // 2 - 1) as i:
                    pair(i)
                pair(NE // 2 - 1, final=True)
                dve.wait_ge(s["flag"], l + 1)
                more = dve.value_load(flag_i[0:1, 0:1], min_val=0, max_val=1)
                r = lambda n: s[f"r_{n}{l}"]
                with dve.If(more > 0):
                    dve.wait_ge(s["m_xg_ps"], (NE + 1) * (l + 1))
                    for j in range(2):
                        dve.wait_ge(s[f"m_ywr{j}"], 8 * NE * (l + 1))
                    with dve.Fori(0, NE) as e:
                        for b in range(STEPS_REST):
                            it = STEPS_REST * e + b
                            onehot(e, b + 1, b % 2, r("dve"))
                            at = lambda name: rest_at(it, name)
                            xs_low(at("xs_high"), b % 2, r("act"), r("dve"))
                            sum_rows(gate, 2, at("gate_low"), r("act"), r("dve"))
                            sum_rows(upp, 3, at("up_low"), r("act"), r("dve"))
                            swiglu((r("act"), at("tanh")), (r("dve"), at("up")), (r("dve"), at("q")), r("dve"))
                            actT_low(at("actT_high"), r("act"), r("dve"))
                            nat_out(at("y_low0"), b % 2, r("act"), r("dve"))
                            dve.wait_ge(s[f"ryw{'ab'[b % 2]}{l}"], 16 * (STEPS_REST // 2 * e + b // 2 + 1))
                    for k in range(2):
                        dve.wait_ge(s[f"rgath{l}"], 48 * (k + 1))
                        add_rows(lambda t, m: gr[0:m, 2 * t + k:2 * t + k + 1], yg[0]).then_inc(s[f"rcomb{l}"], 1)
                        dve.wait_ge(s[f"rcomb{l}"], k + 1)
                with dve.Else():
                    dve.nop()
                for k in range(2):
                    dve.wait_ge(s[("gathered", "gath1")[k]], 48 * (l + 1))
                    add_rows(lambda t, m: gt[0:m, t, 6 + k:7 + k], yg[k]).then_inc(s["combined"], 1)
                    dve.wait_ge(s["combined"], 2 * l + k + 1)
            norm(5, h)


_OUTS = [("y_prompt", (1, 256, 1024)), ("y_sample", (8, 1, 1024)), ("prompt_rwkv_S", (1, 1, 12, 64, 64)), ("prompt_rwkv_shift", (1, 1, 1024)),
         ("prompt_gla_S", (1, 1, 4, 96, 192)), ("prompt_mem_k", (2, 1, 256, 4, 64)), ("prompt_mem_v", (2, 1, 256, 4, 64)),
         ("sample_rwkv_S", (1, 8, 12, 64, 64)), ("sample_rwkv_shift", (1, 8, 1024)), ("sample_gla_S", (1, 8, 4, 96, 192))]


def kernel(**inputs):
    import concourse.bacc as _bacc
    from concourse.bass_utils import run_bass_kernel_spmd as _run

    nc = _bacc.Bacc("TRN2", target_bir_lowering=False, num_devices=1)
    arrays, A, O = {}, {}, {}
    for name, v in inputs.items():
        a = np.ascontiguousarray(v)
        arrays[f"in_{name}"] = a
        A[name] = nc.dram_tensor(f"in_{name}", a.shape, mybir.dt.from_np(a.dtype), kind="ExternalInput").ap()
    for name, shape in _OUTS:
        O[name] = nc.dram_tensor(f"out_{name}", shape, F32, kind="ExternalOutput").ap()
    build(nc, A, O)
    r = _run(nc, [arrays], core_ids=[0])
    return tuple(r.results[0][f"out_{name}"] for name, _ in _OUTS)
```
